# Optimizing a Trainium2 kernel written in Bass

```python
import math
import jax
import jax.numpy as jnp
from jax import lax
import numpy as np

D_MODEL = 1024
BATCH = 1
SEQ = 256
DEPTH = 2

MIX_WIDTH = 1024
MIX_A = MIX_WIDTH // 2
MIX_B = MIX_WIDTH - MIX_A
MIX_C = MIX_WIDTH // 2
MIX_D = MIX_WIDTH - MIX_C

MLSTM_HEADS = 4
MLSTM_DH = MIX_A // MLSTM_HEADS
MLSTM_CHUNK = 64

LRU_HEADS = 4
LRU_DH = MIX_B // LRU_HEADS
LRU_CONV = 4
LRU_C = 8.0

S5_GROUP = 16
S5_GROUPS = MIX_C // S5_GROUP
S5_STATE = 64

GLA_HEADS = 4
GLA_DK = 64
GLA_DV = MIX_D // GLA_HEADS
GLA_GATE_RANK = 16
GLA_GATE_TEMP = 16.0
GLA_CHUNK = 64

N_EXPERTS = 64
TOP_K = 8
N_GROUPS = 8
TOPK_GROUPS = 4
D_EXPERT = 256
D_SHARED = 256
ROUTED_SCALE = 2.5
MOE_BLOCK = 128

N_EVEN = (DEPTH + 1) // 2
N_ODD = DEPTH // 2
ALPHA = (2.0 * DEPTH) ** 0.25
BETA = (8.0 * DEPTH) ** -0.25
EPS = 1e-5
F32 = jnp.float32

EVEN_SPLITS = [MIX_A, 2 * MIX_A, 3 * MIX_A, 4 * MIX_A, 4 * MIX_A + 2 * MLSTM_HEADS, 4 * MIX_A + 2 * MLSTM_HEADS + MIX_B]
EVEN_IN = 4 * MIX_A + 2 * MLSTM_HEADS + 2 * MIX_B
ODD_SPLITS = [MIX_C, MIX_C + GLA_HEADS * GLA_DK, MIX_C + 2 * GLA_HEADS * GLA_DK, MIX_C + 2 * GLA_HEADS * GLA_DK + MIX_D, MIX_C + 2 * GLA_HEADS * GLA_DK + 2 * MIX_D]
ODD_IN = MIX_C + 2 * GLA_HEADS * GLA_DK + 2 * MIX_D + GLA_GATE_RANK

kernel_name = 'hybrid_mlstm_rglru_s5_gla_moe_deepnorm'

def layer_norm(x, w, b):
    xf = x.astype(F32)
    mu = jnp.mean(xf, axis=-1, keepdims=True)
    xc = xf - mu
    y = xc * lax.rsqrt(jnp.mean(xc * xc, axis=-1, keepdims=True) + EPS)
    return (y * w.astype(F32) + b.astype(F32)).astype(x.dtype)

def head_norm(h, w, center):
    if center:
        h = h - jnp.mean(h, axis=-1, keepdims=True)
    y = h * lax.rsqrt(jnp.mean(h * h, axis=-1, keepdims=True) + EPS)
    return y.reshape(h.shape[0], h.shape[1], -1) * w.astype(F32)

def to_chunks(t, L):
    b, s, h = t.shape[:3]
    t = t.reshape((b, s // L, L, h) + t.shape[3:])
    return jnp.moveaxis(t, 3, 1)

def from_chunks(t):
    t = jnp.moveaxis(t, 1, 3)
    b, n, l, h = t.shape[:4]
    return t.reshape((b, n * l, h) + t.shape[4:])

def linear_scan(a, u, axis):
    def combine(lhs, rhs):
        a1, u1 = lhs
        a2, u2 = rhs
        return a1 * a2, a2 * u1 + u2
    return lax.associative_scan(combine, (a, u), axis=axis)[1]

def mlstm(q, k, v, i_pre, f_pre):
    L = MLSTM_CHUNK
    bsz, _, nh, dh = q.shape
    qc = to_chunks(q, L)
    kc = to_chunks(k, L) * (dh ** -0.5)
    vc = to_chunks(v, L)
    ig = to_chunks(i_pre, L)
    b = jnp.cumsum(to_chunks(jax.nn.log_sigmoid(f_pre), L), axis=-1)
    b_last = b[..., -1]
    w_loc = b_last[..., None] - b + ig
    m_loc = jnp.max(w_loc, axis=-1)
    p_loc = jnp.exp(w_loc - m_loc[..., None])
    c_loc = jnp.einsum('bhnl,bhnld,bhnle->bhnde', p_loc, kc, vc)
    n_loc = jnp.einsum('bhnl,bhnld->bhnd', p_loc, kc)

    def step(carry, xs):
        c, n, m = carry
        bl, ml, cl, nl = xs
        m_new = jnp.maximum(bl + m, ml)
        keep = jnp.exp(bl + m - m_new)
        add = jnp.exp(ml - m_new)
        c_new = keep[..., None, None] * c + add[..., None, None] * cl
        n_new = keep[..., None] * n + add[..., None] * nl
        return (c_new, n_new, m_new), (c, n, m)

    init = (jnp.zeros((bsz, nh, dh, dh), F32), jnp.zeros((bsz, nh, dh), F32), jnp.zeros((bsz, nh), F32))
    xs = (jnp.moveaxis(b_last, 2, 0), jnp.moveaxis(m_loc, 2, 0), jnp.moveaxis(c_loc, 2, 0), jnp.moveaxis(n_loc, 2, 0))
    _, (c_prev, n_prev, m_prev) = lax.scan(step, init, xs)
    c_prev = jnp.moveaxis(c_prev, 0, 2)
    n_prev = jnp.moveaxis(n_prev, 0, 2)
    m_prev = jnp.moveaxis(m_prev, 0, 2)
    causal = jnp.tril(jnp.ones((L, L), dtype=bool))
    d_mat = jnp.where(causal, b[..., :, None] - b[..., None, :] + ig[..., None, :], -jnp.inf)
    m_inter = b + m_prev[..., None]
    m_i = jnp.maximum(m_inter, jnp.max(d_mat, axis=-1))
    s = jnp.einsum('bhnid,bhnjd->bhnij', qc, kc) * jnp.exp(d_mat - m_i[..., None])
    w_inter = jnp.exp(m_inter - m_i)
    num = jnp.einsum('bhnij,bhnje->bhnie', s, vc) + w_inter[..., None] * jnp.einsum('bhnid,bhnde->bhnie', qc, c_prev)
    den = jnp.sum(s, axis=-1) + w_inter * jnp.einsum('bhnid,bhnd->bhni', qc, n_prev)
    h = num / jnp.maximum(jnp.abs(den), jnp.exp(-m_i))[..., None]
    return from_chunks(h)

def rglru(xb, gb, conv_w, conv_b, wa, ba, wx, bx, lam):
    bsz, s, c = xb.shape
    xc = lax.conv_general_dilated(xb, conv_w[:, None, :], (1,), [(LRU_CONV - 1, 0)],
                                  dimension_numbers=('NWC', 'WIO', 'NWC'), feature_group_count=c) + conv_b
    xh = xc.reshape(bsz, s, LRU_HEADS, LRU_DH)
    r = jax.nn.sigmoid((jnp.einsum('bshi,hij->bshj', xh, wa).reshape(bsz, s, c) + ba).astype(F32))
    i = jax.nn.sigmoid((jnp.einsum('bshi,hij->bshj', xh, wx).reshape(bsz, s, c) + bx).astype(F32))
    log_a = -LRU_C * r * jax.nn.softplus(-lam.astype(F32))
    a = jnp.exp(log_a)
    u = jnp.sqrt(-jnp.expm1(2.0 * log_a)) * i * xc.astype(F32)
    h = linear_scan(a, u, axis=1)
    return h * jax.nn.gelu(gb.astype(F32))

def even_mixer(x, w_in, gate_b, norm_w, conv_w, conv_b, wa, ba, wx, bx, lam):
    bsz, s, _ = x.shape
    q, k, v, o, g, xb, gb = jnp.split(x @ w_in, EVEN_SPLITS, axis=-1)
    heads = lambda t: t.astype(F32).reshape(bsz, s, MLSTM_HEADS, MLSTM_DH)
    g = g.astype(F32) + gate_b.astype(F32)
    h = mlstm(heads(q), heads(k), heads(v), g[..., :MLSTM_HEADS], g[..., MLSTM_HEADS:])
    y_a = head_norm(h, norm_w, True) * jax.nn.sigmoid(o.astype(F32))
    y_b = rglru(xb, gb, conv_w, conv_b, wa, ba, wx, bx, lam)
    return jnp.concatenate([y_a.astype(x.dtype), y_b.astype(x.dtype)], axis=-1)

def s5(u, lam_re, lam_im, b_re, b_im, c_re, c_im, d_skip, log_dt, glu_w, glu_b):
    bsz, s, _ = u.shape
    uf = u.astype(F32).reshape(bsz, s, S5_GROUPS, S5_GROUP)
    lr = lam_re.astype(F32)
    li = lam_im.astype(F32)
    dt = jnp.exp(log_dt.astype(F32))[:, None]
    mag = jnp.exp(lr * dt)
    abar_re = mag * jnp.cos(li * dt)
    abar_im = mag * jnp.sin(li * dt)
    den = lr * lr + li * li
    nr = abar_re - 1.0
    coef_re = (nr * lr + abar_im * li) / den
    coef_im = (abar_im * lr - nr * li) / den
    br = b_re.astype(F32)
    bi = b_im.astype(F32)
    bbar_re = coef_re[..., None] * br - coef_im[..., None] * bi
    bbar_im = coef_re[..., None] * bi + coef_im[..., None] * br
    bu_re = jnp.einsum('bsgh,gph->bsgp', uf, bbar_re)
    bu_im = jnp.einsum('bsgh,gph->bsgp', uf, bbar_im)
    a_re = jnp.broadcast_to(abar_re, (1, s, S5_GROUPS, S5_STATE))
    a_im = jnp.broadcast_to(abar_im, (1, s, S5_GROUPS, S5_STATE))

    def combine(lhs, rhs):
        a1r, a1i, u1r, u1i = lhs
        a2r, a2i, u2r, u2i = rhs
        return (a1r * a2r - a1i * a2i, a1r * a2i + a1i * a2r,
                a2r * u1r - a2i * u1i + u2r, a2r * u1i + a2i * u1r + u2i)

    _, _, xr, xi = lax.associative_scan(combine, (a_re, a_im, bu_re, bu_im), axis=1)
    y = (jnp.einsum('bsgp,ghp->bsgh', xr, c_re.astype(F32)) - jnp.einsum('bsgp,ghp->bsgh', xi, c_im.astype(F32))
         + d_skip.astype(F32).reshape(S5_GROUPS, S5_GROUP) * uf)
    g = jax.nn.gelu(y.reshape(bsz, s, MIX_C)).astype(u.dtype)
    return g * jax.nn.sigmoid(g @ glu_w + glu_b)

def gla(q, k, v, log_alpha, r, norm_w):
    L = GLA_CHUNK
    bsz, _, nh, dk = q.shape
    dv = v.shape[-1]
    qc = to_chunks(q, L) * (dk ** -0.5)
    kc = to_chunks(k, L)
    vc = to_chunks(v, L)
    bcum = jnp.cumsum(to_chunks(log_alpha, L), axis=3)
    b_last = bcum[..., -1, :]
    q_dec = qc * jnp.exp(bcum)
    k_inv = kc * jnp.exp(-bcum)
    k_end = kc * jnp.exp(b_last[..., None, :] - bcum)
    u = jnp.einsum('bhnld,bhnle->bhnde', k_end, vc)

    def step(state, xs):
        g, uu = xs
        return jnp.exp(g)[..., None] * state + uu, state

    _, s_prev = lax.scan(step, jnp.zeros((bsz, nh, dk, dv), F32), (jnp.moveaxis(b_last, 2, 0), jnp.moveaxis(u, 2, 0)))
    s_prev = jnp.moveaxis(s_prev, 0, 2)
    causal = jnp.tril(jnp.ones((L, L), dtype=bool))
    att = jnp.where(causal, jnp.einsum('bhnid,bhnjd->bhnij', q_dec, k_inv), 0.0)
    o = jnp.einsum('bhnij,bhnje->bhnie', att, vc) + jnp.einsum('bhnid,bhnde->bhnie', q_dec, s_prev)
    o = head_norm(from_chunks(o), norm_w, False)
    return o * jax.nn.silu(r.astype(F32))

def odd_mixer(x, w_in, lam_re, lam_im, b_re, b_im, c_re, c_im, d_skip, log_dt, glu_w, glu_b, gate_w, gate_b, norm_w):
    bsz, s, _ = x.shape
    u, q, k, v, r, glow = jnp.split(x @ w_in, ODD_SPLITS, axis=-1)
    y_c = s5(u, lam_re, lam_im, b_re, b_im, c_re, c_im, d_skip, log_dt, glu_w, glu_b)
    log_alpha = jax.nn.log_sigmoid((glow @ gate_w + gate_b).astype(F32)) / GLA_GATE_TEMP
    hk = lambda t, d: t.astype(F32).reshape(bsz, s, GLA_HEADS, d)
    y_d = gla(hk(q, GLA_DK), hk(k, GLA_DK), hk(v, GLA_DV), hk(log_alpha, GLA_DK), r, norm_w)
    return jnp.concatenate([y_c.astype(x.dtype), y_d.astype(x.dtype)], axis=-1)

def moe(x, router_w, router_bias, w_gate, w_up, w_down, sw_gate, sw_up, sw_down):
    bsz, s, d = x.shape
    xt = x.reshape(-1, d)
    t = xt.shape[0]
    scores = jax.nn.sigmoid((xt @ router_w).astype(F32))
    biased = scores + router_bias.astype(F32)
    grp_score = jnp.sum(lax.top_k(biased.reshape(t, N_GROUPS, -1), 2)[0], axis=-1)
    _, grp_idx = lax.top_k(grp_score, TOPK_GROUPS)
    grp_mask = jnp.sum(jax.nn.one_hot(grp_idx, N_GROUPS, dtype=F32), axis=-2) > 0
    exp_mask = jnp.repeat(grp_mask, N_EXPERTS // N_GROUPS, axis=-1)
    _, idx = lax.top_k(jnp.where(exp_mask, biased, -jnp.inf), TOP_K)
    wts = jnp.take_along_axis(scores, idx, axis=-1)
    wts = wts / jnp.sum(wts, axis=-1, keepdims=True) * ROUTED_SCALE
    n_assign = t * TOP_K
    e_flat = idx.reshape(-1)
    tok = jnp.broadcast_to(jnp.arange(t, dtype=jnp.int32)[:, None], (t, TOP_K)).reshape(-1)
    order = jnp.argsort(e_flat)
    e_s = e_flat[order]
    tok_s = tok[order]
    w_s = wts.reshape(-1)[order]
    counts = jnp.bincount(e_flat, length=N_EXPERTS)
    start = jnp.cumsum(counts) - counts
    padded = (counts + MOE_BLOCK - 1) // MOE_BLOCK * MOE_BLOCK
    pend = jnp.cumsum(padded)
    pstart = pend - padded
    pos = pstart[e_s] + jnp.arange(n_assign) - start[e_s]
    n_blocks = n_assign // MOE_BLOCK + N_EXPERTS
    rows = n_blocks * MOE_BLOCK
    row_tok = jnp.zeros((rows,), jnp.int32).at[pos].set(tok_s)
    row_w = jnp.zeros((rows,), F32).at[pos].set(w_s)
    block_e = jnp.minimum(jnp.searchsorted(pend, jnp.arange(n_blocks) * MOE_BLOCK, side='right'), N_EXPERTS - 1)

    def expert_block(args):
        b_tok, b_w, e = args
        xb = xt[b_tok]
        h = jax.nn.silu(xb @ w_gate[e]) * (xb @ w_up[e])
        return (h @ w_down[e]) * b_w[:, None].astype(xt.dtype)

    y_rows = lax.map(expert_block, (row_tok.reshape(n_blocks, MOE_BLOCK), row_w.reshape(n_blocks, MOE_BLOCK), block_e))
    routed = jax.ops.segment_sum(y_rows.reshape(rows, d), row_tok, num_segments=t)
    shared = (jax.nn.silu(xt @ sw_gate) * (xt @ sw_up)) @ sw_down
    return (routed + shared).reshape(bsz, s, d)

def setup_inputs(seed: int = 0) -> dict:
    key = jax.random.key(seed)
    keys = iter(jax.random.split(key, 64))

    def nrm(shape, scale):
        return jax.random.normal(next(keys), shape, F32) * scale

    def gain(shape):
        return 1.0 + nrm(shape, 0.02)

    D = D_MODEL
    x = nrm((BATCH, SEQ, D), 1.0)
    ln1_w = gain((DEPTH, D))
    ln1_b = nrm((DEPTH, D), 0.02)
    ln2_w = gain((DEPTH, D))
    ln2_b = nrm((DEPTH, D), 0.02)
    w_out = nrm((DEPTH, MIX_WIDTH, D), MIX_WIDTH ** -0.5 * BETA)
    w_in_even = nrm((N_EVEN, D, EVEN_IN), D ** -0.5)
    mlstm_gate_b = jnp.concatenate([nrm((N_EVEN, MLSTM_HEADS), 0.1),
                                    jnp.linspace(3.0, 6.0, MLSTM_HEADS, dtype=F32) + nrm((N_EVEN, MLSTM_HEADS), 0.1)], axis=-1)
    mlstm_norm_w = gain((N_EVEN, MIX_A))
    lru_conv_w = nrm((N_EVEN, LRU_CONV, MIX_B), LRU_CONV ** -0.5)
    lru_conv_b = nrm((N_EVEN, MIX_B), 0.02)
    lru_wa = nrm((N_EVEN, LRU_HEADS, LRU_DH, LRU_DH), LRU_DH ** -0.5)
    lru_ba = nrm((N_EVEN, MIX_B), 0.02)
    lru_wx = nrm((N_EVEN, LRU_HEADS, LRU_DH, LRU_DH), LRU_DH ** -0.5)
    lru_bx = nrm((N_EVEN, MIX_B), 0.02)
    a0 = jax.random.uniform(next(keys), (N_EVEN, MIX_B), F32, minval=0.9, maxval=0.999)
    p0 = a0 ** (1.0 / LRU_C)
    lru_lambda = jnp.log(p0) - jnp.log1p(-p0)
    w_in_odd = nrm((N_ODD, D, ODD_IN), D ** -0.5)
    s5_lam_re = -0.5 + nrm((N_ODD, S5_GROUPS, S5_STATE), 0.01)
    s5_lam_im = jnp.pi * jnp.arange(S5_STATE, dtype=F32) + nrm((N_ODD, S5_GROUPS, S5_STATE), 0.01)
    s5_b_re = nrm((N_ODD, S5_GROUPS, S5_STATE, S5_GROUP), S5_GROUP ** -0.5)
    s5_b_im = nrm((N_ODD, S5_GROUPS, S5_STATE, S5_GROUP), S5_GROUP ** -0.5)
    s5_c_re = nrm((N_ODD, S5_GROUPS, S5_GROUP, S5_STATE), S5_STATE ** -0.5)
    s5_c_im = nrm((N_ODD, S5_GROUPS, S5_GROUP, S5_STATE), S5_STATE ** -0.5)
    s5_d = nrm((N_ODD, MIX_C), 1.0)
    s5_log_dt = jax.random.uniform(next(keys), (N_ODD, S5_GROUPS), F32, minval=math.log(1e-3), maxval=math.log(1e-1))
    s5_glu_w = nrm((N_ODD, MIX_C, MIX_C), MIX_C ** -0.5)
    s5_glu_b = nrm((N_ODD, MIX_C), 0.02)
    gla_gate_w = nrm((N_ODD, GLA_GATE_RANK, GLA_HEADS * GLA_DK), GLA_GATE_RANK ** -0.5)
    gla_gate_b = nrm((N_ODD, GLA_HEADS * GLA_DK), 0.02)
    gla_norm_w = gain((N_ODD, MIX_D))
    router_w = nrm((DEPTH, D, N_EXPERTS), D ** -0.5)
    router_bias = nrm((DEPTH, N_EXPERTS), 0.01)
    exp_w_gate = nrm((DEPTH, N_EXPERTS, D, D_EXPERT), D ** -0.5)
    exp_w_up = nrm((DEPTH, N_EXPERTS, D, D_EXPERT), D ** -0.5)
    exp_w_down = nrm((DEPTH, N_EXPERTS, D_EXPERT, D), D_EXPERT ** -0.5 * BETA)
    sh_w_gate = nrm((DEPTH, D, D_SHARED), D ** -0.5)
    sh_w_up = nrm((DEPTH, D, D_SHARED), D ** -0.5)
    sh_w_down = nrm((DEPTH, D_SHARED, D), D_SHARED ** -0.5 * BETA)
    return {'x': x, 'ln1_w': ln1_w, 'ln1_b': ln1_b, 'ln2_w': ln2_w, 'ln2_b': ln2_b, 'w_out': w_out,
            'w_in_even': w_in_even, 'mlstm_gate_b': mlstm_gate_b, 'mlstm_norm_w': mlstm_norm_w,
            'lru_conv_w': lru_conv_w, 'lru_conv_b': lru_conv_b, 'lru_wa': lru_wa, 'lru_ba': lru_ba,
            'lru_wx': lru_wx, 'lru_bx': lru_bx, 'lru_lambda': lru_lambda,
            'w_in_odd': w_in_odd, 's5_lam_re': s5_lam_re, 's5_lam_im': s5_lam_im, 's5_b_re': s5_b_re,
            's5_b_im': s5_b_im, 's5_c_re': s5_c_re, 's5_c_im': s5_c_im, 's5_d': s5_d, 's5_log_dt': s5_log_dt,
            's5_glu_w': s5_glu_w, 's5_glu_b': s5_glu_b, 'gla_gate_w': gla_gate_w, 'gla_gate_b': gla_gate_b,
            'gla_norm_w': gla_norm_w, 'router_w': router_w, 'router_bias': router_bias,
            'exp_w_gate': exp_w_gate, 'exp_w_up': exp_w_up, 'exp_w_down': exp_w_down,
            'sh_w_gate': sh_w_gate, 'sh_w_up': sh_w_up, 'sh_w_down': sh_w_down}

def reference(x, ln1_w, ln1_b, ln2_w, ln2_b, w_out,
              w_in_even, mlstm_gate_b, mlstm_norm_w,
              lru_conv_w, lru_conv_b, lru_wa, lru_ba, lru_wx, lru_bx, lru_lambda,
              w_in_odd, s5_lam_re, s5_lam_im, s5_b_re, s5_b_im, s5_c_re, s5_c_im, s5_d, s5_log_dt,
              s5_glu_w, s5_glu_b, gla_gate_w, gla_gate_b, gla_norm_w,
              router_w, router_bias, exp_w_gate, exp_w_up, exp_w_down,
              sh_w_gate, sh_w_up, sh_w_down):
    h = x
    for layer in range(DEPTH):
        j = layer // 2
        if layer % 2 == 0:
            mixed = even_mixer(h, w_in_even[j], mlstm_gate_b[j], mlstm_norm_w[j], lru_conv_w[j], lru_conv_b[j],
                               lru_wa[j], lru_ba[j], lru_wx[j], lru_bx[j], lru_lambda[j])
        else:
            mixed = odd_mixer(h, w_in_odd[j], s5_lam_re[j], s5_lam_im[j], s5_b_re[j], s5_b_im[j], s5_c_re[j],
                              s5_c_im[j], s5_d[j], s5_log_dt[j], s5_glu_w[j], s5_glu_b[j], gla_gate_w[j],
                              gla_gate_b[j], gla_norm_w[j])
        h = layer_norm(ALPHA * h + mixed @ w_out[layer], ln1_w[layer], ln1_b[layer])
        ffn = moe(h, router_w[layer], router_bias[layer], exp_w_gate[layer], exp_w_up[layer], exp_w_down[layer],
                  sh_w_gate[layer], sh_w_up[layer], sh_w_down[layer])
        h = layer_norm(ALPHA * h + ffn, ln2_w[layer], ln2_b[layer])
    return h


_drawn_inputs = setup_inputs


def setup_inputs(seed=0):
    import zlib

    import numpy as np

    out = dict(_drawn_inputs(seed))
    spreads = {}
    factors = {'mlstm_norm_w': 2.952,
     'lru_ba': 8.0,
     'lru_bx': 8.0,
     's5_lam_re': 8.0,
     's5_b_im': 3.339,
     's5_c_re': 2.978,
     's5_c_im': 2.819,
     's5_glu_b': 7.737,
     'gla_gate_b': 8.0,
     'gla_norm_w': 4.292}
    for name, (base, spread) in spreads.items():
        noise = np.random.default_rng([zlib.crc32(name.encode()), seed]).standard_normal(out[name].shape)
        drawn = base * np.exp(spread * noise) if base else spread * noise
        out[name] = jnp.asarray(drawn.astype(out[name].dtype))
    for name, factor in factors.items():
        out[name] = (out[name] * factor).astype(out[name].dtype)
    return out
```

```python
import numpy as np
from contextlib import ExitStack

import concourse.bass as bass
from concourse import mybir

F32 = mybir.dt.float32
I32 = mybir.dt.int32
ALU = mybir.AluOpType
ACT = mybir.ActivationFunctionType
AX = mybir.AxisListType

P = 128
D = 1024
SEQ = 256
TT = SEQ // P
KC = D // P
NH = 4
DK = 64
LC = 64
NT = 16
NE = 64
NG = 8
TOPK = 8
TOPK_GROUPS = 4
DE = 256
JE = DE // P
CAP = 64
MAX_PASS = SEQ // CAP
NSLOT = 4
PAIRS = NE // 2
ALPHA = 4.0 ** 0.25
EPS = 1e-5
ROUTED_SCALE = 2.5
EW = KC * DE
BIG = 1e30


class Chain:

    def __init__(self, eng, sem):
        self.eng, self.sem, self.n = eng, sem, 0

    def link(self, ins):
        self.n += 1
        ins.then_inc(self.sem, 1)
        self.eng.wait_ge(self.sem, self.n)


class Banks:

    def __init__(self, tiles, full, done_a, done_d, jobs, fixed, turns=8):
        self.tiles, self.full_sem, self.done = tiles, full, {"a": done_a, "d": done_d}
        self.jobs, last, count, turn = {}, {}, {"a": 0, "d": 0}, 0
        for i, (name, reader) in enumerate(jobs):
            b = fixed[name] if name in fixed else turn % turns
            turn += name not in fixed
            if reader:
                count[reader] += 1
            self.jobs[name] = (b, i + 1, reader, count.get(reader, 0), last.get(b))
            last[b] = name

    def tile(self, name):
        return self.tiles[self.jobs[name][0]]

    def full(self, name):
        return self.full_sem, self.jobs[name][1]

    def read(self, name):
        _, _, reader, n, _ = self.jobs[name]
        return self.done[reader], n

    def wait_free(self, pe, name):
        before = self.jobs[name][4]
        if before:
            pe.wait_ge(*self.read(before))


def build(nc, A, out, stages=("mix0", "moe0", "mix1", "moe1"), dumps=None):
    ctx = ExitStack()
    with ctx:
        def sb(name, shape, dt=F32):
            return ctx.enter_context(nc.sbuf_tensor(name, shape, dt))

        def sem(name):
            return ctx.enter_context(nc.semaphore(name))

        def sems(prefix, names):
            return {n: sem(f"{prefix}{n}") for n in names.split()}

        ew = sb("expert_weights", [P, NSLOT, 3 * EW])
        wring = sb("weight_ring", [P, 2, KC * 512])
        h = sb("h", [P, TT, D])
        hT = sb("hT", [P, KC, SEQ])
        resid = sb("resid", [P, TT, D])
        lnw = sb("ln_w", [P, D])
        lnb = sb("ln_b", [P, D])
        ident = sb("ident", [P, P])
        upper = sb("upper_strict", [P, P])
        ones = sb("ones", [P, P])
        iota = sb("slot_iota", [P, CAP])
        gmask = sb("group_before", [P, NG, NG])
        stats = sb("ln_stats", [P, TT, 2, 6])
        mv = sb("ln_mean_var", [P, TT, 2])
        rstd = sb("ln_rstd", [P, TT])
        epsc = sb("eps", [P, 1])
        bank = [ctx.enter_context(nc.psum_tensor(f"bank{i}", [P, 512], F32)) for i in range(8)]
        onehot = sb("onehot", [P, 2, TT, 2, CAP])
        gated = sb("gated_onehot", [P, 2, TT, 2, CAP])
        gatedT = sb("gated_onehotT", [P, 2, TT, P])
        xg = sb("gathered_xT", [P, KC, 2 * CAP])
        sg = sb("silu_gate", [P, 2, JE, CAP])
        hm = sb("hidden", [P, 2, JE, CAP])
        ysb = sb("expert_out", [P, D])
        rw = sb("router_w", [P, KC, NE])
        rbias = sb("router_bias", [P, NE])
        scores = sb("scores", [P, TT, NE])
        biased = sb("biased", [P, TT, NE])
        masked = sb("masked", [P, TT, NE])
        replaced = sb("replaced", [P, TT, NE])
        chosen = sb("chosen", [P, TT, NE])
        wts = sb("wts", [P, TT, NE])
        top8 = sb("top8", [P, TT, NG, 8])
        grp = sb("grp", [P, TT, NG])
        gcmp = sb("gcmp", [P, TT, NG, NG])
        gcmp2 = sb("gcmp2", [P, TT, NG, NG])
        grank = sb("grank", [P, TT, NG])
        best = sb("best", [P, TT, 8])
        wsum = sb("wsum", [P, TT])
        rank = sb("rank", [P, TT, NE])
        cw = sb("combine_w", [P, TT, NE])
        cnt = sb("cnt", [1, 8])
        npass_i = sb("npass", [1, 1], I32)

        ws = ew[:, 2:4, :].rearrange("p s n -> p (s n)")
        rows = sb("gate_rows", [NH, 6, SEQ])
        sel = sb("row_selector", [NH, NH, P])
        wgate = sb("w_gates", [P, KC, 16])
        cols0 = sb("cols_even", [P, 34])
        lamb = sb("lambda_work", [P, 6, NH])
        gcol = sb("gate_cols", [P, 2, TT, NH])
        maskc = sb("causal_floor", [P, SEQ])
        hstat = sb("head_stats", [P, TT, NH, 6])
        hmv = sb("head_mean_var", [P, TT, NH, 2])
        hrs = sb("head_rstd", [P, TT, NH])
        rden = sb("den_inv", [P, NH, TT])

        zin = sb("scan_input", [P, 2, SEQ])
        gate_w = sb("gla_gate_w", [16, NH * DK])
        lowT = sb("gate_low_rankT", [16, SEQ])
        cols1 = sb("cols_odd", [P, 58])
        prm = sb("s5_work", [P, 13, NT])

        S = sems("s_", "x_loaded consts dve_chain act_chain pool_chain h_ready ring_used out_stored")
        LN = [sems(f"ln{k}_", "params stats std") for k in range(4)]
        MO = [sems(f"moe{l}_", "router_in tA tD hT_a hT_d rank_next sh_gu sh_silu sh_hidden sh_used scores_psum scores "
                   "chosen rank_psum npass gather_lo gather_hi onehot gated pt_full pt_ready "
                   "xg_lo xg_hi gu_full silu hidden y_lo_full y_hi_full y_lo y_hi "
                   "acc_full") for l in range(2)]
        M0 = sems("m0_", "params full done_a done_d splus rows em gcol xc lam_exp log_a a_t gain root "
                  "expd hstat hstd yhead y_lru out_full")
        M1 = sems("m1_", "params full done_a done_d zeros dt mag ang sine coef bbar first step_re step_im cneg "
                  "gla_z gla_ln gla_sum gla_last decays ki masked state hstat hstd yhead z x y5 gelu5 sig5 y_s5 "
                  "out_full")
        for l in range(2):
            MO[l]["gu_in"] = [sem(f"moe{l}_gu_in{s}") for s in range(NSLOT)]
            MO[l]["d_in"] = [sem(f"moe{l}_d_in{s}") for s in range(NSLOT)]
        ring_in = [sem(f"ring_in{i}") for i in range(2)]

        ring = []

        def ring_add(name, parts):
            ring.append((name, parts))

        def blk(src, off, cols, chunks=KC):
            return (off, chunks * cols, chunks, src)

        for st in stages:
            l = int(st[-1])
            if st == "mix0":
                w = A["w_in_even"][0].rearrange("(p c) n -> p c n", c=KC)
                for name, off in (("xb", 2056), ("k", 512), ("q", 0), ("v", 1024), ("gb", 2568), ("o", 1536)):
                    ring_add(f"{name}0", [(0, KC, 512, w[:, :, off:off + 512])])
            if st == "mix1":
                w = A["w_in_odd"][0].rearrange("(p c) n -> p c n", c=KC)
                for name, off in (("u", 0), ("qk", 512), ("v", 1024), ("r", 1536)):
                    ring_add(f"{name}1", [(0, KC, 512, w[:, :, off:off + 512])])
                out_b = A["w_out"][1].rearrange("(m p) n -> p m n", p=P)
                ring_add("out_b1", [(0, 4, D, out_b[:, 4:8, :])])
                ring_add("glu1", [(0, 4, 512, A["s5_glu_w"][0].rearrange("(q p) n -> p q n", p=P))])
                ring_add("out_a1", [(0, 4, D, out_b[:, 0:4, :])])
            if st == "mix0":
                w = A["w_out"][l].rearrange("(m p) n -> p m n", p=P)
                ring_add(f"out_b{l}", [(0, 4, D, w[:, 4:8, :])])
                ring_add(f"out_a{l}", [(0, 4, D, w[:, 0:4, :])])
            if st.startswith("moe"):
                g = A["sh_w_gate"][l].rearrange("(p c) f -> p c f", c=KC)
                u = A["sh_w_up"][l].rearrange("(p c) f -> p c f", c=KC)
                d = A["sh_w_down"][l].rearrange("(p j) n -> p j n", j=JE)
                ring_add(f"sh_gu{l}", [(0, KC, DE, g), (EW, KC, DE, u)])
                ring_add(f"sh_d{l}", [(0, JE, D, d)])
        ring_no = {name: n for n, (name, _) in enumerate(ring)}

        def slot_of(name):
            return wring[:, ring_no[name] % 2, :]

        def ring_load(sp, n):
            if n >= 2:
                sp.wait_ge(S["ring_used"], n - 1)
            for off, c, w, src in ring[n][1]:
                sp.dma_start(wring[:, n % 2, off:off + c * w].rearrange("p (c w) -> p c w", w=w), src)\
                  .then_inc(ring_in[n % 2], 16)

        def ring_arrived(eng, name):
            n = ring_no[name]
            parts = sum(len(ring[m][1]) for m in range(n + 1) if m % 2 == n % 2)
            eng.wait_ge(ring_in[n % 2], 16 * parts)

        def ew_g(s):
            return ew[:, s, 0:EW].rearrange("p (c q j) -> p c j q", c=KC, j=JE)

        def ew_u(s):
            return ew[:, s, EW:2 * EW].rearrange("p (c q j) -> p c j q", c=KC, j=JE)

        def ew_d(s):
            return ew[:, s, 2 * EW:3 * EW].rearrange("p (j n) -> p j n", j=JE)

        stage_no = {st: k for k, st in enumerate(stages)}
        block = ctx.enter_context(nc.Block())

        def wait_h(eng, st):
            k = stage_no[st]
            if k == 0:
                eng.wait_ge(S["x_loaded"], 16)
            else:
                eng.wait_ge(S["h_ready"], k)

        def expert_load(sp, m, l, e, s):
            src_g = A["exp_w_gate"][l, e].rearrange("(p c) f -> p (c f)", c=KC)
            src_u = A["exp_w_up"][l, e].rearrange("(p c) f -> p (c f)", c=KC)
            sp.dma_start(ew[:, s, 0:EW], src_g).then_inc(m["gu_in"][s], 16)
            sp.dma_start(ew[:, s, EW:2 * EW], src_u).then_inc(m["gu_in"][s], 16)

        def down_src(l, e):
            return A["exp_w_down"][l, e].rearrange("(p j) n -> p (j n)", j=JE)

        def sp_ln_params(sp, k, w, b):
            if k:
                sp.wait_ge(S["h_ready"], k)
            sp.dma_start(lnw[:, :], w.partition_broadcast(P)).then_inc(LN[k]["params"], 16)
            sp.dma_start(lnb[:, :], b.partition_broadcast(P)).then_inc(LN[k]["params"], 16)

        def sp_mix0(sp):
            k = stage_no["mix0"]
            for dst, src in ((wgate[:, :, 0:8], A["w_in_even"][0].rearrange("(p c) n -> p c n", c=KC)[:, :, 2048:2056]),
                             (cols0[:, :], A["cols_even"]),
                             (gated[:, :, :, :, :].rearrange("p u t a s -> p (u t a s)").rearrange("p (h j) -> p h j", h=NH),
                              A["lru_wa"][0].rearrange("h i j -> i h j")),
                             (gatedT[:, :, :, :].rearrange("p u t s -> p (u t s)").rearrange("p (h j) -> p h j", h=NH),
                              A["lru_wx"][0].rearrange("h i j -> i h j")),
                             (onehot[:, :, :, :, :].rearrange("p u t a s -> p (u t a s)"),
                              A["mlstm_norm_w"][0].partition_broadcast(P))):
                sp.dma_start(dst, src).then_inc(M0["params"], 16)
            for name in ("xb0", "k0", "q0", "v0", "gb0", "o0", "out_b0", "out_a0"):
                ring_load(sp, ring_no[name])
            sp_ln_params(sp, k, A["ln1_w"][0], A["ln1_b"][0])

        def sp_mix1(sp):
            k = stage_no["mix1"]
            if k:
                sp.wait_ge(S["h_ready"], k)
            for dst, src in ((cols1[:, :], A["cols_odd"]),
                             (xg[:, :, :].rearrange("p c s -> p (c s)"), A["b_odd"]),
                             (resid[:, 1, :], A["c_odd"]),
                             (wgate[:, :, :], A["w_in_odd"][0].rearrange("(p c) n -> p c n", c=KC)[:, :, 2048:2064]),
                             (gate_w[:, :], A["gla_gate_w"][0]),
                             (onehot[:, :, :, :, :].rearrange("p u t a s -> p (u t a s)"),
                              A["gla_norm_w"][0].partition_broadcast(P))):
                sp.dma_start(dst, src).then_inc(M1["params"], 16)
            for name in ("u1", "qk1", "v1", "r1", "out_b1", "glu1", "out_a1"):
                ring_load(sp, ring_no[name])
            sp_ln_params(sp, k, A["ln1_w"][1], A["ln1_b"][1])

        def sp_moe(sp, l):
            m = MO[l]
            k = stage_no[f"moe{l}"]
            if k:
                sp.wait_ge(S["h_ready"], k)
            sp.dma_start(rw[:, :, :], A["router_w"][l].rearrange("(p c) e -> p c e", c=KC))\
              .then_inc(m["router_in"], 16)
            sp.dma_start(rbias[:, :], A["router_bias"][l].partition_broadcast(P)).then_inc(m["router_in"], 16)
            for s in range(NSLOT):
                expert_load(sp, m, l, s, s)
                sp.dma_start(ew[:, s, 2 * EW:3 * EW], down_src(l, s)).then_inc(m["d_in"][s], 16)
            ring_load(sp, ring_no[f"sh_gu{l}"])
            ring_load(sp, ring_no[f"sh_d{l}"])
            sp_ln_params(sp, k, A["ln2_w"][l], A["ln2_b"][l])

            def group(base, it):
                for s in range(NSLOT):
                    sp.wait_ge(m["gu_full"], (base - 1) * NSLOT + s + 1)
                    expert_load(sp, m, l, it * NSLOT + s, s)
                    if s % 2:
                        sp.wait_ge(m["y_hi_full"], (base - 1) * 2 + s // 2 + 1)
                        for q in (s - 1, s):
                            sp.dma_start(ew[:, q, 2 * EW:3 * EW], down_src(l, it * NSLOT + q)).then_inc(m["d_in"][q], 16)

            with sp.Fori(1, NE // NSLOT) as it:
                group(it, it)
            sp.wait_ge(m["npass"], 1)
            npass = sp.value_load(npass_i[0:1, 0:1], min_val=1, max_val=MAX_PASS)
            with sp.If(npass > 1):
                with sp.Fori(1, npass) as ps:
                    with sp.Fori(0, NE // NSLOT) as it:
                        group(ps * (NE // NSLOT) + it, it)

        @block.sync
        def _(sp):
            sp.dma_start(h[:, :, :], A["x"][0].rearrange("(t p) d -> p t d", p=P)).then_inc(S["x_loaded"], 16)
            for st in stages:
                if st == "mix0":
                    sp_mix0(sp)
                if st == "mix1":
                    sp_mix1(sp)
                if st.startswith("moe"):
                    sp_moe(sp, int(st[-1]))
            sp.wait_ge(S["h_ready"], len(stages))
            sp.dma_start(out[0].rearrange("(t p) d -> p t d", p=P), h[:, :, :]).then_inc(S["out_stored"], 16)
            sp.wait_ge(S["out_stored"], 16)

        def view(off, *shape, base=ws):
            n = int(np.prod(shape))
            v = base[:, off:off + n]
            if len(shape) == 2:
                v = v.rearrange("p (a b) -> p a b", a=shape[0])
            if len(shape) == 3:
                v = v.rearrange("p (a b c) -> p a b c", a=shape[0], b=shape[1])
            return v

        DH = 128
        views, at = {}, 0
        for name, shape in (("qT", (NH, SEQ)), ("kT", (NH, SEQ)), ("v1", (TT, NH, DH + 1)), ("og", (TT, 512)),
                            ("xbp", (NH, SEQ + 3)), ("xc", (NH, SEQ)), ("rg", (NH, SEQ)), ("ig", (NH, SEQ)),
                            ("gg", (NH, SEQ)), ("mixT", (8, SEQ))):
            views[name] = view(at, *shape)
            at += int(np.prod(shape))
        V = dict(views)
        argw = sb("decay_scores", [P, NH, SEQ + P])
        hbuf = resid[:, 0, :].rearrange("p (t n) -> p t n", t=TT)
        abuf = ysb[:, :].rearrange("p (h t) -> p h t", h=NH)
        tbuf = resid[:, 1, :].rearrange("p (h t) -> p h t", h=NH)
        wa_v = gated[:, :, :, :, :].rearrange("p u t a s -> p (u t a s)").rearrange("p (h j) -> p h j", h=NH)
        wx_v = gatedT[:, :, :, :].rearrange("p u t s -> p (u t s)").rearrange("p (h j) -> p h j", h=NH)
        normw = onehot[:, :, :, :, :].rearrange("p u t a s -> p (u t a s)")
        B0 = Banks(bank, M0["full"], M0["done_a"], M0["done_d"],
                   [("T0", "a"), ("T1", "d"), ("T2", "a"), ("T3", "d"), ("gates", "d"), ("xb0", "a"), ("xb1", "a"),
                    ("k0", "a"), ("k1", "a"), ("q0", "a"), ("q1", "a"), ("cols", "d"), ("bc0", "d"), ("bc1", "d"),
                    ("r0", "a"), ("r1", "a"), ("i0", "a"), ("i1", "a"), ("v0", "a"), ("v1", "a"),
                    ("S0", "d"), ("S1", "d"), ("S2", "d"), ("S3", "d"), ("gb0", "a"), ("gb1", "a"),
                    ("N0", "d"), ("N1", "d"), ("N2", "d"), ("N3", "d"), ("o0", "a"), ("o1", "a"),
                    ("out0", None), ("out1", None), ("out2", None), ("out3", None), ("yT0", "a"), ("yT1", "d")],
                   {"out0": 0, "out1": 1, "out2": 2, "out3": 3, "yT0": 4, "yT1": 5})

        ws1 = ew[:, :, :].rearrange("p s n -> p (s n)")
        views, at = {}, 0
        for name, shape in (("cos", (NT, SEQ)), ("sin", (NT, SEQ)), ("uT", (4, SEQ)), ("v", (TT, 512)),
                            ("og", (TT, 512)), ("mixT", (8, SEQ)), ("gT", (4, SEQ)), ("la", (2, SEQ)),
                            ("e1", (2, SEQ)), ("bc", (2, SEQ)), ("e2", (2, SEQ)), ("e3", (2, SEQ)), ("qd", (2, SEQ)),
                            ("ki", (2, SEQ)), ("ke", (2, SEQ)), ("att", (NH, TT, P)), ("m1", (2, SEQ)),
                            ("m2", (2, SEQ)), ("z", (4, 2, SEQ)), ("x", (4, 2, SEQ))):
            views[name] = view(at, *shape, base=ws1)
            at += int(np.prod(shape))
        W = dict(views)
        W["ke_tok"] = W["la"]
        W["state"] = argw[:, :, :].rearrange("p h n -> p (h n)").rearrange("p (c q n) -> p c q n", c=3, q=4)
        W["braw"] = xg[:, :, :].rearrange("p c s -> p (c s)").rearrange("p (w i n) -> p w i n", w=2, i=NT)
        W["craw"] = resid[:, 1, :].rearrange("p (w i n) -> p w i n", w=2, i=NT)
        W["bT"] = ysb[:, :].rearrange("p (w q n) -> p w q n", w=2, q=4)
        W["bbar"] = W["z"].rearrange("p a b n -> p (a b n)").rearrange("p (w i n) -> p w i n", w=4, i=NT)
        W["p1"] = gated[:, :, :, :, :].rearrange("p u t a s -> p (u t a s)").rearrange("p (w n) -> p w n", w=2)
        W["p2"] = gatedT[:, :, :, :].rearrange("p u t s -> p (u t s)").rearrange("p (w n) -> p w n", w=2)
        restart = maskc
        odd_jobs = [("T0", "a"), ("T1", "d"), ("T2", "a"), ("T3", "d"), ("low", "a"), ("u0", "a"), ("u1", "a"),
                    ("ga", "d"), ("bT0", "a"), ("bT1", "a")]
        odd_jobs += [(f"bu{i}", "d") for i in range(4)] + [("qk0", "d"), ("qk1", "d")]
        odd_jobs += [(f"bu{i}", "d") for i in range(4, 8)] + [("v0", "a"), ("v1", "a"), ("att0", "a"), ("att1", "a"),
                                                             ("keT", "a")]
        odd_jobs += [(f"bu{i}", "d") for i in range(8, 12)] + [("U0", "d"), ("U1", "d"), ("U2", "d"), ("o0", "d"),
                                                              ("o1", "d"), ("r0", "a"), ("r1", "a")]
        odd_jobs += [("yT0", "a"), ("yT1", "a"), ("bu12", "d"), ("bu13", "d"), ("out0", None), ("out1", None),
                     ("out2", None), ("out3", None), ("bu14", "d"), ("bu15", "d"), ("y0", "d"), ("y1", "d"),
                     ("gl0", "a"), ("gl1", "a")]
        B1 = Banks(bank, M1["full"], M1["done_a"], M1["done_d"], odd_jobs,
                   {"out0": 0, "out1": 1, "out2": 2, "out3": 3, "yT0": 4, "yT1": 5, "bu12": 4, "bu13": 5,
                    "bu14": 4, "bu15": 5, "y0": 6, "y1": 7, "gl0": 4, "gl1": 5}, turns=6)
        N_STEPS = 8

        def pool_mix1(pool, chain):
            if stage_no["mix1"]:
                pool.wait_ge(S["h_ready"], stage_no["mix1"])
            nc.gpsimd.memset(restart[:, :], 1.0)
            nc.gpsimd.memset(W["att"], 0.0)
            chain.link(nc.gpsimd.memset(W["state"], 0.0))
            nc.gpsimd.memset(restart[:, 0:SEQ:LC], 0.0).then_inc(M1["zeros"], 1)
            for k in range(N_STEPS):
                n = 1 << k
                pool.wait_ge(M1["step_im"], k + 1)
                pool.wait_ge(M1["step_re"], k + 1)
                new = W["cos"][:, :, n:2 * n]
                tmp = W["gT"].rearrange("p a t -> p (a t)")[:, 0:NT * n].rearrange("p (i t) -> p i t", i=NT) if n <= 64 \
                    else W["mixT"].rearrange("p a t -> p (a t)").rearrange("p (i t) -> p i t", i=NT)
                cr = W["cos"][:, :, n - 1:n].broadcast_to([P, NT, n])
                ci = W["sin"][:, :, n - 1:n].broadcast_to([P, NT, n])
                nc.gpsimd.tensor_tensor(new, W["cos"][:, :, 0:n], cr, ALU.mult)
                chain.link(nc.gpsimd.tensor_tensor(tmp, W["sin"][:, :, 0:n], ci, ALU.mult))
                nc.gpsimd.tensor_tensor(new, new, tmp, ALU.subtract).then_inc(M1["step_re"], 1)
                if k == 4:
                    pool_bbar(pool, chain)
            for i in range(NT):
                pool_rotate(pool, chain, i)
                if i == 7:
                    pool.wait_ge(*B1.read("att1"))
                    pool.wait_ge(M1["x"], 8)
                    for b in range(2):
                        part = W["att"].rearrange("p h t s -> p (h t) s")[b * LC:(b + 1) * LC, :, b * LC:(b + 1) * LC]
                        nc.gpsimd.affine_select(out=part, in_=part, compare_op=ALU.is_ge, fill=0.0, base=0,
                                                pattern=[[0, NH * TT], [1, LC]], channel_multiplier=-1)\
                                 .then_inc(M1["masked"], 1)
                        pool.wait_ge(M1["masked"], b + 1)

        def pool_bbar(pool, chain):
            pool.wait_ge(M1["params"], 96)
            pool.wait_ge(M1["coef"], 1)
            cr = prm[:, 8, :].unsqueeze(2).broadcast_to([P, NT, 32])
            ci = prm[:, 9, :].unsqueeze(2).broadcast_to([P, NT, 32])
            nc.gpsimd.tensor_tensor(W["bbar"][:, 0], W["braw"][:, 0], cr, ALU.mult)
            nc.gpsimd.tensor_tensor(W["bbar"][:, 1], W["braw"][:, 1], cr, ALU.mult)
            nc.gpsimd.tensor_tensor(W["bbar"][:, 2], W["braw"][:, 1], ci, ALU.mult)
            chain.link(nc.gpsimd.tensor_tensor(W["bbar"][:, 3], W["braw"][:, 0], ci, ALU.mult))
            nc.gpsimd.tensor_tensor(W["bbar"][:, 0], W["bbar"][:, 0], W["bbar"][:, 2], ALU.subtract)
            nc.gpsimd.tensor_tensor(W["bbar"][:, 1], W["bbar"][:, 1], W["bbar"][:, 3], ALU.add).then_inc(M1["bbar"], 1)

        def pool_rotate(pool, chain, i):
            q = i % 4
            pool.wait_ge(M1["z"], i + 1)
            if i == 0:
                pool.wait_ge(M1["step_im"], N_STEPS + 1)
                pool.wait_ge(M1["step_re"], N_STEPS + 1)
            if i >= 1:
                pool.wait_ge(M1["x"], i)
            if i >= 4:
                pool.wait_ge(M1["y5"], i - 3)
            c = W["cos"][:, i, :].unsqueeze(1).broadcast_to([P, 2, SEQ])
            sn = W["sin"][:, i, :].unsqueeze(1).broadcast_to([P, 2, SEQ])
            nc.gpsimd.tensor_tensor(W["p1"], W["z"][:, q], c, ALU.mult)
            chain.link(nc.gpsimd.tensor_tensor(W["p2"], W["z"][:, q], sn, ALU.mult))
            nc.gpsimd.tensor_tensor(W["x"][:, q, 0, :], W["p1"][:, 0, :], W["p2"][:, 1, :], ALU.subtract)
            nc.gpsimd.tensor_tensor(W["x"][:, q, 1, :], W["p1"][:, 1, :], W["p2"][:, 0, :], ALU.add).then_inc(M1["x"], 1)

        @block.gpsimd
        def _(pool):
            chain = Chain(pool, S["pool_chain"])
            chain.link(nc.gpsimd.memset(ident[:, :], 0.0))
            nc.gpsimd.affine_select(out=ident[:, :], in_=ident[:, :], compare_op=ALU.not_equal, fill=1.0,
                                    base=0, pattern=[[-1, P]], channel_multiplier=1).then_inc(S["consts"], 1)
            chain.link(nc.gpsimd.memset(upper[:, :], 1.0))
            nc.gpsimd.affine_select(out=upper[:, :], in_=upper[:, :], compare_op=ALU.is_gt, fill=0.0,
                                    base=0, pattern=[[1, P]], channel_multiplier=-1).then_inc(S["consts"], 1)
            nc.gpsimd.memset(ones[:, :], 1.0).then_inc(S["consts"], 1)
            nc.gpsimd.iota(iota[:, :], pattern=[[1, CAP]], base=0, channel_multiplier=0,
                           allow_small_or_imprecise_dtypes=True).then_inc(S["consts"], 1)
            chain.link(nc.gpsimd.memset(gmask[:, :, :], 1.0))
            nc.gpsimd.affine_select(out=gmask[:, :, :], in_=gmask[:, :, :], compare_op=ALU.is_gt, fill=0.0,
                                    base=0, pattern=[[1, NG], [-1, NG]], channel_multiplier=0)\
                     .then_inc(S["consts"], 1)
            chain.link(nc.gpsimd.memset(maskc[:, :], 0.0))
            nc.gpsimd.affine_select(out=maskc[:, 0:P], in_=maskc[:, 0:P], compare_op=ALU.is_ge, fill=-BIG,
                                    base=0, pattern=[[1, P]], channel_multiplier=-1).then_inc(S["consts"], 1)
            chain.link(nc.gpsimd.memset(sel[:, :, :], 0.0))
            nc.gpsimd.affine_select(out=sel[:, :, :], in_=sel[:, :, :], compare_op=ALU.not_equal, fill=1.0,
                                    base=0, pattern=[[-1, NH], [0, P]], channel_multiplier=1).then_inc(S["consts"], 1)
            nc.gpsimd.memset(epsc[:, :], EPS).then_inc(S["consts"], 1)

            if "mix1" in stages:
                pool_mix1(pool, chain)

        N_CONSTS = 8

        def channel_major(pe, B, w, name, i):
            B.wait_free(pe, f"{name}{i}")
            for a in range(2):
                for c in range(KC):
                    last = nc.tensor.matmul(B.tile(f"{name}{i}")[:, a * SEQ:(a + 1) * SEQ],
                                            w[:, c, (2 * i + a) * P:(2 * i + a + 1) * P], hT[:, c, :],
                                            start=(c == 0), stop=(c == KC - 1))
            last.then_inc(B.full_sem, 1)
            return last

        def token_major(pe, B, w, name, t):
            B.wait_free(pe, f"{name}{t}")
            for c in range(KC):
                last = nc.tensor.matmul(B.tile(f"{name}{t}")[:, :], hT[:, c, t * P:(t + 1) * P], w[:, c, :],
                                        start=(c == 0), stop=(c == KC - 1))
            last.then_inc(B.full_sem, 1)

        def ring_view(name, chunks=KC):
            return slot_of(name).rearrange("p (c n) -> p c n", c=chunks)

        def ring_done(pe, B, name):
            pe.wait_ge(*B.full(name))
            pe.sem_inc(S["ring_used"], 1)

        def pe_transposes(pe, B):
            for b in range(4):
                for c in (2 * b, 2 * b + 1):
                    for t in range(TT):
                        last = nc.tensor.transpose(B.tile(f"T{b}")[:, (c % 2) * SEQ + t * P:(c % 2) * SEQ + (t + 1) * P],
                                                   h[:, t, :].rearrange("p (q c) -> p c q", c=KC)[:, c, :],
                                                   ident[:, :])
                last.then_inc(B.full_sem, 1)
            for b in range(4):
                pe.wait_ge(*B.read(f"T{b}"))

        def pe_out(pe, B, l, mixT, done_sem, part, names):
            ring_arrived(pe, f"out_{part}{l}")
            w = ring_view(f"out_{part}{l}", 4)
            first = part == "b"
            for t in range(TT):
                for n in range(2):
                    if first:
                        B.wait_free(pe, f"out{2 * t + n}")
                    for m in range(4):
                        last = nc.tensor.matmul(bank[2 * t + n][:, :], mixT[:, m + 4 * first, t * P:(t + 1) * P],
                                                w[:, m, n * 512:(n + 1) * 512],
                                                start=(first and m == 0), stop=(not first and m == 3))
                    if first:
                        last.then_inc(B.full_sem, 1)
            return last

        def pe_mix0(pe):
            B = B0
            wait_h(pe, "mix0")
            pe_transposes(pe, B)
            pe.wait_ge(M0["params"], 80)
            B.wait_free(pe, "gates")
            for g in range(2):
                for c in range(KC):
                    last = nc.tensor.matmul(B.tile("gates")[0:NH, g * SEQ:(g + 1) * SEQ], wgate[:, c, g * NH:(g + 1) * NH],
                                            hT[:, c, :], start=(c == 0), stop=(c == KC - 1))
            last.then_inc(B.full_sem, 1)
            for name in ("xb", "k", "q"):
                ring_arrived(pe, f"{name}0")
                channel_major(pe, B, ring_view(f"{name}0"), name, 0)
                channel_major(pe, B, ring_view(f"{name}0"), name, 1)
                ring_done(pe, B, f"{name}1")
            B.wait_free(pe, "cols")
            pe.wait_ge(M0["rows"], 1)
            pe.wait_ge(M0["em"], 1)
            for i, row in enumerate((0, 5)):
                for t in range(TT):
                    last = nc.tensor.transpose(B.tile("cols")[:, (i * TT + t) * NH:(i * TT + t + 1) * NH],
                                               rows[:, row, t * P:(t + 1) * P], ident[0:NH, 0:NH])
            last.then_inc(B.full_sem, 1)
            for i in range(2):
                B.wait_free(pe, f"bc{i}")
                for a in range(2):
                    last = nc.tensor.matmul(B.tile(f"bc{i}")[:, a * SEQ:(a + 1) * SEQ], sel[:, 2 * i + a, :],
                                            rows[:, 4, :], start=True, stop=True)
                last.then_inc(B.full_sem, 1)
            pe.wait_ge(M0["xc"], 1)
            for name, w in (("r", wa_v), ("i", wx_v)):
                for i in range(2):
                    B.wait_free(pe, f"{name}{i}")
                    for a in range(2):
                        last = nc.tensor.matmul(B.tile(f"{name}{i}")[:, a * SEQ:(a + 1) * SEQ], w[:, 2 * i + a, :],
                                                V["xc"][:, 2 * i + a, :], start=True, stop=True)
                    last.then_inc(B.full_sem, 1)
            ring_arrived(pe, "v0")
            for t in range(TT):
                token_major(pe, B, ring_view("v0"), "v", t)
            ring_done(pe, B, "v1")
            pe.wait_ge(*B.read("q1"))
            for hd in range(NH):
                B.wait_free(pe, f"S{hd}")
                nc.tensor.matmul(B.tile(f"S{hd}")[:, 0:SEQ], V["kT"][:, hd, 0:P], V["qT"][:, hd, :], start=True, stop=True)
                nc.tensor.matmul(B.tile(f"S{hd}")[:, SEQ:SEQ + P], V["kT"][:, hd, P:SEQ], V["qT"][:, hd, P:SEQ],
                                 start=True, stop=True).then_inc(B.full_sem, 1)
            ring_arrived(pe, "gb0")
            for i in range(2):
                channel_major(pe, B, ring_view("gb0"), "gb", i)
            ring_done(pe, B, "gb1")
            pe.wait_ge(*B.read("v1"))
            for hd in range(NH):
                B.wait_free(pe, f"N{hd}")
                pe.wait_ge(*B.read(f"S{hd}"))
                acc = B.tile(f"N{hd}")
                nc.tensor.matmul(acc[:, 0:DH + 1], argw[:, hd, 0:P], V["v1"][:, 0, hd, :], start=True, stop=True)
                nc.tensor.matmul(acc[:, SEQ:SEQ + DH + 1], argw[:, hd, P:SEQ], V["v1"][:, 0, hd, :], start=True, stop=False)
                nc.tensor.matmul(acc[:, SEQ:SEQ + DH + 1], argw[:, hd, SEQ:SEQ + P], V["v1"][:, 1, hd, :],
                                 start=False, stop=True).then_inc(B.full_sem, 1)
            ring_arrived(pe, "o0")
            for t in range(TT):
                token_major(pe, B, ring_view("o0"), "o", t)
            ring_done(pe, B, "o1")
            pe.wait_ge(M0["y_lru"], 1)
            pe_out(pe, B, 0, V["mixT"], None, "b", None)
            ring_done(pe, B, "out3")
            pe.wait_ge(M0["yhead"], 1)
            pe_head_transposes(pe, B)
            pe_out(pe, B, 0, V["mixT"], None, "a", None).then_inc(M0["out_full"], 1)
            pe.wait_ge(M0["out_full"], 1)
            pe.sem_inc(S["ring_used"], 1)

        def pe_mix1(pe):
            B = B1
            wait_h(pe, "mix1")
            pe_transposes(pe, B)
            pe.wait_ge(M1["params"], 96)
            B.wait_free(pe, "low")
            for c in range(KC):
                last = nc.tensor.matmul(B.tile("low")[0:16, 0:SEQ], wgate[:, c, :], hT[:, c, :],
                                        start=(c == 0), stop=(c == KC - 1))
            last.then_inc(B.full_sem, 1)
            ring_arrived(pe, "u1")
            for i in range(2):
                channel_major(pe, B, ring_view("u1"), "u", i)
            ring_done(pe, B, "u1")
            B.wait_free(pe, "ga")
            pe.wait_ge(*B.read("low"))
            for a in range(2):
                last = nc.tensor.matmul(B.tile("ga")[:, a * SEQ:(a + 1) * SEQ], gate_w[:, a * P:(a + 1) * P],
                                        lowT[:, :], start=True, stop=True)
            last.then_inc(B.full_sem, 1)
            pe.wait_ge(M1["bbar"], 1)
            for w in range(2):
                B.wait_free(pe, f"bT{w}")
                for q in range(4):
                    last = nc.tensor.transpose(B.tile(f"bT{w}")[:, q * P:(q + 1) * P],
                                               W["bbar"][:, w, 4 * q:4 * q + 4, :].rearrange("p i n -> p (i n)"),
                                               ident[:, :])
                last.then_inc(B.full_sem, 1)
            pe.wait_ge(*B.read("bT1"))

            def inputs(tiles):
                for i in tiles:
                    q, j = i // 4, 32 * (i % 4)
                    B.wait_free(pe, f"bu{i}")
                    for w in range(2):
                        last = nc.tensor.matmul(B.tile(f"bu{i}")[:, w * SEQ:(w + 1) * SEQ], W["bT"][j:j + 32, w, q, :],
                                                W["uT"][j:j + 32, q, :], start=True, stop=True)
                    last.then_inc(B.full_sem, 1)

            def outputs(tiles):
                for i in tiles:
                    q, j = i // 4, 32 * (i % 4)
                    pe.wait_ge(M1["x"], i + 1)
                    for w in range(2):
                        last = nc.tensor.matmul(bank[6 + q // 2][j:j + 32, (q % 2) * SEQ:(q % 2 + 1) * SEQ],
                                                W["craw"][:, w, i, :], W["x"][:, i % 4, w, :], start=(w == 0), stop=(w == 1))
                    last.then_inc(M1["y5"], 1)

            inputs(range(0, 4))
            ring_arrived(pe, "qk1")
            for i in range(2):
                channel_major(pe, B, ring_view("qk1"), "qk", i)
            ring_done(pe, B, "qk1")
            pe.wait_ge(M1["cneg"], 1)
            outputs(range(0, 4))
            inputs(range(4, 8))
            ring_arrived(pe, "v1")
            for t in range(TT):
                token_major(pe, B, ring_view("v1"), "v", t)
            ring_done(pe, B, "v1")
            pe.wait_ge(*B.read("qk1"))
            for hh in range(2):
                B.wait_free(pe, f"att{hh}")
                for pr in range(2):
                    for t in range(TT):
                        last = nc.tensor.matmul(B.tile(f"att{hh}")[:, (2 * pr + t) * P:(2 * pr + t + 1) * P],
                                                W["ki"][hh * DK:(hh + 1) * DK, pr, t * P:(t + 1) * P],
                                                W["qd"][hh * DK:(hh + 1) * DK, pr, t * P:(t + 1) * P],
                                                start=True, stop=True)
                last.then_inc(B.full_sem, 1)
            B.wait_free(pe, "keT")
            for pr in range(2):
                for t in range(TT):
                    last = nc.tensor.transpose(B.tile("keT")[:, (2 * pr + t) * P:(2 * pr + t + 1) * P],
                                               W["ke"][:, pr, t * P:(t + 1) * P], ident[:, :])
            last.then_inc(B.full_sem, 1)
            outputs(range(4, 8))
            inputs(range(8, 12))
            pe.wait_ge(*B.read("keT"))
            pe.wait_ge(*B.read("v1"))
            for c in range(3):
                t, lo = c // 2, (c % 2) * LC
                B.wait_free(pe, f"U{c}")
                for hd in range(NH):
                    last = nc.tensor.matmul(B.tile(f"U{c}")[:, hd * P:(hd + 1) * P],
                                            W["ke_tok"].rearrange("p a n -> p (a n)")[lo:lo + LC, (2 * (hd // 2) + t) * P:
                                                                                   (2 * (hd // 2) + t + 1) * P],
                                            W["v"][lo:lo + LC, t, hd * P:(hd + 1) * P], start=True, stop=True)
                last.then_inc(B.full_sem, 1)
            pe.wait_ge(M1["masked"], 2)
            pe.wait_ge(*B.read("U2"))
            for t in range(TT):
                B.wait_free(pe, f"o{t}")
                for hd in range(NH):
                    dst = B.tile(f"o{t}")[:, hd * P:(hd + 1) * P]
                    last = nc.tensor.matmul(dst, W["att"][:, hd, t, :], W["v"][:, t, hd * P:(hd + 1) * P], start=True,
                                            stop=False, skip_group_check=True)
                    for b in range(2):
                        c = 2 * t + b
                        if c > 0:
                            last = nc.tensor.matmul(dst[b * LC:(b + 1) * LC, :], W["qd"][:, hd // 2, c * LC:(c + 1) * LC],
                                                    W["state"][:, c - 1, hd, :], start=False, stop=True,
                                                    skip_group_check=True)
                last.then_inc(B.full_sem, 1)
            ring_arrived(pe, "r1")
            for t in range(TT):
                token_major(pe, B, ring_view("r1"), "r", t)
            ring_done(pe, B, "r1")
            outputs(range(8, 12))
            pe.wait_ge(M1["yhead"], 1)
            pe_head_transposes(pe, B)
            inputs((12, 13))
            pe_out(pe, B, 1, W["mixT"], None, "b", None)
            ring_done(pe, B, "out3")
            inputs((14, 15))
            outputs(range(12, 16))
            pe.wait_ge(M1["y5"], NT)
            pe.sem_inc(B.full_sem, 2)
            ring_arrived(pe, "glu1")
            pe.wait_ge(M1["gelu5"], 1)
            for i in range(2):
                B.wait_free(pe, f"gl{i}")
                for a in range(2):
                    for q in range(4):
                        last = nc.tensor.matmul(B.tile(f"gl{i}")[:, a * SEQ:(a + 1) * SEQ],
                                                ring_view("glu1", 8)[:, q, (2 * i + a) * P:(2 * i + a + 1) * P],
                                                W["gT"][:, q, :], start=(q == 0), stop=(q == 3))
                last.then_inc(B.full_sem, 1)
            ring_done(pe, B, "gl1")
            pe.wait_ge(M1["y_s5"], 1)
            pe_out(pe, B, 1, W["mixT"], None, "a", None).then_inc(M1["out_full"], 1)
            pe.wait_ge(M1["out_full"], 1)
            pe.sem_inc(S["ring_used"], 1)

        def pe_head_transposes(pe, B):
            for i in range(2):
                B.wait_free(pe, f"yT{i}")
                for a in range(2):
                    for t in range(TT):
                        last = nc.tensor.transpose(B.tile(f"yT{i}")[:, a * SEQ + t * P:a * SEQ + (t + 1) * P],
                                                   hbuf[:, t, (2 * i + a) * P:(2 * i + a + 1) * P], ident[:, :])
                last.then_inc(B.full_sem, 1)
            for i in range(2):
                pe.wait_ge(*B.read(f"yT{i}"))

        def pe_transpose_h(pe, m):
            for c in range(KC):
                for t in range(TT):
                    last = nc.tensor.transpose(bank[c // 2][:, (c % 2) * SEQ + t * P:(c % 2) * SEQ + (t + 1) * P],
                                               h[:, t, :].rearrange("p (q c) -> p c q", c=KC)[:, c, :],
                                               ident[:, :])
                if c % 2 == 1:
                    last.then_inc(m["tA"] if (c // 2) % 2 == 0 else m["tD"], 1)

        def pe_moe(pe, l):
            m = MO[l]
            wait_h(pe, f"moe{l}")
            pe_transpose_h(pe, m)
            pe.wait_ge(m["hT_a"], 2)
            pe.wait_ge(m["hT_d"], 2)
            pe.wait_ge(m["router_in"], 32)
            for t in range(TT):
                for c in range(KC):
                    last = nc.tensor.matmul(bank[6][:, t * NE:(t + 1) * NE], hT[:, c, t * P:(t + 1) * P],
                                            rw[:, c, :], start=(c == 0), stop=(c == KC - 1))
            last.then_inc(m["scores_psum"], 1)
            ring_arrived(pe, f"sh_gu{l}")
            sl = slot_of(f"sh_gu{l}")
            for w, b in ((0, 4), (1, 5)):
                wv = sl[:, w * EW:(w + 1) * EW].rearrange("p (c q j) -> p c j q", c=KC, j=JE)
                for j in range(JE):
                    for c in range(KC):
                        last = nc.tensor.matmul(bank[b][:, j * SEQ:(j + 1) * SEQ], wv[:, c, j, :], hT[:, c, :],
                                                start=(c == 0), stop=(c == KC - 1))
                last.then_inc(m["sh_gu"], 1)
            last = None
            pe.wait_ge(m["chosen"], 1)
            nc.tensor.matmul(bank[7][:, 0:NE], upper[:, :], chosen[:, 0, :], start=True, stop=True)
            nc.tensor.matmul(bank[7][:, NE:2 * NE], ones[:, :], chosen[:, 0, :], start=True, stop=False)
            nc.tensor.matmul(bank[7][:, NE:2 * NE], upper[:, :], chosen[:, 1, :], start=False, stop=True)
            nc.tensor.matmul(bank[7][0:1, 2 * NE:3 * NE], ones[:, 0:1], chosen[:, 0, :], start=True, stop=False)
            nc.tensor.matmul(bank[7][0:1, 2 * NE:3 * NE], ones[:, 0:1], chosen[:, 1, :], start=False, stop=True)\
              .then_inc(m["rank_psum"], 1)
            ring_arrived(pe, f"sh_d{l}")
            pe.wait_ge(m["sh_hidden"], 1)
            wd = slot_of(f"sh_d{l}")[:, 0:JE * D].rearrange("p (j n) -> p j n", j=JE)
            for t in range(TT):
                for n in range(2):
                    for j in range(JE):
                        last = nc.tensor.matmul(bank[2 * t + n][:, :], shid[:, j, t * P:(t + 1) * P],
                                                wd[:, j, n * 512:(n + 1) * 512], start=(j == 0), stop=False,
                                                skip_group_check=True)
            last.then_inc(S["ring_used"], 2)
            pe.wait_ge(m["npass"], 1)
            npass = pe.value_load(npass_i[0:1, 0:1], min_val=1, max_val=MAX_PASS)

            def scatter(par, done):
                for t in range(TT):
                    for n in range(2):
                        last = nc.tensor.matmul(bank[2 * t + n][:, :], gatedT[:, par, t, :],
                                                ysb[:, n * 512:(n + 1) * 512], start=False, stop=done,
                                                skip_group_check=True)
                return last

            with pe.Fori(0, npass) as ps:
                with pe.Fori(0, NE // NSLOT) as it:
                    for u in range(2):
                        n = ps * PAIRS + it * 2 + u
                        g = ps * (NE // NSLOT) + it
                        pe.wait_ge(m["onehot"], n + 1)
                        pe.wait_ge(m["y_lo"], n + 1)
                        for c in range(KC):
                            if c == KC // 2:
                                pe.wait_ge(m["y_hi"], n + 1)
                            for t in range(TT):
                                last = nc.tensor.matmul(
                                    bank[4 + c // 4][:, (c % 4) * P:(c % 4 + 1) * P],
                                    h[:, t, :].rearrange("p (q c) -> p c q", c=KC)[:, c, :],
                                    onehot[:, u, t, :, :].rearrange("p a s -> p (a s)"),
                                    start=(t == 0), stop=(t == TT - 1))
                            if c == KC // 2 - 1:
                                last.then_inc(m["gather_lo"], 1)
                        last.then_inc(m["gather_hi"], 1)
                        pe.wait_ge(m["gated"], n + 1)
                        for t in range(TT):
                            last = nc.tensor.transpose(bank[7][:, t * P:(t + 1) * P],
                                                       gated[:, u, t, :, :].rearrange("p a s -> p (a s)"), ident[:, :])
                        last.then_inc(m["pt_full"], 1)
                        scatter(1 - u, False)
                        pe.wait_ge(m["xg_lo"], n + 1)
                        pe.wait_ge(m["xg_hi"], n + 1)
                        for a in range(2):
                            s = 2 * u + a
                            pe.wait_ge(m["gu_in"][s], 32 * g + 32)
                            if a == 1:
                                pe.wait_ge(m["pt_ready"], n + 2)
                            for w, wv in ((0, ew_g(s)), (1, ew_u(s))):
                                for j in range(JE):
                                    for c in range(KC):
                                        last = nc.tensor.matmul(
                                            bank[6 + a][:, w * P + j * CAP:w * P + (j + 1) * CAP],
                                            wv[:, c, j, :], xg[:, c, a * CAP:(a + 1) * CAP],
                                            start=(c == 0), stop=(c == KC - 1))
                            last.then_inc(m["gu_full"], 1)
                        for half, b in ((0, 4), (1, 5)):
                            for a in range(2):
                                s = 2 * u + a
                                if half == 0:
                                    pe.wait_ge(m["hidden"], 2 * n + a + 1)
                                    pe.wait_ge(m["d_in"][s], 16 * g + 16)
                                for j in range(JE):
                                    last = nc.tensor.matmul(bank[b][a * CAP:(a + 1) * CAP, :], hm[:, a, j, :],
                                                            ew_d(s)[:, j, half * 512:(half + 1) * 512],
                                                            start=(j == 0), stop=(j == JE - 1))
                            last.then_inc(m["y_lo_full"] if half == 0 else m["y_hi_full"], 1)
            pe.wait_ge(m["y_lo"], npass * PAIRS + 1)
            pe.wait_ge(m["y_hi"], npass * PAIRS + 1)
            scatter(1, True).then_inc(m["acc_full"], 1)

        sh_silu = resid[:, 0, :].rearrange("p (w j t) -> p w j t", w=2, j=JE)[:, 0]
        shid = resid[:, 0, :].rearrange("p (w j t) -> p w j t", w=2, j=JE)[:, 1]

        @block.tensor
        def _(pe):
            pe.wait_ge(S["consts"], N_CONSTS)
            for st in stages:
                if st == "mix0":
                    pe_mix0(pe)
                if st == "mix1":
                    pe_mix1(pe)
                if st.startswith("moe"):
                    pe_moe(pe, int(st[-1]))

        def act_copies(act, B, name, dst):
            act.wait_ge(*B.full(name))
            nc.scalar.copy(dst, B.tile(name)[:, :].rearrange("p (a t) -> p a t", a=2)).then_inc(B.done["a"], 1)

        def act_mix0(act, chain):
            B = B0
            act_copies(act, B, "T0", hT[:, 0:2, :])
            act_copies(act, B, "T2", hT[:, 4:6, :])
            act.wait_ge(*B.read("gates"))
            chain.link(nc.scalar.activation(rows[:, 2, :], rows[:, 1, :], ACT.Abs))
            chain.link(nc.scalar.activation(rows[:, 2, :], rows[:, 2, :], ACT.Exp, scale=-1.0))
            nc.scalar.activation(rows[:, 2, :], rows[:, 2, :], ACT.Ln, bias=1.0).then_inc(M0["splus"], 1)
            act.wait_ge(M0["params"], 80)
            chain.link(nc.scalar.activation(lamb[:, 0, :], cols0[:, 28:32], ACT.Abs))
            nc.scalar.activation(lamb[:, 0, :], lamb[:, 0, :], ACT.Exp, scale=-1.0).then_inc(M0["lam_exp"], 1)
            for i in range(2):
                act_copies(act, B, f"xb{i}", V["xbp"][:, 2 * i:2 * i + 2, 3:SEQ + 3])
            act.wait_ge(M0["rows"], 1)
            nc.scalar.activation(rows[:, 5, :], rows[:, 5, :], ACT.Exp, scale=-1.0).then_inc(M0["em"], 1)
            for name, dst in (("k", V["kT"]), ("q", V["qT"])):
                for i in range(2):
                    act_copies(act, B, f"{name}{i}", dst[:, 2 * i:2 * i + 2, :])
            for name, dst, col in (("r", V["rg"], 20), ("i", V["ig"], 24)):
                for i in range(2):
                    act.wait_ge(*B.full(f"{name}{i}"))
                    for a in range(2):
                        last = nc.scalar.activation(dst[:, 2 * i + a, :], B.tile(f"{name}{i}")[:, a * SEQ:(a + 1) * SEQ],
                                                    ACT.Sigmoid, bias=cols0[:, col + 2 * i + a:col + 2 * i + a + 1])
                    last.then_inc(B.done["a"], 1)
            for t in range(TT):
                act.wait_ge(*B.full(f"v{t}"))
                nc.scalar.copy(V["v1"][:, t, :, 0:DH], B.tile(f"v{t}")[:, :].rearrange("p (h n) -> p h n", h=NH))\
                  .then_inc(B.done["a"], 1)
            for hd in range(NH):
                act.wait_ge(*B.read(f"bc{hd // 2}"))
                nc.scalar.activation(argw[:, hd, :], argw[:, hd, :], ACT.Exp).then_inc(M0["expd"], 1)
            act.wait_ge(M0["log_a"], 1)
            nc.scalar.activation(abuf, V["rg"], ACT.Exp)
            nc.scalar.activation(tbuf, V["rg"], ACT.Tanh).then_inc(M0["a_t"], 1)
            for i in range(2):
                act.wait_ge(*B.full(f"gb{i}"))
                nc.scalar.activation(V["gg"][:, 2 * i:2 * i + 2, :], B.tile(f"gb{i}")[:, :].rearrange("p (a t) -> p a t", a=2),
                                     ACT.Gelu_apprx_tanh).then_inc(B.done["a"], 1)
            act.wait_ge(M0["gain"], 1)
            nc.scalar.activation(tbuf, tbuf, ACT.Sqrt).then_inc(M0["root"], 1)
            for t in range(TT):
                act.wait_ge(*B.full(f"o{t}"))
                nc.scalar.activation(V["og"][:, t, :], B.tile(f"o{t}")[:, :], ACT.Sigmoid).then_inc(B.done["a"], 1)
            act_head_norm(act, M0)
            act_copies(act, B, "yT0", V["mixT"][:, 0:2, :])

        def act_mix1(act, chain):
            B = B1
            act.wait_ge(M1["params"], 96)
            nc.scalar.activation(prm[:, 0, :], cols1[:, 32:48], ACT.Exp).then_inc(M1["dt"], 1)
            act.wait_ge(M1["ang"], 1)
            nc.scalar.activation(prm[:, 1, :], prm[:, 1, :], ACT.Exp)
            nc.scalar.activation(prm[:, 4, :], prm[:, 3, :], ACT.Sin, scale=0.5)
            nc.scalar.activation(prm[:, 5, :], prm[:, 3, :], ACT.Sin).then_inc(M1["sine"], 1)
            act_copies(act, B, "T0", hT[:, 0:2, :])
            act_copies(act, B, "T2", hT[:, 4:6, :])
            act.wait_ge(*B.full("low"))
            nc.scalar.copy(lowT[:, :], B.tile("low")[0:16, 0:SEQ]).then_inc(B.done["a"], 1)
            for i in range(2):
                act_copies(act, B, f"u{i}", W["uT"][:, 2 * i:2 * i + 2, :])
            act.wait_ge(*B.read("ga"))
            chain.link(nc.scalar.activation(W["e1"], W["la"], ACT.Abs))
            chain.link(nc.scalar.activation(W["e1"], W["e1"], ACT.Exp, scale=-1.0))
            nc.scalar.activation(W["e1"], W["e1"], ACT.Ln, bias=1.0).then_inc(M1["gla_ln"], 1)
            for w in range(2):
                act.wait_ge(*B.full(f"bT{w}"))
                nc.scalar.copy(W["bT"][:, w, :, :], B.tile(f"bT{w}")[:, :].rearrange("p (q n) -> p q n", q=4))\
                  .then_inc(B.done["a"], 1)
            act.wait_ge(M1["gla_last"], 1)
            nc.scalar.activation(W["e1"], W["bc"], ACT.Exp, scale=1.0 / 16)
            nc.scalar.activation(W["e2"], W["bc"], ACT.Exp, scale=-1.0 / 16)
            nc.scalar.activation(W["e3"], W["e3"], ACT.Exp, scale=1.0 / 16).then_inc(M1["decays"], 1)
            for t in range(TT):
                act.wait_ge(*B.full(f"v{t}"))
                nc.scalar.copy(W["v"][:, t, :], B.tile(f"v{t}")[:, :]).then_inc(B.done["a"], 1)
            act.wait_ge(M1["zeros"], 1)
            for hh in range(2):
                act.wait_ge(*B.full(f"att{hh}"))
                for b in range(2):
                    lo, hi = b * LC, (b + 1) * LC
                    src = B.tile(f"att{hh}")[lo:hi, :].rearrange("p (r t s) -> p r t s", r=2, t=TT)
                    for pr in range(2):
                        last = nc.scalar.copy(W["att"][lo:hi, 2 * pr + hh, :, lo:hi], src[:, pr, :, lo:hi])
                last.then_inc(B.done["a"], 1)
            act_copies(act, B, "keT", W["ke_tok"])
            for t in range(TT):
                act.wait_ge(*B.full(f"r{t}"))
                nc.scalar.activation(W["og"][:, t, :], B.tile(f"r{t}")[:, :], ACT.Silu).then_inc(B.done["a"], 1)
            act_head_norm(act, M1)
            for i in range(2):
                act_copies(act, B, f"yT{i}", W["mixT"][:, 4 + 2 * i:6 + 2 * i, :])
            act.wait_ge(*B.read("y1"))
            nc.scalar.activation(W["gT"], W["gT"], ACT.Gelu_apprx_tanh).then_inc(M1["gelu5"], 1)
            for i in range(2):
                act.wait_ge(*B.full(f"gl{i}"))
                for a in range(2):
                    q = 2 * i + a
                    last = nc.scalar.activation(W["mixT"][:, q, :], B.tile(f"gl{i}")[:, a * SEQ:(a + 1) * SEQ], ACT.Sigmoid,
                                                bias=cols1[:, 52 + q:53 + q])
                last.then_inc(B.done["a"], 1)

        def act_head_norm(act, M):
            act.wait_ge(S["consts"], N_CONSTS)
            act.wait_ge(M["hstat"], 1)
            nc.scalar.activation(hrs[:, :, :], hmv[:, :, :, 1], ACT.Sqrt, bias=epsc[:, 0:1]).then_inc(M["hstd"], 1)

        def act_moe(act, l, chain):
            m = MO[l]
            for i, b in enumerate((0, 2)):
                act.wait_ge(m["tA"], 1 + i)
                nc.scalar.copy(hT[:, 2 * b:2 * b + 2, :], bank[b][:, :].rearrange("p (c t) -> p c t", c=2))\
                  .then_inc(m["hT_a"], 1)
            act.wait_ge(m["scores_psum"], 1)
            nc.scalar.activation(scores[:, :, :], bank[6][:, 0:TT * NE].rearrange("p (t e) -> p t e", t=TT),
                                 ACT.Sigmoid).then_inc(m["scores"], 1)
            act.wait_ge(m["sh_gu"], 1)
            nc.scalar.activation(sh_silu, bank[4][:, :].rearrange("p (j t) -> p j t", j=JE), ACT.Silu)\
              .then_inc(m["sh_silu"], 1)
            act.wait_ge(m["npass"], 1)
            npass = act.value_load(npass_i[0:1, 0:1], min_val=1, max_val=MAX_PASS)
            with act.Fori(0, npass) as ps:
                with act.Fori(0, NE // NSLOT) as it:
                    for u in range(2):
                        n = ps * PAIRS + it * 2 + u
                        act.wait_ge(m["gather_lo"], n + 1)
                        nc.scalar.copy(xg[:, 0:4, :], bank[4][:, :].rearrange("p (c s) -> p c s", c=4))\
                          .then_inc(m["xg_lo"], 1)
                        for a in range(2):
                            act.wait_ge(m["gu_full"], 2 * n + a + 1)
                            nc.scalar.activation(sg[:, a, :, :],
                                                 bank[6 + a][:, 0:P].rearrange("p (j s) -> p j s", j=JE),
                                                 ACT.Silu).then_inc(m["silu"], 1)
                        act.wait_ge(m["y_hi_full"], n + 1)
                        nc.scalar.copy(ysb[:, 512:1024], bank[5][:, :]).then_inc(m["y_hi"], 1)

        def act_ln(act, k):
            act.wait_ge(S["consts"], N_CONSTS)
            act.wait_ge(LN[k]["stats"], 1)
            nc.scalar.activation(rstd[:, :], mv[:, :, 1], ACT.Sqrt, bias=epsc[:, 0:1]).then_inc(LN[k]["std"], 1)

        @block.scalar
        def _(act):
            chain = Chain(act, S["act_chain"])
            for st in stages:
                if st == "mix0":
                    act_mix0(act, chain)
                if st == "mix1":
                    act_mix1(act, chain)
                if st.startswith("moe"):
                    act_moe(act, int(st[-1]), chain)
                act_ln(act, stage_no[st])

        def dve_ln(dve, chain, k):
            ln = LN[k]
            for t in range(TT):
                for n in range(2):
                    last = nc.vector.scalar_tensor_tensor(out=resid[:, t, n * 512:(n + 1) * 512],
                                                          in0=h[:, t, n * 512:(n + 1) * 512], scalar=ALPHA,
                                                          in1=bank[2 * t + n][:, :], op0=ALU.mult, op1=ALU.add)
            chain.link(last)
            for t in range(TT):
                for n in range(2):
                    last = nc.vector.bn_stats(stats[:, t, n, :], resid[:, t, n * 512:(n + 1) * 512])
            chain.link(last)
            for t in range(TT):
                last = nc.vector.bn_aggr(mv[:, t, :], stats[:, t, :, :])
            last.then_inc(ln["stats"], 1)
            dve.wait_ge(ln["std"], 1)
            chain.link(nc.vector.reciprocal(rstd[:, :], rstd[:, :]))
            for t in range(TT):
                last = nc.vector.tensor_scalar(resid[:, t, :], resid[:, t, :], mv[:, t, 0:1], rstd[:, t:t + 1],
                                               ALU.subtract, ALU.mult)
            chain.link(last)
            dve.wait_ge(ln["params"], 32)
            for t in range(TT):
                last = nc.vector.tensor_tensor(resid[:, t, :], resid[:, t, :], lnw[:, :], ALU.mult)
            chain.link(last)
            for t in range(TT):
                last = nc.vector.tensor_tensor(h[:, t, :], resid[:, t, :], lnb[:, :], ALU.add)
            last.then_inc(S["h_ready"], 1)

        def dve_copies(dve, B, name, dst):
            dve.wait_ge(*B.full(name))
            nc.vector.tensor_copy(dst, B.tile(name)[:, :].rearrange("p (a t) -> p a t", a=2)).then_inc(B.done["d"], 1)

        def dve_mix0(dve, chain):
            B = B0
            for i, row in enumerate((1, 3)):
                dve_copies(dve, B, f"T{row}", hT[:, 2 * row:2 * row + 2, :])
            nc.vector.memset(V["xbp"][:, :, 0:3], 0.0)
            chain.link(nc.vector.memset(V["v1"][:, :, :, DH:DH + 1], 1.0))
            dve.wait_ge(M0["params"], 80)
            dve.wait_ge(*B.full("gates"))
            nc.vector.tensor_scalar(rows[:, 0, :], B.tile("gates")[0:NH, 0:SEQ], cols0[0:NH, 32:33], None, ALU.add)
            nc.vector.tensor_scalar(rows[:, 1, :], B.tile("gates")[0:NH, SEQ:2 * SEQ], cols0[0:NH, 33:34], None, ALU.add)\
              .then_inc(B.done["d"], 1)
            dve.wait_ge(*B.read("gates"))
            dve.wait_ge(M0["splus"], 1)
            chain.link(nc.vector.scalar_tensor_tensor(out=rows[:, 1, :], in0=rows[:, 1, :], scalar=0.0,
                                                      in1=rows[:, 2, :], op0=ALU.min, op1=ALU.subtract))
            one = ones[0:NH, 0:1].broadcast_to([NH, SEQ])
            chain.link(nc.vector.tensor_tensor_scan(rows[:, 3, :], one, rows[:, 1, :], 0.0, ALU.mult, ALU.add))
            chain.link(nc.vector.tensor_tensor(rows[:, 0, :], rows[:, 0, :], rows[:, 3, :], ALU.subtract))
            chain.link(nc.vector.tensor_tensor_scan(rows[:, 4, :], one, rows[:, 0, :], 0.0, ALU.mult, ALU.max))
            chain.link(nc.vector.tensor_tensor(rows[:, 5, :], rows[:, 3, :], rows[:, 4, :], ALU.add))
            nc.vector.tensor_scalar(rows[:, 4, :], rows[:, 4, :], -1.0, None, ALU.mult).then_inc(M0["rows"], 1)
            dve.wait_ge(M0["lam_exp"], 1)
            L = lamb
            chain.link(nc.vector.tensor_scalar(L[:, 1, :], L[:, 0, :], 2.0, None, ALU.add))
            chain.link(nc.vector.reciprocal(L[:, 1, :], L[:, 1, :]))
            chain.link(nc.vector.tensor_tensor(L[:, 1, :], L[:, 0, :], L[:, 1, :], ALU.mult))
            chain.link(nc.vector.tensor_tensor(L[:, 2, :], L[:, 1, :], L[:, 1, :], ALU.mult))
            terms = [1.0 / (2 * q + 1) for q in range(9)]
            chain.link(nc.vector.tensor_scalar(L[:, 3, :], L[:, 2, :], terms[8], terms[7], ALU.mult, ALU.add))
            for q in range(6, -1, -1):
                chain.link(nc.vector.tensor_tensor(L[:, 3, :], L[:, 3, :], L[:, 2, :], ALU.mult))
                chain.link(nc.vector.tensor_scalar(L[:, 3, :], L[:, 3, :], terms[q], None, ALU.add))
            chain.link(nc.vector.scalar_tensor_tensor(out=L[:, 3, :], in0=L[:, 3, :], scalar=2.0, in1=L[:, 1, :],
                                                      op0=ALU.mult, op1=ALU.mult))
            chain.link(nc.vector.scalar_tensor_tensor(out=L[:, 4, :], in0=cols0[:, 28:32], scalar=0.0, in1=L[:, 3, :],
                                                      op0=ALU.min, op1=ALU.subtract))
            chain.link(nc.vector.tensor_scalar(L[:, 4, :], L[:, 4, :], 8.0, None, ALU.mult))
            dve.wait_ge(*B.read("xb1"))
            for hd in range(NH):
                last = nc.vector.tensor_scalar(V["xc"][:, hd, :], V["xbp"][:, hd, 0:SEQ], cols0[:, hd:hd + 1],
                                               cols0[:, 16 + hd:17 + hd], ALU.mult, ALU.add)
            for tap in range(1, 4):
                chain.link(last)
                for hd in range(NH):
                    last = nc.vector.scalar_tensor_tensor(out=V["xc"][:, hd, :], in0=V["xbp"][:, hd, tap:tap + SEQ],
                                                          scalar=cols0[:, 4 * tap + hd:4 * tap + hd + 1],
                                                          in1=V["xc"][:, hd, :], op0=ALU.mult, op1=ALU.add)
            last.then_inc(M0["xc"], 1)
            dve.wait_ge(*B.full("cols"))
            nc.vector.tensor_copy(gcol[:, :, :, :], B.tile("cols")[:, 0:16].rearrange("p (i t h) -> p i t h", i=2, t=TT))\
              .then_inc(B.done["d"], 1)
            dve.wait_ge(*B.read("cols"))
            for hd in range(NH):
                name, off = f"bc{hd // 2}", (hd % 2) * SEQ
                if hd % 2 == 0:
                    dve.wait_ge(*B.full(name))
                nc.vector.scalar_tensor_tensor(out=argw[:, hd, 0:SEQ], in0=B.tile(name)[:, off:off + SEQ],
                                               scalar=gcol[:, 0, 0, hd:hd + 1], in1=maskc[:, :],
                                               op0=ALU.add, op1=ALU.min)
                last = nc.vector.scalar_tensor_tensor(out=argw[:, hd, SEQ:SEQ + P],
                                                      in0=B.tile(name)[:, off + P:off + SEQ],
                                                      scalar=gcol[:, 0, 1, hd:hd + 1], in1=maskc[:, 0:P],
                                                      op0=ALU.add, op1=ALU.min)
                if hd % 2 == 1:
                    last.then_inc(B.done["d"], 1)
            dve.wait_ge(*B.read("r1"))
            nc.vector.tensor_tensor(V["rg"], V["rg"], L[:, 4, :].unsqueeze(2).broadcast_to([P, NH, SEQ]), ALU.mult)\
              .then_inc(M0["log_a"], 1)
            for hd in range(NH):
                dve.wait_ge(*B.full(f"S{hd}"))
                dve.wait_ge(M0["expd"], hd + 1)
                nc.vector.scalar_tensor_tensor(out=argw[:, hd, :], in0=B.tile(f"S{hd}")[:, 0:SEQ + P],
                                               scalar=DH ** -0.5, in1=argw[:, hd, :], op0=ALU.mult, op1=ALU.mult)\
                  .then_inc(B.done["d"], 1)
            dve.wait_ge(M0["a_t"], 1)
            chain.link(nc.vector.tensor_scalar(V["rg"], tbuf, -1.0, 1.0, ALU.mult, ALU.add))
            chain.link(nc.vector.reciprocal(V["rg"], V["rg"]))
            nc.vector.scalar_tensor_tensor(out=tbuf, in0=tbuf, scalar=-2.0, in1=V["rg"], op0=ALU.mult, op1=ALU.mult)\
              .then_inc(M0["gain"], 1)
            dve.wait_ge(*B.read("i1"))
            chain.link(nc.vector.tensor_tensor(V["ig"], V["ig"], V["xc"], ALU.mult))
            dve.wait_ge(M0["root"], 1)
            chain.link(nc.vector.tensor_tensor(V["ig"], V["ig"], tbuf, ALU.mult))
            for hd in range(NH):
                last = nc.vector.tensor_tensor_scan(V["xc"][:, hd, :], abuf[:, hd, :], V["ig"][:, hd, :], 0.0,
                                                    ALU.mult, ALU.add)
            chain.link(last)
            dve.wait_ge(*B.read("gb1"))
            nc.vector.tensor_tensor(V["mixT"][:, 4:8, :], V["xc"], V["gg"], ALU.mult).then_inc(M0["y_lru"], 1)
            for hd in range(NH):
                dve.wait_ge(*B.full(f"N{hd}"))
                acc = B.tile(f"N{hd}")
                den = acc[:, :].rearrange("p (t n) -> p t n", t=TT)[:, :, DH]
                chain.link(nc.vector.tensor_copy(rden[:, hd, :], den))
                chain.link(nc.vector.scalar_tensor_tensor(out=rden[:, hd, :], in0=rden[:, hd, :], scalar=-1.0,
                                                          in1=rden[:, hd, :], op0=ALU.mult, op1=ALU.max))
                chain.link(nc.vector.tensor_tensor(rden[:, hd, :], rden[:, hd, :], gcol[:, 1, :, hd], ALU.max))
                chain.link(nc.vector.reciprocal(rden[:, hd, :], rden[:, hd, :]))
                for t in range(TT):
                    last = nc.vector.tensor_scalar(hbuf[:, t, hd * DH:(hd + 1) * DH], acc[:, t * SEQ:t * SEQ + DH],
                                                   rden[:, hd, t:t + 1], None, ALU.mult)
                last.then_inc(B.done["d"], 1)
            dve.wait_ge(*B.read("N3"))
            dve_head_norm(dve, chain, M0, True)
            dve.wait_ge(*B.read("o1"))
            for t in range(TT):
                last = nc.vector.tensor_tensor(hbuf[:, t, :], hbuf[:, t, :], V["og"][:, t, :], ALU.mult)
            last.then_inc(M0["yhead"], 1)
            dve_copies(dve, B, "yT1", V["mixT"][:, 2:4, :])
            dve.wait_ge(M0["out_full"], 1)

        def dve_s5_params(dve, chain):
            p = prm
            lr, li = cols1[:, 0:16], cols1[:, 16:32]
            dve.wait_ge(M1["params"], 96)
            dve.wait_ge(M1["dt"], 1)
            nc.vector.tensor_tensor(p[:, 1, :], lr, p[:, 0, :], ALU.mult)
            chain.link(nc.vector.tensor_tensor(p[:, 2, :], li, p[:, 0, :], ALU.mult))
            magic, turn = 1.5 * 2.0 ** 23, 2.0 * np.pi
            c1 = 6.28125
            c2 = float(np.float32(round((turn - c1) * 2 ** 20) / 2 ** 20))
            c3 = turn - c1 - c2
            chain.link(nc.vector.tensor_scalar(p[:, 3, :], p[:, 2, :], 1.0 / turn, magic, ALU.mult, ALU.add))
            chain.link(nc.vector.tensor_scalar(p[:, 3, :], p[:, 3, :], magic, None, ALU.subtract))
            for part in (c1, c2, c3):
                chain.link(nc.vector.scalar_tensor_tensor(out=p[:, 2, :], in0=p[:, 3, :], scalar=-part, in1=p[:, 2, :],
                                                          op0=ALU.mult, op1=ALU.add))
            nc.vector.tensor_scalar(p[:, 3, :], p[:, 2, :], 3.1415925, -3.1415925, ALU.min, ALU.max)\
              .then_inc(M1["ang"], 1)
            dve.wait_ge(M1["sine"], 1)
            chain.link(nc.vector.tensor_tensor(p[:, 4, :], p[:, 4, :], p[:, 4, :], ALU.mult))
            chain.link(nc.vector.tensor_scalar(p[:, 4, :], p[:, 4, :], -2.0, 1.0, ALU.mult, ALU.add))
            nc.vector.tensor_copy(W["cos"][:, :, 0], p[:, 4, :]).then_inc(M1["step_re"], 1)
            nc.vector.tensor_copy(W["sin"][:, :, 0], p[:, 5, :]).then_inc(M1["step_im"], 1)
            nc.vector.tensor_tensor(p[:, 6, :], p[:, 1, :], p[:, 4, :], ALU.mult)
            nc.vector.tensor_tensor(p[:, 7, :], p[:, 1, :], p[:, 5, :], ALU.mult)
            nc.vector.tensor_tensor(p[:, 10, :], lr, lr, ALU.mult)
            chain.link(nc.vector.tensor_tensor(p[:, 11, :], li, li, ALU.mult))
            nc.vector.tensor_tensor(p[:, 10, :], p[:, 10, :], p[:, 11, :], ALU.add)
            chain.link(nc.vector.tensor_scalar(p[:, 6, :], p[:, 6, :], 1.0, None, ALU.subtract))
            nc.vector.reciprocal(p[:, 10, :], p[:, 10, :])
            nc.vector.tensor_tensor(p[:, 8, :], p[:, 6, :], lr, ALU.mult)
            nc.vector.tensor_tensor(p[:, 11, :], p[:, 7, :], li, ALU.mult)
            nc.vector.tensor_tensor(p[:, 9, :], p[:, 7, :], lr, ALU.mult)
            chain.link(nc.vector.tensor_tensor(p[:, 12, :], p[:, 6, :], li, ALU.mult))
            nc.vector.tensor_tensor(p[:, 8, :], p[:, 8, :], p[:, 11, :], ALU.add)
            chain.link(nc.vector.tensor_tensor(p[:, 9, :], p[:, 9, :], p[:, 12, :], ALU.subtract))
            nc.vector.tensor_tensor(p[:, 8, :], p[:, 8, :], p[:, 10, :], ALU.mult)
            nc.vector.tensor_tensor(p[:, 9, :], p[:, 9, :], p[:, 10, :], ALU.mult).then_inc(M1["coef"], 1)
            nc.vector.tensor_scalar(W["craw"][:, 1], W["craw"][:, 1], -1.0, None, ALU.mult).then_inc(M1["cneg"], 1)

        def dve_mix1(dve, chain):
            B = B1
            dve_s5_params(dve, chain)
            for row in (1, 3):
                dve_copies(dve, B, f"T{row}", hT[:, 2 * row:2 * row + 2, :])
            for k in range(N_STEPS):
                n = 1 << k
                dve.wait_ge(M1["step_re"], k + 1)
                dve.wait_ge(M1["step_im"], k + 1)
                new = W["sin"][:, :, n:2 * n]
                tmp = W["x"].rearrange("p a b t -> p (a b t)")[:, 0:NT * n].rearrange("p (i t) -> p i t", i=NT)
                cr = W["cos"][:, :, n - 1:n].broadcast_to([P, NT, n])
                ci = W["sin"][:, :, n - 1:n].broadcast_to([P, NT, n])
                nc.vector.tensor_tensor(new, W["sin"][:, :, 0:n], cr, ALU.mult)
                chain.link(nc.vector.tensor_tensor(tmp, W["cos"][:, :, 0:n], ci, ALU.mult))
                nc.vector.tensor_tensor(new, new, tmp, ALU.add).then_inc(M1["step_im"], 1)
            dve.wait_ge(*B.full("ga"))
            for a in range(2):
                last = nc.vector.tensor_scalar(W["la"][:, a, :], B.tile("ga")[:, a * SEQ:(a + 1) * SEQ],
                                               cols1[:, 56 + a:57 + a], None, ALU.add)
            last.then_inc(B.done["d"], 1)
            dve.wait_ge(*B.read("ga"))
            dve.wait_ge(M1["gla_ln"], 1)
            chain.link(nc.vector.scalar_tensor_tensor(out=W["la"], in0=W["la"], scalar=0.0, in1=W["e1"],
                                                      op0=ALU.min, op1=ALU.subtract))
            dve.wait_ge(M1["zeros"], 1)
            for a in range(2):
                last = nc.vector.tensor_tensor_scan(W["bc"][:, a, :], restart[:, :], W["la"][:, a, :], 0.0, ALU.mult, ALU.add)
            chain.link(last)
            by_chunk = W["bc"].rearrange("p a (c s) -> p (a c) s", s=LC)
            nc.vector.tensor_tensor(W["e3"].rearrange("p a (c s) -> p (a c) s", s=LC),
                                    by_chunk[:, :, LC - 1:LC].broadcast_to([P, 2 * SEQ // LC, LC]), by_chunk,
                                    ALU.subtract).then_inc(M1["gla_last"], 1)
            dve.wait_ge(M1["step_re"], N_STEPS + 1)
            dve.wait_ge(M1["step_im"], N_STEPS + 1)

            def scan_tile(i):
                q = i % 4
                dve.wait_ge(*B.full(f"bu{i}"))
                if i == 0:
                    dve.wait_ge(*B.read("bT1"))
                if i >= 4:
                    dve.wait_ge(M1["x"], i - 3)
                bu = B.tile(f"bu{i}")[:, :].rearrange("p (w t) -> p w t", w=2)
                c = W["cos"][:, i, :].unsqueeze(1).broadcast_to([P, 2, SEQ])
                sn = W["sin"][:, i, :].unsqueeze(1).broadcast_to([P, 2, SEQ])
                nc.vector.tensor_tensor(W["m1"], bu, c, ALU.mult)
                nc.vector.tensor_tensor(W["m2"], bu, sn, ALU.mult).then_inc(B.done["d"], 1)
                dve.wait_ge(*B.read(f"bu{i}"))
                nc.vector.tensor_tensor(zin[:, 0, :], W["m1"][:, 0, :], W["m2"][:, 1, :], ALU.add)
                chain.link(nc.vector.tensor_tensor(zin[:, 1, :], W["m1"][:, 1, :], W["m2"][:, 0, :], ALU.subtract))
                mag = prm[:, 1, i:i + 1].broadcast_to([P, SEQ])
                for w in range(2):
                    last = nc.vector.tensor_tensor_scan(W["z"][:, q, w, :], mag, zin[:, w, :], 0.0, ALU.mult, ALU.add)
                last.then_inc(M1["z"], 1)

            for i in range(4):
                scan_tile(i)
            dve.wait_ge(M1["decays"], 1)
            dve.wait_ge(*B.full("qk1"))
            k_ps = B.tile("qk1")[:, :].rearrange("p (a t) -> p a t", a=2)
            nc.vector.scalar_tensor_tensor(out=W["qd"], in0=B.tile("qk0")[:, :].rearrange("p (a t) -> p a t", a=2),
                                           scalar=DK ** -0.5, in1=W["e1"], op0=ALU.mult, op1=ALU.mult)\
              .then_inc(B.done["d"], 1)
            nc.vector.tensor_tensor(W["ki"], k_ps, W["e2"], ALU.mult).then_inc(M1["ki"], 1)
            nc.vector.tensor_tensor(W["ke"], k_ps, W["e3"], ALU.mult).then_inc(B.done["d"], 1)
            for i in range(4, 12):
                scan_tile(i)
            dve.wait_ge(M1["zeros"], 1)
            for c in range(3):
                dve.wait_ge(*B.full(f"U{c}"))
                for hd in range(NH):
                    lo = (hd % 2) * DK
                    new = W["state"][lo:lo + DK, c, hd, :]
                    add = B.tile(f"U{c}")[lo:lo + DK, hd * P:(hd + 1) * P]
                    if c == 0:
                        last = nc.vector.tensor_copy(new, add)
                    else:
                        end = c * LC + LC - 1
                        last = nc.vector.scalar_tensor_tensor(out=new, in0=W["state"][lo:lo + DK, c - 1, hd, :],
                                                              scalar=W["e1"][lo:lo + DK, hd // 2, end:end + 1], in1=add,
                                                              op0=ALU.mult, op1=ALU.add)
                last.then_inc(B.done["d"], 1)
                dve.wait_ge(*B.read(f"U{c}"))
            for t in range(TT):
                dve.wait_ge(*B.full(f"o{t}"))
                nc.vector.tensor_copy(hbuf[:, t, :], B.tile(f"o{t}")[:, :]).then_inc(B.done["d"], 1)
            dve.wait_ge(*B.read("o1"))
            dve_head_norm(dve, chain, M1, False)
            dve.wait_ge(*B.read("r1"))
            for t in range(TT):
                last = nc.vector.tensor_tensor(hbuf[:, t, :], hbuf[:, t, :], W["og"][:, t, :], ALU.mult)
            last.then_inc(M1["yhead"], 1)
            for i in range(12, 16):
                scan_tile(i)
            dve.wait_ge(*B.full("y1"))
            for q in range(4):
                last = nc.vector.scalar_tensor_tensor(out=W["gT"][:, q, :], in0=W["uT"][:, q, :], scalar=cols1[:, 48 + q:49 + q],
                                                      in1=B.tile(f"y{q // 2}")[:, (q % 2) * SEQ:(q % 2 + 1) * SEQ],
                                                      op0=ALU.mult, op1=ALU.add)
                if q % 2:
                    last.then_inc(B.done["d"], 1)
            dve.wait_ge(*B.read("gl1"))
            nc.vector.tensor_tensor(W["mixT"][:, 0:4, :], W["mixT"][:, 0:4, :], W["gT"], ALU.mult).then_inc(M1["y_s5"], 1)
            dve.wait_ge(M1["out_full"], 1)

        def dve_head_norm(dve, chain, M, center):
            for t in range(TT):
                for hd in range(NH):
                    last = nc.vector.bn_stats(hstat[:, t, hd, :], hbuf[:, t, hd * DH:(hd + 1) * DH])
            chain.link(last)
            for t in range(TT):
                for hd in range(NH):
                    last = nc.vector.bn_aggr(hmv[:, t, hd, :], hstat[:, t, hd, :])
            if not center:
                chain.link(last)
                chain.link(nc.vector.tensor_tensor(hrs[:, :, :], hmv[:, :, :, 0], hmv[:, :, :, 0], ALU.mult))
                last = nc.vector.tensor_tensor(hmv[:, :, :, 1], hmv[:, :, :, 1], hrs[:, :, :], ALU.add)
            last.then_inc(M["hstat"], 1)
            dve.wait_ge(M["hstd"], 1)
            chain.link(nc.vector.reciprocal(hrs[:, :, :], hrs[:, :, :]))
            for t in range(TT):
                for hd in range(NH):
                    part = hbuf[:, t, hd * DH:(hd + 1) * DH]
                    if center:
                        last = nc.vector.tensor_scalar(part, part, hmv[:, t, hd, 0:1], hrs[:, t, hd:hd + 1],
                                                       ALU.subtract, ALU.mult)
                    else:
                        last = nc.vector.tensor_scalar(part, part, hrs[:, t, hd:hd + 1], None, ALU.mult)
            chain.link(last)
            for t in range(TT):
                last = nc.vector.tensor_tensor(hbuf[:, t, :], hbuf[:, t, :], normw, ALU.mult)
            chain.link(last)

        def dve_route(dve, m, chain):
            dve.wait_ge(m["scores"], 1)
            dve.wait_ge(m["router_in"], 32)
            chain.link(nc.vector.tensor_tensor(biased[:, :, :], scores[:, :, :],
                                               rbias[:, :].unsqueeze(1).broadcast_to([P, TT, NE]), ALU.add))
            for t in range(TT):
                for g in range(NG):
                    last = nc.vector.max(top8[:, t, g, :], biased[:, t, g * 8:(g + 1) * 8])
            chain.link(last)
            chain.link(nc.vector.tensor_tensor(grp[:, :, :], top8[:, :, :, 0], top8[:, :, :, 1], ALU.add))
            for t in range(TT):
                other = grp[:, t, :].unsqueeze(1).broadcast_to([P, NG, NG])
                own = grp[:, t, :].unsqueeze(2).broadcast_to([P, NG, NG])
                nc.vector.tensor_tensor(gcmp[:, t, :, :], other, own, ALU.is_gt)
                last = nc.vector.tensor_tensor(gcmp2[:, t, :, :], other, own, ALU.is_equal)
            chain.link(last)
            for t in range(TT):
                last = nc.vector.tensor_tensor(gcmp2[:, t, :, :], gcmp2[:, t, :, :], gmask[:, :, :], ALU.mult)
            chain.link(last)
            for t in range(TT):
                last = nc.vector.tensor_tensor(gcmp[:, t, :, :], gcmp[:, t, :, :], gcmp2[:, t, :, :], ALU.add)
            chain.link(last)
            chain.link(nc.vector.tensor_reduce(grank[:, :, :], gcmp[:, :, :, :], AX.X, ALU.add))
            chain.link(nc.vector.tensor_scalar(grank[:, :, :], grank[:, :, :], TOPK_GROUPS - 0.5, -BIG,
                                               ALU.is_gt, ALU.mult))
            for t in range(TT):
                last = nc.vector.tensor_tensor(masked[:, t, :].rearrange("p (g e) -> p g e", g=NG),
                                               biased[:, t, :].rearrange("p (g e) -> p g e", g=NG),
                                               grank[:, t, :].unsqueeze(2).broadcast_to([P, NG, NE // NG]), ALU.add)
            chain.link(last)
            for t in range(TT):
                last = nc.vector.max(best[:, t, :], masked[:, t, :])
            chain.link(last)
            for t in range(TT):
                last = nc.vector.match_replace(replaced[:, t, :], best[:, t, :], masked[:, t, :], -3.0 * BIG)
            chain.link(last)
            nc.vector.tensor_tensor(chosen[:, :, :], replaced[:, :, :], masked[:, :, :], ALU.not_equal)\
              .then_inc(m["chosen"], 1)
            dve.wait_ge(m["chosen"], 1)
            chain.link(nc.vector.tensor_tensor(wts[:, :, :], chosen[:, :, :], scores[:, :, :], ALU.mult))
            chain.link(nc.vector.tensor_reduce(wsum[:, :], wts[:, :, :], AX.X, ALU.add))
            chain.link(nc.vector.reciprocal(wsum[:, :], wsum[:, :]))
            for t in range(TT):
                last = nc.vector.tensor_scalar(cw[:, t, :], wts[:, t, :], wsum[:, t:t + 1], ROUTED_SCALE,
                                               ALU.mult, ALU.mult)
            chain.link(last)
            dve.wait_ge(m["rank_psum"], 1)
            chain.link(nc.vector.tensor_reduce(cnt[0:1, 0:1], bank[7][0:1, 2 * NE:3 * NE], AX.X, ALU.max))
            for i in range(1, MAX_PASS):
                last = nc.vector.tensor_scalar(cnt[0:1, i:i + 1], cnt[0:1, 0:1], CAP * i + 0.5, None, ALU.is_gt)
            chain.link(last)
            chain.link(nc.vector.tensor_reduce(cnt[0:1, MAX_PASS:MAX_PASS + 1], cnt[0:1, 1:MAX_PASS], AX.X, ALU.add))
            nc.vector.tensor_scalar(npass_i[0:1, 0:1], cnt[0:1, MAX_PASS:MAX_PASS + 1], 1.0, None, ALU.add)\
              .then_inc(m["npass"], 1)
            for t in range(TT):
                last = nc.vector.scalar_tensor_tensor(out=rank[:, t, :], in0=bank[7][:, t * NE:(t + 1) * NE],
                                                      scalar=1.0, in1=chosen[:, t, :], op0=ALU.add, op1=ALU.mult)
            chain.link(last)
            chain.link(nc.vector.tensor_scalar(rank[:, :, :], rank[:, :, :], 1.0, None, ALU.subtract))

        def dve_moe(dve, l, chain):
            m = MO[l]
            for i, b in enumerate((1, 3)):
                dve.wait_ge(m["tD"], 1 + i)
                nc.vector.tensor_copy(hT[:, 2 * b:2 * b + 2, :], bank[b][:, :].rearrange("p (c t) -> p c t", c=2))\
                  .then_inc(m["hT_d"], 1)
            dve_route(dve, m, chain)
            dve.wait_ge(m["sh_silu"], 1)
            dve.wait_ge(m["sh_gu"], 2)
            nc.vector.tensor_tensor(shid, sh_silu, bank[5][:, :].rearrange("p (j t) -> p j t", j=JE), ALU.mult)\
              .then_inc(m["sh_hidden"], 1)
            nc.vector.memset(gatedT[:, 1, :, :], 0.0).then_inc(m["pt_ready"], 1)
            nc.vector.memset(ysb[:, 512:1024], 0.0).then_inc(m["y_hi"], 1)
            nc.vector.memset(ysb[:, 0:512], 0.0).then_inc(m["y_lo"], 1)
            dve.wait_ge(m["npass"], 1)
            npass = dve.value_load(npass_i[0:1, 0:1], min_val=1, max_val=MAX_PASS)
            with dve.Fori(0, npass) as ps:
                with dve.Fori(0, NE // NSLOT) as it:
                    for u in range(2):
                        n = ps * PAIRS + it * 2 + u
                        e = it * NSLOT + 2 * u
                        slots = iota[:, :].unsqueeze(1).unsqueeze(1).broadcast_to([P, TT, 2, CAP])
                        nc.vector.tensor_tensor(
                            onehot[:, u, :, :, :], slots,
                            rank[:, :, bass.ds(e, 2)].unsqueeze(3).broadcast_to([P, TT, 2, CAP]),
                            ALU.is_equal).then_inc(m["onehot"], 1)
                        dve.wait_ge(m["onehot"], n + 1)
                        nc.vector.tensor_tensor(
                            gated[:, u, :, :, :], onehot[:, u, :, :, :],
                            cw[:, :, bass.ds(e, 2)].unsqueeze(3).broadcast_to([P, TT, 2, CAP]),
                            ALU.mult).then_inc(m["gated"], 1)
                        dve.wait_ge(m["gather_hi"], n + 1)
                        nc.vector.tensor_copy(xg[:, 4:8, :], bank[5][:, :].rearrange("p (c s) -> p c s", c=4))\
                          .then_inc(m["xg_hi"], 1)
                        dve.wait_ge(m["pt_full"], n + 1)
                        nc.vector.tensor_copy(gatedT[:, u, :, :], bank[7][:, 0:TT * P].rearrange("p (t s) -> p t s", t=TT))\
                          .then_inc(m["pt_ready"], 1)
                        for a in range(2):
                            dve.wait_ge(m["silu"], 2 * n + a + 1)
                            nc.vector.tensor_tensor(
                                hm[:, a, :, :], sg[:, a, :, :],
                                bank[6 + a][:, P:2 * P].rearrange("p (j s) -> p j s", j=JE), ALU.mult)\
                              .then_inc(m["hidden"], 1)
                        dve.wait_ge(m["y_lo_full"], n + 1)
                        nc.vector.tensor_copy(ysb[:, 0:512], bank[4][:, :]).then_inc(m["y_lo"], 1)
                nc.vector.tensor_scalar(rank[:, :, :], rank[:, :, :], float(CAP), None, ALU.subtract)\
                  .then_inc(m["rank_next"], 1)
                dve.wait_ge(m["rank_next"], ps + 1)
            dve.wait_ge(m["acc_full"], 1)

        @block.vector
        def _(dve):
            chain = Chain(dve, S["dve_chain"])
            dve.wait_ge(S["consts"], N_CONSTS)
            for st in stages:
                if st == "mix0":
                    dve_mix0(dve, chain)
                if st == "mix1":
                    dve_mix1(dve, chain)
                if st.startswith("moe"):
                    dve_moe(dve, int(st[-1]), chain)
                dve_ln(dve, chain, stage_no[st])


_INS = ["x", "ln1_w", "ln1_b", "ln2_w", "ln2_b", "w_out", "w_in_even", "w_in_odd", "mlstm_norm_w", "gla_norm_w",
        "lru_wa", "lru_wx", "s5_glu_w", "gla_gate_w", "router_w", "router_bias",
        "exp_w_gate", "exp_w_up", "exp_w_down", "sh_w_gate", "sh_w_up", "sh_w_down"]
STAGES = ("mix0", "moe0", "mix1", "moe1")


def packed(inputs):
    def chans(a):
        a = np.asarray(a)
        return a.reshape(-1, P).T

    even = np.zeros((P, 34), np.float32)
    even[:, 0:16] = np.concatenate([chans(np.asarray(inputs["lru_conv_w"])[0, k]) for k in range(4)], axis=1)
    even[:, 16:20] = chans(inputs["lru_conv_b"])
    even[:, 20:24] = chans(inputs["lru_ba"])
    even[:, 24:28] = chans(inputs["lru_bx"])
    even[:, 28:32] = chans(inputs["lru_lambda"])
    even[0:4, 32:34] = np.asarray(inputs["mlstm_gate_b"])[0].reshape(2, 4).T

    odd = np.zeros((P, 58), np.float32)
    odd[:, 0:16] = np.asarray(inputs["s5_lam_re"]).reshape(NT, P).T
    odd[:, 16:32] = np.asarray(inputs["s5_lam_im"]).reshape(NT, P).T
    odd[:, 32:48] = np.repeat(np.asarray(inputs["s5_log_dt"]).reshape(-1), 64).reshape(NT, P).T
    odd[:, 48:52] = chans(inputs["s5_d"])
    odd[:, 52:56] = chans(inputs["s5_glu_b"])
    odd[:, 56:58] = chans(inputs["gla_gate_b"])

    def by_state(re, im):
        m = np.zeros((P, 2, NT, 32), np.float32)
        for w, a in enumerate((re, im)):
            a = a.reshape(NT, 2, 64, 16)
            for g in range(2):
                m[g * 64:(g + 1) * 64, w, :, g * 16:(g + 1) * 16] = a[:, g].transpose(1, 0, 2)
        return m.reshape(P, -1)

    b = by_state(np.asarray(inputs["s5_b_re"])[0], np.asarray(inputs["s5_b_im"])[0])
    c = by_state(np.asarray(inputs["s5_c_re"])[0].transpose(0, 2, 1), np.asarray(inputs["s5_c_im"])[0].transpose(0, 2, 1))
    return {"cols_even": even, "cols_odd": odd, "b_odd": b, "c_odd": c}


def kernel(**inputs):
    import concourse.bacc as _bacc
    from concourse.bass_utils import run_bass_kernel_spmd as _run

    nc = _bacc.Bacc("TRN2", target_bir_lowering=False, num_devices=1)
    arrays, A = {}, {}
    given = {n: np.ascontiguousarray(inputs[n]) for n in _INS}
    given.update(packed(inputs))
    for name, a in given.items():
        arrays[f"in_{name}"] = a
        A[name] = nc.dram_tensor(f"in_{name}", a.shape, mybir.dt.from_np(a.dtype), kind="ExternalInput").ap()
    out = nc.dram_tensor("out_0", (1, SEQ, D), F32, kind="ExternalOutput").ap()
    build(nc, A, out, STAGES)
    r = _run(nc, [arrays], core_ids=[0])
    return r.results[0]["out_0"]
```

```python
import numpy as np
from contextlib import ExitStack

import concourse.bass as bass
from concourse import mybir

F32 = mybir.dt.float32
BF16 = mybir.dt.bfloat16
I32 = mybir.dt.int32
ALU = mybir.AluOpType
ACT = mybir.ActivationFunctionType
AX = mybir.AxisListType

P = 128
D = 1024
SEQ = 256
TT = SEQ // P
KC = D // P
NH = 4
DK = 64
LC = 64
NT = 16
NE = 64
NG = 8
TOPK = 8
TOPK_GROUPS = 4
DE = 256
JE = DE // P
CAP = 64
MAX_PASS = SEQ // CAP
NSLOT = 4
PAIRS = NE // 2
ALPHA = 4.0 ** 0.25
EPS = 1e-5
ROUTED_SCALE = 2.5
EW = KC * DE
BIG = 1e30


class Chain:

    def __init__(self, eng, sem):
        self.eng, self.sem, self.n = eng, sem, 0

    def link(self, ins):
        self.n += 1
        ins.then_inc(self.sem, 1)
        self.eng.wait_ge(self.sem, self.n)


class Banks:

    def __init__(self, tiles, full, done_a, done_d, jobs, fixed, turns=8):
        self.tiles, self.full_sem, self.done = tiles, full, {"a": done_a, "d": done_d}
        self.jobs, last, count, turn = {}, {}, {"a": 0, "d": 0}, 0
        for i, (name, reader) in enumerate(jobs):
            b = fixed[name] if name in fixed else turn % turns
            turn += name not in fixed
            if reader:
                count[reader] += 1
            self.jobs[name] = (b, i + 1, reader, count.get(reader, 0), last.get(b))
            last[b] = name

    def tile(self, name):
        return self.tiles[self.jobs[name][0]]

    def full(self, name):
        return self.full_sem, self.jobs[name][1]

    def read(self, name):
        _, _, reader, n, _ = self.jobs[name]
        return self.done[reader], n

    def wait_free(self, pe, name):
        before = self.jobs[name][4]
        if before:
            pe.wait_ge(*self.read(before))


def build(nc, A, out, stages=("mix0", "moe0", "mix1", "moe1")):
    ctx = ExitStack()
    with ctx:
        def sb(name, shape, dt=F32):
            return ctx.enter_context(nc.sbuf_tensor(name, shape, dt))

        def sem(name):
            return ctx.enter_context(nc.semaphore(name))

        def sems(prefix, names):
            return {n: sem(f"{prefix}{n}") for n in names.split()}

        ew = sb("expert_weights", [P, NSLOT, 3 * EW])
        wring = sb("weight_ring", [P, 2, KC * 512])
        h = sb("h", [P, TT, D])
        hT = sb("hT", [P, KC, SEQ])
        resid = sb("resid", [P, TT, D])
        lnw = sb("ln_w", [P, D])
        lnb = sb("ln_b", [P, D])
        ident = sb("ident", [P, P])
        upper = sb("upper_strict", [P, P])
        ones = sb("ones", [P, P])
        iota = sb("slot_iota", [P, CAP])
        gmask = sb("group_before", [P, NG, NG])
        stats = sb("ln_stats", [P, TT, 2, 6])
        mv = sb("ln_mean_var", [P, TT, 2])
        rstd = sb("ln_rstd", [P, TT])
        epsc = sb("eps", [P, 1])
        bank = [ctx.enter_context(nc.psum_tensor(f"bank{i}", [P, 512], F32)) for i in range(8)]
        onehot_f = sb("onehot", [P, 512])
        onehot = onehot_f[:, 0:2 * TT * CAP].bitcast(BF16).rearrange("p (u t a s) -> p u t a s", u=2, t=TT, a=2)
        gated = sb("gated_onehot", [P, 2, TT, 2, CAP])
        onehotT_f = sb("onehotT", [P, 2, TT, P])
        onehotT = onehotT_f[:, :, :, :].rearrange("p u t s -> p (u t s)")[:, 0:TT * P].bitcast(BF16)\
            .rearrange("p (u t s) -> p u t s", u=2, t=TT)
        slot_gate = sb("slot_gate", [P, 2])
        xg = sb("gathered_xT", [P, KC, 2 * CAP])
        sg = sb("silu_gate", [P, DE])
        hslot = sb("hidden", [P, DE])
        hm = sb("hiddenT", [P, JE, P])
        ysb = sb("expert_out", [P, D])
        h_rest = (ysb[:, :], xg[:, :, :].rearrange("p c s -> p (c s)"))
        rw = sb("router_w", [P, KC, NE])
        rbias = sb("router_bias", [P, NE])
        scores = sb("scores", [P, TT, NE])
        biased = sb("biased", [P, TT, NE])
        masked = sb("masked", [P, TT, NE])
        replaced = sb("replaced", [P, TT, NE])
        chosen = sb("chosen", [P, TT, NE])
        wts = sb("wts", [P, TT, NE])
        top8 = sb("top8", [P, TT, NG, 8])
        grp = sb("grp", [P, TT, NG])
        gcmp = sb("gcmp", [P, TT, NG, NG])
        gcmp2 = sb("gcmp2", [P, TT, NG, NG])
        grank = sb("grank", [P, TT, NG])
        best = sb("best", [P, TT, 8])
        argw = sb("decay_scores", [P, NH, SEQ + P])
        y_part = argw[:, :, :].rearrange("p h n -> p (h n)").bitcast(BF16).rearrange("p (i n) -> p i n", i=3)
        wsum = sb("wsum", [P, TT])
        rank = sb("rank", [P, TT, NE + 2])
        cw = sb("combine_w", [P, TT, NE + 2])
        cnt = sb("cnt", [1, 8])
        npass_i = sb("npass", [1, 1], I32)

        ws = ew[:, 2:4, :].rearrange("p s n -> p (s n)")
        work6 = sb("gate_rows", [P, 6, SEQ])
        rows = work6[0:NH]
        zin = work6[:, 0:2, :]
        sel = sb("row_selector", [NH, NH, P])
        wgate = sb("w_gates", [P, KC, 16])
        cols0 = sb("cols_even", [P, 34])
        lamb = sb("lambda_work", [P, 6, NH])
        gcol = sb("gate_cols", [P, 2, TT, NH])
        maskc = sb("causal_floor", [P, SEQ])
        hstat = sb("head_stats", [P, TT, NH, 6])
        hmv = sb("head_mean_var", [P, TT, NH, 2])
        hrs = sb("head_rstd", [P, TT, NH])
        rden = sb("den_inv", [P, NH, TT])

        gate_w = sb("gla_gate_w", [16, NH * DK])
        lowT = sb("gate_low_rankT", [16, SEQ])
        cols1 = sb("cols_odd", [P, 58])
        prm = sb("s5_work", [P, 13, NT])

        S = sems("s_", "x_loaded consts dve_chain act_chain pool_chain h_ready ring_used out_stored "
                 "ln_stats ln_std")
        LN = [sems(f"ln{k}_", "params") for k in range(4)]
        MO = [sems(f"moe{l}_", "router_in tA tD hT_a hT_d rank_next sh_gu sh_silu sh_hidden scores_psum scores "
                   "chosen rank_psum npass gather_lo gather_hi onehot gated pt_full pt_ready "
                   "xg_lo xg_hi gu_full silu hidden ht_full ht_ready y_lo_full y_hi_full y_lo y_hi "
                   "acc_full top_parts rest low_part y_rest y_parts") for l in range(2)]
        M0 = sems("m0_", "params full done_a done_d splus rows em xc lam_exp log_a a_t gain root "
                  "expd hstat hstd yhead y_lru out_full")
        M1 = sems("m1_", "cols params full done_a done_d zeros dt ang sine coef bbar step_re step_im cneg "
                  "gla_ln gla_last decays ki masked hstat hstd yhead z x y5 gelu5 y_s5 "
                  "out_full")
        for l in range(2):
            MO[l]["gu_in"] = [sem(f"moe{l}_gu_in{s}") for s in range(NSLOT)]
            MO[l]["d_in"] = [sem(f"moe{l}_d_in{s}") for s in range(NSLOT)]
        ring_in = [sem(f"ring_in{i}") for i in range(2)]

        ring = []

        def ring_add(name, parts):
            ring.append((name, parts))

        for st in stages:
            l = int(st[-1])
            if st == "mix0":
                w = A["w_in_even"][0].rearrange("(p c) n -> p c n", c=KC)
                for name, off in (("xb", 2056), ("k", 512), ("q", 0), ("v", 1024), ("gb", 2568), ("o", 1536)):
                    ring_add(f"{name}0", [(0, KC, 512, w[:, :, off:off + 512])])
            if st == "mix1":
                w = A["w_in_odd"][0].rearrange("(p c) n -> p c n", c=KC)
                for name, off in (("u", 0), ("qk", 512), ("v", 1024), ("r", 1536)):
                    ring_add(f"{name}1", [(0, KC, 512, w[:, :, off:off + 512])])
                out_b = A["w_out"][1].rearrange("(m p) n -> p m n", p=P)
                ring_add("glu1", [(0, 4, 512, A["s5_glu_w"][0].rearrange("(q p) n -> p q n", p=P))])
                ring_add("out_b1", [(0, 4, D, out_b[:, 4:8, :])])
                ring_add("out_a1", [(0, 4, D, out_b[:, 0:4, :])])
            if st == "mix0":
                w = A["w_out"][l].rearrange("(m p) n -> p m n", p=P)
                ring_add(f"out_b{l}", [(0, 4, D, w[:, 4:8, :])])
                ring_add(f"out_a{l}", [(0, 4, D, w[:, 0:4, :])])
            if st.startswith("moe"):
                g = A["sh_w_gate"][l].rearrange("(p c) f -> p c f", c=KC)
                u = A["sh_w_up"][l].rearrange("(p c) f -> p c f", c=KC)
                d = A["sh_w_down"][l].rearrange("(p j) n -> p j n", j=JE)
                ring_add(f"sh_gu{l}", [(0, KC, DE, g), (EW, KC, DE, u)])
                ring_add(f"sh_d{l}", [(0, JE, D, d)])
        ring_no = {name: n for n, (name, _) in enumerate(ring)}

        def slot_of(name):
            return wring[:, ring_no[name] % 2, :]

        h_part = [[resid[:, 1, :].bitcast(BF16).rearrange("p (t d) -> p t d", t=TT)] +
                  [slot_of(f"sh_d{l}")[:, JE * D + i * D:JE * D + (i + 1) * D].bitcast(BF16)
                   .rearrange("p (t d) -> p t d", t=TT) for i in range(2)]
                  if f"moe{l}" in stages else None for l in range(2)]

        def ring_load(sp, n):
            if n >= 2:
                sp.wait_ge(S["ring_used"], n - 1)
            for off, c, w, src in ring[n][1]:
                sp.dma_start(wring[:, n % 2, off:off + c * w].rearrange("p (c w) -> p c w", w=w), src)\
                  .then_inc(ring_in[n % 2], 16)

        def ring_arrived(eng, name):
            n = ring_no[name]
            parts = sum(len(ring[m][1]) for m in range(n + 1) if m % 2 == n % 2)
            eng.wait_ge(ring_in[n % 2], 16 * parts)

        def ew_gu(s, c):
            return ew[:, s, 0:2 * EW].rearrange("p (w c f) -> p w c f", w=2, c=KC)[:, :, c, :]

        def ew_d(s):
            return ew[:, s, 2 * EW:3 * EW].rearrange("p (j n) -> p j n", j=JE)

        stage_no = {st: k for k, st in enumerate(stages)}
        block = ctx.enter_context(nc.Block())

        def wait_h(eng, st, t=TT - 1):
            k = stage_no[st]
            if k == 0:
                eng.wait_ge(S["x_loaded"], 16)
            else:
                eng.wait_ge(S["h_ready"], TT * (k - 1) + t + 1)

        def expert_load(sp, m, l, e, s):
            src_g = A["exp_w_gate"][l, e].rearrange("(p c) f -> p (c f)", c=KC)
            src_u = A["exp_w_up"][l, e].rearrange("(p c) f -> p (c f)", c=KC)
            sp.dma_start(ew[:, s, 0:EW], src_g).then_inc(m["gu_in"][s], 16)
            sp.dma_start(ew[:, s, EW:2 * EW], src_u).then_inc(m["gu_in"][s], 16)

        def down_src(l, e):
            return A["exp_w_down"][l, e].rearrange("(p j) n -> p (j n)", j=JE)

        def sp_ln_params(sp, k, w, b):
            if k:
                sp.wait_ge(S["h_ready"], TT * k)
            sp.dma_start(lnw[:, :], w.partition_broadcast(P)).then_inc(LN[k]["params"], 16)
            sp.dma_start(lnb[:, :], b.partition_broadcast(P)).then_inc(LN[k]["params"], 16)

        def sp_mix0(sp):
            k = stage_no["mix0"]
            for dst, src in ((wgate[:, :, 0:8], A["w_in_even"][0].rearrange("(p c) n -> p c n", c=KC)[:, :, 2048:2056]),
                             (cols0[:, :], A["cols_even"]),
                             (gated[:, :, :, :, :].rearrange("p u t a s -> p (u t a s)").rearrange("p (h j) -> p h j", h=NH),
                              A["lru_wa"][0].rearrange("h i j -> i h j")),
                             (onehotT_f[:, :, :, :].rearrange("p u t s -> p (u t s)").rearrange("p (h j) -> p h j", h=NH),
                              A["lru_wx"][0].rearrange("h i j -> i h j")),
                             (onehot_f[:, :],
                              A["mlstm_norm_w"][0].partition_broadcast(P))):
                sp.dma_start(dst, src).then_inc(M0["params"], 16)
            for name in ("xb0", "k0", "q0", "v0", "gb0", "o0", "out_b0", "out_a0"):
                ring_load(sp, ring_no[name])
            sp_ln_params(sp, k, A["ln1_w"][0], A["ln1_b"][0])

        def sp_mix1(sp):
            k = stage_no["mix1"]
            ring_load(sp, ring_no["u1"])
            if k:
                sp.wait_ge(MO[0]["acc_full"], TT)
            for dst, src in ((xg[:, :, :].rearrange("p c s -> p (c s)"), A["b_odd"]),
                             (wgate[:, :, :], A["w_in_odd"][0].rearrange("(p c) n -> p c n", c=KC)[:, :, 2048:2064]),
                             (gate_w[:, :], A["gla_gate_w"][0]),
                             (onehot_f[:, :],
                              A["gla_norm_w"][0].partition_broadcast(P))):
                sp.dma_start(dst, src).then_inc(M1["params"], 16)
            if k:
                sp.wait_ge(S["h_ready"], TT * k)
            sp.wait_ge(M1["coef"], 1)
            sp.dma_start(resid[:, 1, :], A["c_odd"]).then_inc(M1["cols"], 16)
            for name in ("qk1", "v1", "r1", "glu1", "out_b1", "out_a1"):
                ring_load(sp, ring_no[name])
            sp_ln_params(sp, k, A["ln1_w"][1], A["ln1_b"][1])

        def first_load(sp, m, l, s):
            expert_load(sp, m, l, s, s)
            sp.dma_start(ew[:, s, 2 * EW:3 * EW], down_src(l, s)).then_inc(m["d_in"][s], 16)

        EARLY_SLOTS = (2, 1)

        def sp_moe(sp, l):
            m = MO[l]
            k = stage_no[f"moe{l}"]
            sp.dma_start(rw[:, :, :], A["router_w"][l].rearrange("(p c) e -> p c e", c=KC))\
              .then_inc(m["router_in"], 16)
            sp.dma_start(rbias[:, :], A["router_bias"][l].partition_broadcast(P)).then_inc(m["router_in"], 16)
            ring_load(sp, ring_no[f"sh_gu{l}"])
            early = EARLY_SLOTS[l] if k else 0
            if l == 1 and k:
                sp.wait_ge(*B1.full("o1"))
            for s in range(early):
                first_load(sp, m, l, s)
            ring_load(sp, ring_no[f"sh_d{l}"])
            if k:
                sp.wait_ge(S["h_ready"], TT * k)
            for s in range(early, NSLOT):
                first_load(sp, m, l, s)
            sp_ln_params(sp, k, A["ln2_w"][l], A["ln2_b"][l])

            def group(base, it):
                for u in range(2):
                    sp.wait_ge(m["gu_full"], (base - 1) * 2 + u + 1)
                    for s in (2 * u, 2 * u + 1):
                        expert_load(sp, m, l, it * NSLOT + s, s)
                    sp.wait_ge(m["y_hi_full"], (base - 1) * 2 + u + 1)
                    for s in (2 * u, 2 * u + 1):
                        sp.dma_start(ew[:, s, 2 * EW:3 * EW], down_src(l, it * NSLOT + s)).then_inc(m["d_in"][s], 16)

            with sp.Fori(1, NE // NSLOT) as it:
                group(it, it)
            sp.wait_ge(m["npass"], 1)
            npass = sp.value_load(npass_i[0:1, 0:1], min_val=1, max_val=MAX_PASS)
            with sp.If(npass > 1):
                with sp.Fori(1, npass) as ps:
                    with sp.Fori(0, NE // NSLOT) as it:
                        group(ps * (NE // NSLOT) + it, it)

        def view(off, *shape, base=ws):
            n = int(np.prod(shape))
            v = base[:, off:off + n]
            if len(shape) == 2:
                v = v.rearrange("p (a b) -> p a b", a=shape[0])
            if len(shape) == 3:
                v = v.rearrange("p (a b c) -> p a b c", a=shape[0], b=shape[1])
            return v

        DH = 128
        views, at = {}, 0
        for name, shape in (("qT", (NH, SEQ)), ("kT", (NH, SEQ)), ("v1", (TT, NH, DH + 1)), ("og", (TT, 512)),
                            ("xbp", (NH, SEQ + 3)), ("xc", (NH, SEQ)), ("rg", (NH, SEQ)), ("ig", (NH, SEQ)),
                            ("gg", (NH, SEQ)), ("mixT", (8, SEQ))):
            views[name] = view(at, *shape)
            at += int(np.prod(shape))
        V = dict(views)
        hbuf = resid[:, 0, :].rearrange("p (t n) -> p t n", t=TT)
        abuf = ysb[:, :].rearrange("p (h t) -> p h t", h=NH)
        tbuf = resid[:, 1, :].rearrange("p (h t) -> p h t", h=NH)
        wa_v = gated[:, :, :, :, :].rearrange("p u t a s -> p (u t a s)").rearrange("p (h j) -> p h j", h=NH)
        wx_v = onehotT_f[:, :, :, :].rearrange("p u t s -> p (u t s)").rearrange("p (h j) -> p h j", h=NH)
        normw = onehot_f[:, :]
        B0 = Banks(bank, M0["full"], M0["done_a"], M0["done_d"],
                   [("T0", "a"), ("T1", "d"), ("T2", "a"), ("T3", "d"), ("gates", "d"), ("xb0", "a"), ("xb1", "a"),
                    ("k0", "a"), ("k1", "a"), ("q0", "a"), ("q1", "a"), ("cols", "d"), ("bc0", "d"), ("bc1", "d"),
                    ("r0", "a"), ("r1", "a"), ("i0", "a"), ("i1", "a"), ("v0", "a"), ("v1", "a"),
                    ("S0", "d"), ("S1", "d"), ("S2", "d"), ("S3", "d"), ("gb0", "a"), ("gb1", "a"),
                    ("N0", "d"), ("N1", "d"), ("N2", "d"), ("N3", "d"), ("o0", "a"), ("o1", "a"),
                    ("out0", None), ("out1", None), ("out2", None), ("out3", None), ("yT0", "a"), ("yT1", "d")],
                   {"out0": 0, "out1": 1, "out2": 2, "out3": 3, "yT0": 4, "yT1": 5})

        ws1 = ew[:, :, :].rearrange("p s n -> p (s n)")
        views, at = {}, 0
        for name, shape in (("la", (2, SEQ)), ("e1", (2, SEQ)), ("bc", (2, SEQ)), ("e2", (2, SEQ)), ("e3", (2, SEQ)),
                            ("qd", (2, SEQ)), ("ki", (2, SEQ)), ("ke", (2, SEQ)), ("att", (NH, TT, P)),
                            ("v", (TT, 512)), ("cos", (NT, SEQ)), ("sin", (NT, SEQ)), ("uT", (4, SEQ)),
                            ("og", (TT, 512)), ("mixT", (8, SEQ)), ("gT", (4, SEQ)), ("m1", (2, SEQ)),
                            ("m2", (2, SEQ)), ("z", (4, 2, SEQ)), ("x", (4, 2, SEQ))):
            views[name] = view(at, *shape, base=ws1)
            at += int(np.prod(shape))
        W = dict(views)
        W["ke_tok"] = W["la"]
        W["state"] = argw[:, :, :].rearrange("p h n -> p (h n)").rearrange("p (c q n) -> p c q n", c=3, q=4)
        W["braw"] = xg[:, :, :].rearrange("p c s -> p (c s)").rearrange("p (w i n) -> p w i n", w=2, i=NT)
        W["craw"] = resid[:, 1, :].rearrange("p (w i n) -> p w i n", w=2, i=NT)
        W["bT"] = ysb[:, :].rearrange("p (w q n) -> p w q n", w=2, q=4)
        W["bbar"] = W["z"].rearrange("p a b n -> p (a b n)").rearrange("p (w i n) -> p w i n", w=4, i=NT)
        W["p1"] = gated[:, :, :, :, :].rearrange("p u t a s -> p (u t a s)").rearrange("p (w n) -> p w n", w=2)
        W["p2"] = onehotT_f[:, :, :, :].rearrange("p u t s -> p (u t s)").rearrange("p (w n) -> p w n", w=2)
        restart = maskc
        odd_jobs = [("T0", "a"), ("T1", "d"), ("T2", "a"), ("T3", "d"), ("low", "a"), ("u0", "a"), ("u1", "a"),
                    ("ga", "d"), ("bT0", "a"), ("bT1", "a")]
        odd_jobs += [(f"bu{i}", "d") for i in range(4)] + [("qk0", "d"), ("qk1", "d")]
        odd_jobs += [(f"bu{i}", "d") for i in range(4, 7)] + [("v0", "a")]
        odd_jobs += [(f"bu{i}", "d") for i in range(7, 10)] + [("v1", "a"), ("att0", "a"), ("att1", "a"), ("keT", "a")]
        odd_jobs += [(f"bu{i}", "d") for i in range(10, 13)] + [("U0", "d"), ("U1", "d"), ("U2", "d"), ("r0", "a")]
        odd_jobs += [(f"bu{i}", "d") for i in range(13, 16)] + [("o0", "d"), ("o1", "d"), ("r1", "a")]
        odd_jobs += [("y0", "d"), ("y1", "d"), ("yT0", "a"), ("yT1", "a"), ("gl0", "a"), ("gl1", "a"),
                     ("out0", None), ("out1", None), ("out2", None), ("out3", None)]
        B1 = Banks(bank, M1["full"], M1["done_a"], M1["done_d"], odd_jobs,
                   {"out0": 0, "out1": 1, "out2": 2, "out3": 3, "yT0": 4, "yT1": 5, "T0": 4, "T1": 5, "T2": 6, "T3": 7,
                    "y0": 6, "y1": 7, "gl0": 4, "gl1": 5},
                   turns=6)
        N_STEPS = 8

        @block.sync
        def _(sp):
            if "mix1" in stages:
                sp.dma_start(cols1[:, :], A["cols_odd"]).then_inc(M1["cols"], 16)
            sp.dma_start(h[:, :, :], A["x"][0].rearrange("(t p) d -> p t d", p=P)).then_inc(S["x_loaded"], 16)
            for st in stages:
                if st == "mix0":
                    sp_mix0(sp)
                if st == "mix1":
                    sp_mix1(sp)
                if st.startswith("moe"):
                    sp_moe(sp, int(st[-1]))
            for t in range(TT):
                sp.wait_ge(S["h_ready"], TT * (len(stages) - 1) + t + 1)
                sp.dma_start(out[0, t * P:(t + 1) * P, :], h[:, t, :]).then_inc(S["out_stored"], 16)
            sp.wait_ge(S["out_stored"], 16 * TT)

        def pool_mix1(pool, chain):
            if stage_no["mix1"]:
                pool.wait_ge(MO[0]["acc_full"], TT)
            nc.gpsimd.memset(restart[:, :], 1.0)
            nc.gpsimd.memset(W["att"], 0.0)
            chain.link(nc.gpsimd.memset(W["state"], 0.0))
            nc.gpsimd.memset(restart[:, 0:SEQ:LC], 0.0).then_inc(M1["zeros"], 1)
            pool_bbar(pool, chain)
            for k in range(N_STEPS):
                n = 1 << k
                pool.wait_ge(M1["step_im"], k + 1)
                pool.wait_ge(M1["step_re"], k + 1)
                new = W["cos"][:, :, n:2 * n]
                tmp = W["gT"].rearrange("p a t -> p (a t)")[:, 0:NT * n].rearrange("p (i t) -> p i t", i=NT) if n <= 64 \
                    else W["mixT"].rearrange("p a t -> p (a t)").rearrange("p (i t) -> p i t", i=NT)
                cr = W["cos"][:, :, n - 1:n].broadcast_to([P, NT, n])
                ci = W["sin"][:, :, n - 1:n].broadcast_to([P, NT, n])
                nc.gpsimd.tensor_tensor(new, W["cos"][:, :, 0:n], cr, ALU.mult)
                chain.link(nc.gpsimd.tensor_tensor(tmp, W["sin"][:, :, 0:n], ci, ALU.mult))
                nc.gpsimd.tensor_tensor(new, new, tmp, ALU.subtract).then_inc(M1["step_re"], 1)
            for i in range(NT):
                pool_rotate(pool, chain, i)
                if i == 10:
                    pool.wait_ge(*B1.read("att1"))
                    pool.wait_ge(M1["x"], i + 1)
                    for b in range(2):
                        part = W["att"].rearrange("p h t s -> p (h t) s")[b * LC:(b + 1) * LC, :, b * LC:(b + 1) * LC]
                        nc.gpsimd.affine_select(out=part, in_=part, compare_op=ALU.is_ge, fill=0.0, base=0,
                                                pattern=[[0, NH * TT], [1, LC]], channel_multiplier=-1)\
                                 .then_inc(M1["masked"], 1)
                        pool.wait_ge(M1["masked"], b + 1)

        def pool_bbar(pool, chain):
            pool.wait_ge(M1["params"], 64)
            pool.wait_ge(M1["coef"], 1)
            cr = prm[:, 8, :].unsqueeze(2).broadcast_to([P, NT, 32])
            ci = prm[:, 9, :].unsqueeze(2).broadcast_to([P, NT, 32])
            nc.gpsimd.tensor_tensor(W["bbar"][:, 0], W["braw"][:, 0], cr, ALU.mult)
            nc.gpsimd.tensor_tensor(W["bbar"][:, 1], W["braw"][:, 1], cr, ALU.mult)
            nc.gpsimd.tensor_tensor(W["bbar"][:, 2], W["braw"][:, 1], ci, ALU.mult)
            chain.link(nc.gpsimd.tensor_tensor(W["bbar"][:, 3], W["braw"][:, 0], ci, ALU.mult))
            nc.gpsimd.tensor_tensor(W["bbar"][:, 0], W["bbar"][:, 0], W["bbar"][:, 2], ALU.subtract)
            nc.gpsimd.tensor_tensor(W["bbar"][:, 1], W["bbar"][:, 1], W["bbar"][:, 3], ALU.add).then_inc(M1["bbar"], 1)

        def pool_moe(pool, l):
            m = MO[l]
            for t in range(TT):
                pool.wait_ge(m["top_parts"], t + 1)
                nc.gpsimd.tensor_tensor(h_rest[t], h[:, t, :], h_part[l][0][:, t, :], ALU.subtract).then_inc(m["rest"], 1)

        def pool_rotate(pool, chain, i):
            q = i % 4
            pool.wait_ge(M1["z"], i + 1)
            if i == 0:
                pool.wait_ge(M1["step_im"], N_STEPS + 1)
                pool.wait_ge(M1["step_re"], N_STEPS + 1)
            if i >= 1:
                pool.wait_ge(M1["x"], i)
            if i >= 4:
                pool.wait_ge(M1["y5"], i - 3)
            c = W["cos"][:, i, :].unsqueeze(1).broadcast_to([P, 2, SEQ])
            sn = W["sin"][:, i, :].unsqueeze(1).broadcast_to([P, 2, SEQ])
            nc.gpsimd.tensor_tensor(W["p1"], W["z"][:, q], c, ALU.mult)
            chain.link(nc.gpsimd.tensor_tensor(W["p2"], W["z"][:, q], sn, ALU.mult))
            nc.gpsimd.tensor_tensor(W["x"][:, q, 0, :], W["p1"][:, 0, :], W["p2"][:, 1, :], ALU.subtract)
            nc.gpsimd.tensor_tensor(W["x"][:, q, 1, :], W["p1"][:, 1, :], W["p2"][:, 0, :], ALU.add).then_inc(M1["x"], 1)

        @block.gpsimd
        def _(pool):
            chain = Chain(pool, S["pool_chain"])
            chain.link(nc.gpsimd.memset(ident[:, :], 0.0))
            nc.gpsimd.affine_select(out=ident[:, :], in_=ident[:, :], compare_op=ALU.not_equal, fill=1.0,
                                    base=0, pattern=[[-1, P]], channel_multiplier=1).then_inc(S["consts"], 1)
            chain.link(nc.gpsimd.memset(upper[:, :], 1.0))
            nc.gpsimd.affine_select(out=upper[:, :], in_=upper[:, :], compare_op=ALU.is_gt, fill=0.0,
                                    base=0, pattern=[[1, P]], channel_multiplier=-1).then_inc(S["consts"], 1)
            nc.gpsimd.memset(ones[:, :], 1.0).then_inc(S["consts"], 1)
            nc.gpsimd.iota(iota[:, :], pattern=[[1, CAP]], base=0, channel_multiplier=0,
                           allow_small_or_imprecise_dtypes=True).then_inc(S["consts"], 1)
            chain.link(nc.gpsimd.memset(gmask[:, :, :], 1.0))
            nc.gpsimd.affine_select(out=gmask[:, :, :], in_=gmask[:, :, :], compare_op=ALU.is_gt, fill=0.0,
                                    base=0, pattern=[[1, NG], [-1, NG]], channel_multiplier=0)\
                     .then_inc(S["consts"], 1)
            chain.link(nc.gpsimd.memset(maskc[:, :], 0.0))
            nc.gpsimd.affine_select(out=maskc[:, 0:P], in_=maskc[:, 0:P], compare_op=ALU.is_ge, fill=-BIG,
                                    base=0, pattern=[[1, P]], channel_multiplier=-1).then_inc(S["consts"], 1)
            chain.link(nc.gpsimd.memset(sel[:, :, :], 0.0))
            nc.gpsimd.affine_select(out=sel[:, :, :], in_=sel[:, :, :], compare_op=ALU.not_equal, fill=1.0,
                                    base=0, pattern=[[-1, NH], [0, P]], channel_multiplier=1).then_inc(S["consts"], 1)
            nc.gpsimd.memset(epsc[:, :], EPS).then_inc(S["consts"], 1)

            for st in stages:
                if st == "mix1":
                    pool_mix1(pool, chain)
                if st.startswith("moe"):
                    pool_moe(pool, int(st[-1]))

        N_CONSTS = 8

        def channel_major(pe, B, w, name, i):
            B.wait_free(pe, f"{name}{i}")
            for a in range(2):
                for c in range(KC):
                    last = nc.tensor.matmul(B.tile(f"{name}{i}")[:, a * SEQ:(a + 1) * SEQ],
                                            w[:, c, (2 * i + a) * P:(2 * i + a + 1) * P], hT[:, c, :],
                                            start=(c == 0), stop=(c == KC - 1))
            last.then_inc(B.full_sem, 1)
            return last

        def token_major(pe, B, w, name, t):
            B.wait_free(pe, f"{name}{t}")
            for c in range(KC):
                last = nc.tensor.matmul(B.tile(f"{name}{t}")[:, :], hT[:, c, t * P:(t + 1) * P], w[:, c, :],
                                        start=(c == 0), stop=(c == KC - 1))
            last.then_inc(B.full_sem, 1)

        def ring_view(name, chunks=KC):
            return slot_of(name).rearrange("p (c n) -> p c n", c=chunks)

        def ring_done(pe, B, name):
            pe.wait_ge(*B.full(name))
            pe.sem_inc(S["ring_used"], 1)

        def pe_transposes(pe, B, st):
            for t in range(TT):
                wait_h(pe, st, t)
                for b in range(4):
                    for c in (2 * b, 2 * b + 1):
                        last = nc.tensor.transpose(B.tile(f"T{b}")[:, (c % 2) * SEQ + t * P:(c % 2) * SEQ + (t + 1) * P],
                                                   h[:, t, :].rearrange("p (q c) -> p c q", c=KC)[:, c, :],
                                                   ident[:, :])
                    if t == TT - 1:
                        last.then_inc(B.full_sem, 1)
            for b in range(4):
                pe.wait_ge(*B.read(f"T{b}"))

        def pe_out(pe, B, l, mixT, part, out_full=None):
            ring_arrived(pe, f"out_{part}{l}")
            w = ring_view(f"out_{part}{l}", 4)
            first = part == "b"
            for t in range(TT):
                for n in range(2):
                    if first:
                        B.wait_free(pe, f"out{2 * t + n}")
                    for m in range(4):
                        last = nc.tensor.matmul(bank[2 * t + n][:, :], mixT[:, m + 4 * first, t * P:(t + 1) * P],
                                                w[:, m, n * 512:(n + 1) * 512],
                                                start=(first and m == 0), stop=(not first and m == 3))
                    if first:
                        last.then_inc(B.full_sem, 1)
                if not first:
                    last.then_inc(out_full, 1)

        def pe_mix0(pe):
            B = B0
            pe_transposes(pe, B, "mix0")
            pe.wait_ge(M0["params"], 80)
            B.wait_free(pe, "gates")
            for g in range(2):
                for c in range(KC):
                    last = nc.tensor.matmul(B.tile("gates")[0:NH, g * SEQ:(g + 1) * SEQ], wgate[:, c, g * NH:(g + 1) * NH],
                                            hT[:, c, :], start=(c == 0), stop=(c == KC - 1))
            last.then_inc(B.full_sem, 1)
            for name in ("xb", "k", "q"):
                ring_arrived(pe, f"{name}0")
                channel_major(pe, B, ring_view(f"{name}0"), name, 0)
                channel_major(pe, B, ring_view(f"{name}0"), name, 1)
                ring_done(pe, B, f"{name}1")
            B.wait_free(pe, "cols")
            pe.wait_ge(M0["rows"], 1)
            pe.wait_ge(M0["em"], 1)
            for i, row in enumerate((0, 5)):
                for t in range(TT):
                    last = nc.tensor.transpose(B.tile("cols")[:, (i * TT + t) * NH:(i * TT + t + 1) * NH],
                                               rows[:, row, t * P:(t + 1) * P], ident[0:NH, 0:NH])
            last.then_inc(B.full_sem, 1)
            for i in range(2):
                B.wait_free(pe, f"bc{i}")
                for a in range(2):
                    last = nc.tensor.matmul(B.tile(f"bc{i}")[:, a * SEQ:(a + 1) * SEQ], sel[:, 2 * i + a, :],
                                            rows[:, 4, :], start=True, stop=True)
                last.then_inc(B.full_sem, 1)
            pe.wait_ge(M0["xc"], 1)
            for name, w in (("r", wa_v), ("i", wx_v)):
                for i in range(2):
                    B.wait_free(pe, f"{name}{i}")
                    for a in range(2):
                        last = nc.tensor.matmul(B.tile(f"{name}{i}")[:, a * SEQ:(a + 1) * SEQ], w[:, 2 * i + a, :],
                                                V["xc"][:, 2 * i + a, :], start=True, stop=True)
                    last.then_inc(B.full_sem, 1)
            ring_arrived(pe, "v0")
            for t in range(TT):
                token_major(pe, B, ring_view("v0"), "v", t)
            ring_done(pe, B, "v1")
            pe.wait_ge(*B.read("q1"))
            for hd in range(NH):
                B.wait_free(pe, f"S{hd}")
                nc.tensor.matmul(B.tile(f"S{hd}")[:, 0:SEQ], V["kT"][:, hd, 0:P], V["qT"][:, hd, :], start=True, stop=True)
                nc.tensor.matmul(B.tile(f"S{hd}")[:, SEQ:SEQ + P], V["kT"][:, hd, P:SEQ], V["qT"][:, hd, P:SEQ],
                                 start=True, stop=True).then_inc(B.full_sem, 1)
            ring_arrived(pe, "gb0")
            for i in range(2):
                channel_major(pe, B, ring_view("gb0"), "gb", i)
            ring_done(pe, B, "gb1")
            pe.wait_ge(*B.read("v1"))
            for hd in range(NH):
                B.wait_free(pe, f"N{hd}")
                pe.wait_ge(*B.read(f"S{hd}"))
                acc = B.tile(f"N{hd}")
                nc.tensor.matmul(acc[:, 0:DH + 1], argw[:, hd, 0:P], V["v1"][:, 0, hd, :], start=True, stop=True)
                nc.tensor.matmul(acc[:, SEQ:SEQ + DH + 1], argw[:, hd, P:SEQ], V["v1"][:, 0, hd, :], start=True, stop=False)
                nc.tensor.matmul(acc[:, SEQ:SEQ + DH + 1], argw[:, hd, SEQ:SEQ + P], V["v1"][:, 1, hd, :],
                                 start=False, stop=True).then_inc(B.full_sem, 1)
            ring_arrived(pe, "o0")
            for t in range(TT):
                token_major(pe, B, ring_view("o0"), "o", t)
            ring_done(pe, B, "o1")
            pe.wait_ge(M0["y_lru"], 1)
            pe_out(pe, B, 0, V["mixT"], "b")
            ring_done(pe, B, "out3")
            pe.wait_ge(M0["yhead"], 1)
            pe_head_transposes(pe, B)
            pe_out(pe, B, 0, V["mixT"], "a", M0["out_full"])
            pe.wait_ge(M0["out_full"], TT)
            pe.sem_inc(S["ring_used"], 1)

        def pe_mix1(pe):
            B = B1
            pe_transposes(pe, B, "mix1")
            pe.wait_ge(M1["params"], 64)
            B.wait_free(pe, "low")
            for c in range(KC):
                last = nc.tensor.matmul(B.tile("low")[0:16, 0:SEQ], wgate[:, c, :], hT[:, c, :],
                                        start=(c == 0), stop=(c == KC - 1))
            last.then_inc(B.full_sem, 1)
            ring_arrived(pe, "u1")
            for i in range(2):
                channel_major(pe, B, ring_view("u1"), "u", i)
            ring_done(pe, B, "u1")
            B.wait_free(pe, "ga")
            pe.wait_ge(*B.read("low"))
            for a in range(2):
                last = nc.tensor.matmul(B.tile("ga")[:, a * SEQ:(a + 1) * SEQ], gate_w[:, a * P:(a + 1) * P],
                                        lowT[:, :], start=True, stop=True)
            last.then_inc(B.full_sem, 1)
            pe.wait_ge(M1["bbar"], 1)
            for w in range(2):
                B.wait_free(pe, f"bT{w}")
                for q in range(4):
                    last = nc.tensor.transpose(B.tile(f"bT{w}")[:, q * P:(q + 1) * P],
                                               W["bbar"][:, w, 4 * q:4 * q + 4, :].rearrange("p i n -> p (i n)"),
                                               ident[:, :])
                last.then_inc(B.full_sem, 1)
            pe.wait_ge(*B.read("bT1"))

            def inputs(tiles):
                for i in tiles:
                    q, j = i // 4, 32 * (i % 4)
                    B.wait_free(pe, f"bu{i}")
                    for w in range(2):
                        last = nc.tensor.matmul(B.tile(f"bu{i}")[:, w * SEQ:(w + 1) * SEQ], W["bT"][j:j + 32, w, q, :],
                                                W["uT"][j:j + 32, q, :], start=True, stop=True)
                    last.then_inc(B.full_sem, 1)

            def outputs(tiles):
                for i in tiles:
                    q, j = i // 4, 32 * (i % 4)
                    pe.wait_ge(M1["x"], i + 1)
                    for w in range(2):
                        last = nc.tensor.matmul(bank[6 + q // 2][j:j + 32, (q % 2) * SEQ:(q % 2 + 1) * SEQ],
                                                W["craw"][:, w, i, :], W["x"][:, i % 4, w, :], start=(w == 0), stop=(w == 1))
                    last.then_inc(M1["y5"], 1)

            inputs(range(0, 4))
            ring_arrived(pe, "qk1")
            for i in range(2):
                channel_major(pe, B, ring_view("qk1"), "qk", i)
            ring_done(pe, B, "qk1")
            pe.wait_ge(M1["cneg"], 1)
            outputs(range(0, 3))
            inputs(range(4, 7))
            ring_arrived(pe, "v1")
            token_major(pe, B, ring_view("v1"), "v", 0)
            outputs(range(3, 6))
            inputs(range(7, 10))
            token_major(pe, B, ring_view("v1"), "v", 1)
            ring_done(pe, B, "v1")
            pe.wait_ge(*B.read("qk1"))
            for hh in range(2):
                B.wait_free(pe, f"att{hh}")
                for pr in range(2):
                    for t in range(TT):
                        last = nc.tensor.matmul(B.tile(f"att{hh}")[:, (2 * pr + t) * P:(2 * pr + t + 1) * P],
                                                W["ki"][hh * DK:(hh + 1) * DK, pr, t * P:(t + 1) * P],
                                                W["qd"][hh * DK:(hh + 1) * DK, pr, t * P:(t + 1) * P],
                                                start=True, stop=True)
                last.then_inc(B.full_sem, 1)
            B.wait_free(pe, "keT")
            for pr in range(2):
                for t in range(TT):
                    last = nc.tensor.transpose(B.tile("keT")[:, (2 * pr + t) * P:(2 * pr + t + 1) * P],
                                               W["ke"][:, pr, t * P:(t + 1) * P], ident[:, :])
            last.then_inc(B.full_sem, 1)
            outputs(range(6, 9))
            inputs(range(10, 13))
            pe.wait_ge(*B.read("keT"))
            pe.wait_ge(*B.read("v1"))
            for c in range(3):
                t, lo = c // 2, (c % 2) * LC
                B.wait_free(pe, f"U{c}")
                for hd in range(NH):
                    last = nc.tensor.matmul(B.tile(f"U{c}")[:, hd * P:(hd + 1) * P],
                                            W["ke_tok"].rearrange("p a n -> p (a n)")[lo:lo + LC, (2 * (hd // 2) + t) * P:
                                                                                   (2 * (hd // 2) + t + 1) * P],
                                            W["v"][lo:lo + LC, t, hd * P:(hd + 1) * P], start=True, stop=True)
                last.then_inc(B.full_sem, 1)
            ring_arrived(pe, "r1")
            token_major(pe, B, ring_view("r1"), "r", 0)
            outputs(range(9, 12))
            inputs(range(13, 16))
            pe.wait_ge(M1["masked"], 2)
            pe.wait_ge(*B.read("U2"))
            for t in range(TT):
                B.wait_free(pe, f"o{t}")
                for hd in range(NH):
                    dst = B.tile(f"o{t}")[:, hd * P:(hd + 1) * P]
                    last = nc.tensor.matmul(dst, W["att"][:, hd, t, :], W["v"][:, t, hd * P:(hd + 1) * P], start=True,
                                            stop=False, skip_group_check=True)
                    for b in range(2):
                        c = 2 * t + b
                        if c > 0:
                            last = nc.tensor.matmul(dst[b * LC:(b + 1) * LC, :], W["qd"][:, hd // 2, c * LC:(c + 1) * LC],
                                                    W["state"][:, c - 1, hd, :], start=False, stop=True,
                                                    skip_group_check=True)
                last.then_inc(B.full_sem, 1)
            token_major(pe, B, ring_view("r1"), "r", 1)
            ring_done(pe, B, "r1")
            outputs(range(12, 16))
            pe.wait_ge(M1["y5"], NT)
            pe.sem_inc(B.full_sem, 2)
            pe.wait_ge(M1["yhead"], 1)
            pe_head_transposes(pe, B)
            ring_arrived(pe, "glu1")
            pe.wait_ge(M1["gelu5"], 1)
            for i in range(2):
                B.wait_free(pe, f"gl{i}")
                for a in range(2):
                    for q in range(4):
                        last = nc.tensor.matmul(B.tile(f"gl{i}")[:, a * SEQ:(a + 1) * SEQ],
                                                ring_view("glu1", 8)[:, q, (2 * i + a) * P:(2 * i + a + 1) * P],
                                                W["gT"][:, q, :], start=(q == 0), stop=(q == 3))
                last.then_inc(B.full_sem, 1)
            ring_done(pe, B, "gl1")
            pe_out(pe, B, 1, W["mixT"], "b")
            ring_done(pe, B, "out3")
            pe.wait_ge(M1["y_s5"], 1)
            pe_out(pe, B, 1, W["mixT"], "a", M1["out_full"])
            pe.wait_ge(M1["out_full"], TT)
            pe.sem_inc(S["ring_used"], 1)

        def pe_head_transposes(pe, B):
            for i in range(2):
                B.wait_free(pe, f"yT{i}")
                for a in range(2):
                    for t in range(TT):
                        last = nc.tensor.transpose(B.tile(f"yT{i}")[:, a * SEQ + t * P:a * SEQ + (t + 1) * P],
                                                   hbuf[:, t, (2 * i + a) * P:(2 * i + a + 1) * P], ident[:, :])
                last.then_inc(B.full_sem, 1)
            for i in range(2):
                pe.wait_ge(*B.read(f"yT{i}"))

        def pe_transpose_h(pe, l):
            m = MO[l]
            for t in range(TT):
                wait_h(pe, f"moe{l}", t)
                for c in range(KC):
                    last = nc.tensor.transpose(bank[4 + c // 2][:, (c % 2) * SEQ + t * P:(c % 2) * SEQ + (t + 1) * P],
                                               h[:, t, :].rearrange("p (q c) -> p c q", c=KC)[:, c, :],
                                               ident[:, :])
                    if c % 2 == 1 and t == TT - 1:
                        last.then_inc(m["tA"] if (c // 2) % 2 == 0 else m["tD"], 1)

        def pe_moe(pe, l):
            m = MO[l]
            pe_transpose_h(pe, l)
            pe.wait_ge(m["hT_a"], 2)
            pe.wait_ge(m["hT_d"], 2)
            pe.wait_ge(m["router_in"], 32)
            for t in range(TT):
                for c in range(KC):
                    last = nc.tensor.matmul(bank[6][:, t * NE:(t + 1) * NE], hT[:, c, t * P:(t + 1) * P],
                                            rw[:, c, :], start=(c == 0), stop=(c == KC - 1))
            last.then_inc(m["scores_psum"], 1)
            ring_arrived(pe, f"sh_gu{l}")
            sl = slot_of(f"sh_gu{l}")
            for w in range(2):
                wv = sl[:, w * EW:(w + 1) * EW].rearrange("p (c q j) -> p c j q", c=KC, j=JE)
                for j in range(JE):
                    for c in range(KC):
                        last = nc.tensor.matmul(bank[w][:, j * SEQ:(j + 1) * SEQ], wv[:, c, j, :], hT[:, c, :],
                                                start=(c == 0), stop=(c == KC - 1))
                last.then_inc(m["sh_gu"], 1)
                if w == 0:
                    pe.wait_ge(m["chosen"], 1)
                    nc.tensor.matmul(bank[7][:, 0:NE], upper[:, :], chosen[:, 0, :], start=True, stop=True)
                    nc.tensor.matmul(bank[7][:, NE:2 * NE], ones[:, :], chosen[:, 0, :], start=True, stop=False)
                    nc.tensor.matmul(bank[7][:, NE:2 * NE], upper[:, :], chosen[:, 1, :], start=False, stop=True)
                    nc.tensor.matmul(bank[7][0:1, 2 * NE:3 * NE], ones[:, 0:1], chosen[:, 0, :], start=True, stop=False)
                    nc.tensor.matmul(bank[7][0:1, 2 * NE:3 * NE], ones[:, 0:1], chosen[:, 1, :], start=False, stop=True)\
                      .then_inc(m["rank_psum"], 1)

            def scatter(par, done):
                for t in range(TT):
                    for n in range(2):
                        for i in range(3):
                            last = nc.tensor.matmul(bank[2 * t + n][:, :], onehotT[:, par, t, :],
                                                    y_part[:, i, n * 512:(n + 1) * 512], start=False,
                                                    stop=(done and i == 2), skip_group_check=True)
                    if done:
                        last.then_inc(m["acc_full"], 1)

            def gather(par):
                for t in range(TT):
                    last = nc.tensor.transpose(bank[6][:, t * P:(t + 1) * P],
                                               gated[:, par, t, :, :].rearrange("p a s -> p (a s)"), ident[:, :])
                last.then_inc(m["pt_full"], 1)
                for c in range(KC):
                    for t in range(TT):
                        for i in range(3):
                            last = nc.tensor.matmul(bank[4 + c // 4][:, (c % 4) * P:(c % 4 + 1) * P],
                                                    h_part[l][i][:, t, :].rearrange("p (q c) -> p c q", c=KC)[:, c, :],
                                                    onehot[:, par, t, :, :].rearrange("p a s -> p (a s)"),
                                                    start=(t == 0 and i == 0), stop=(t == TT - 1 and i == 2))
                    if c == KC // 2 - 1:
                        last.then_inc(m["gather_lo"], 1)
                last.then_inc(m["gather_hi"], 1)

            pe.wait_ge(m["low_part"], TT)
            pe.wait_ge(m["gated"], 1)
            gather(0)
            ring_arrived(pe, f"sh_d{l}")
            pe.wait_ge(m["sh_hidden"], 1)
            wd = slot_of(f"sh_d{l}")[:, 0:JE * D].rearrange("p (j n) -> p j n", j=JE)
            for t in range(TT):
                for n in range(2):
                    for j in range(JE):
                        last = nc.tensor.matmul(bank[2 * t + n][:, :], shid[:, j, t * P:(t + 1) * P],
                                                wd[:, j, n * 512:(n + 1) * 512], start=(j == 0), stop=False,
                                                skip_group_check=True)
            last.then_inc(S["ring_used"], 2)
            pe.wait_ge(m["npass"], 1)
            npass = pe.value_load(npass_i[0:1, 0:1], min_val=1, max_val=MAX_PASS)
            with pe.Fori(0, npass) as ps:
                with pe.Fori(0, NE // NSLOT) as it:
                    for u in range(2):
                        n = ps * PAIRS + it * 2 + u
                        g = ps * (NE // NSLOT) + it
                        pe.wait_ge(m["xg_lo"], n + 1)
                        pe.wait_ge(m["xg_hi"], n + 1)
                        pe.wait_ge(m["pt_ready"], n + 2)
                        for a in range(2):
                            pe.wait_ge(m["gu_in"][2 * u + a], 32 * g + 32)
                        for c in range(KC):
                            for a in range(2):
                                last = nc.tensor.matmul(
                                    bank[6][a * CAP:(a + 1) * CAP, :].rearrange("p (w f) -> p w f", w=2),
                                    xg[:, c, a * CAP:(a + 1) * CAP], ew_gu(2 * u + a, c),
                                    start=(c == 0), stop=(c == KC - 1))
                        last.then_inc(m["gu_full"], 1)
                        pe.wait_ge(m["y_parts"], n + 1)
                        scatter(1 - u, False)
                        pe.wait_ge(m["hidden"], n + 1)
                        for j in range(JE):
                            last = nc.tensor.transpose(bank[7][:, j * P:(j + 1) * P],
                                                       hslot[:, :].rearrange("p (q j) -> p j q", j=JE)[:, j, :],
                                                       ident[:, :])
                        last.then_inc(m["ht_full"], 1)
                        pe.wait_ge(m["gated"], n + 2)
                        gather(1 - u)
                        pe.wait_ge(m["ht_ready"], n + 1)
                        for a in range(2):
                            pe.wait_ge(m["d_in"][2 * u + a], 16 * g + 16)
                        for half, b, free, full in ((0, 4, "xg_lo", "y_lo_full"), (1, 5, "xg_hi", "y_hi_full")):
                            pe.wait_ge(m[free], n + 2)
                            for j in range(JE):
                                for a in range(2):
                                    last = nc.tensor.matmul(bank[b][a * CAP:(a + 1) * CAP, :],
                                                            hm[:, j, a * CAP:(a + 1) * CAP],
                                                            ew_d(2 * u + a)[:, j, half * 512:(half + 1) * 512],
                                                            start=(j == 0), stop=(j == JE - 1))
                            last.then_inc(m[full], 1)
            pe.wait_ge(m["y_parts"], npass * PAIRS + 1)
            scatter(1, True)

        sh_silu = resid[:, 0, :].rearrange("p (w j t) -> p w j t", w=2, j=JE)[:, 0]
        shid = resid[:, 0, :].rearrange("p (w j t) -> p w j t", w=2, j=JE)[:, 1]

        @block.tensor
        def _(pe):
            pe.wait_ge(S["consts"], N_CONSTS)
            for st in stages:
                if st == "mix0":
                    pe_mix0(pe)
                if st == "mix1":
                    pe_mix1(pe)
                if st.startswith("moe"):
                    pe_moe(pe, int(st[-1]))

        def act_copies(act, B, name, dst):
            act.wait_ge(*B.full(name))
            nc.scalar.copy(dst, B.tile(name)[:, :].rearrange("p (a t) -> p a t", a=2)).then_inc(B.done["a"], 1)

        def act_mix0(act, chain):
            B = B0
            act_copies(act, B, "T0", hT[:, 0:2, :])
            act_copies(act, B, "T2", hT[:, 4:6, :])
            act.wait_ge(*B.read("gates"))
            chain.link(nc.scalar.activation(rows[:, 2, :], rows[:, 1, :], ACT.Abs))
            chain.link(nc.scalar.activation(rows[:, 2, :], rows[:, 2, :], ACT.Exp, scale=-1.0))
            nc.scalar.activation(rows[:, 2, :], rows[:, 2, :], ACT.Ln, bias=1.0).then_inc(M0["splus"], 1)
            act.wait_ge(M0["params"], 80)
            chain.link(nc.scalar.activation(lamb[:, 0, :], cols0[:, 28:32], ACT.Abs))
            nc.scalar.activation(lamb[:, 0, :], lamb[:, 0, :], ACT.Exp, scale=-1.0).then_inc(M0["lam_exp"], 1)
            for i in range(2):
                act_copies(act, B, f"xb{i}", V["xbp"][:, 2 * i:2 * i + 2, 3:SEQ + 3])
            act.wait_ge(M0["rows"], 1)
            nc.scalar.activation(rows[:, 5, :], rows[:, 5, :], ACT.Exp, scale=-1.0).then_inc(M0["em"], 1)
            for name, dst in (("k", V["kT"]), ("q", V["qT"])):
                for i in range(2):
                    act_copies(act, B, f"{name}{i}", dst[:, 2 * i:2 * i + 2, :])
            for name, dst, col in (("r", V["rg"], 20), ("i", V["ig"], 24)):
                for i in range(2):
                    act.wait_ge(*B.full(f"{name}{i}"))
                    for a in range(2):
                        last = nc.scalar.activation(dst[:, 2 * i + a, :], B.tile(f"{name}{i}")[:, a * SEQ:(a + 1) * SEQ],
                                                    ACT.Sigmoid, bias=cols0[:, col + 2 * i + a:col + 2 * i + a + 1])
                    last.then_inc(B.done["a"], 1)
            for t in range(TT):
                act.wait_ge(*B.full(f"v{t}"))
                nc.scalar.copy(V["v1"][:, t, :, 0:DH], B.tile(f"v{t}")[:, :].rearrange("p (h n) -> p h n", h=NH))\
                  .then_inc(B.done["a"], 1)
            for hd in range(NH):
                act.wait_ge(*B.read(f"bc{hd // 2}"))
                nc.scalar.activation(argw[:, hd, :], argw[:, hd, :], ACT.Exp).then_inc(M0["expd"], 1)
            act.wait_ge(M0["log_a"], 1)
            nc.scalar.activation(abuf, V["rg"], ACT.Exp)
            nc.scalar.activation(tbuf, V["rg"], ACT.Tanh).then_inc(M0["a_t"], 1)
            for i in range(2):
                act.wait_ge(*B.full(f"gb{i}"))
                nc.scalar.activation(V["gg"][:, 2 * i:2 * i + 2, :], B.tile(f"gb{i}")[:, :].rearrange("p (a t) -> p a t", a=2),
                                     ACT.Gelu_apprx_tanh).then_inc(B.done["a"], 1)
            act.wait_ge(M0["gain"], 1)
            nc.scalar.activation(tbuf, tbuf, ACT.Sqrt).then_inc(M0["root"], 1)
            for t in range(TT):
                act.wait_ge(*B.full(f"o{t}"))
                nc.scalar.activation(V["og"][:, t, :], B.tile(f"o{t}")[:, :], ACT.Sigmoid).then_inc(B.done["a"], 1)
            act_head_norm(act, M0)
            act_copies(act, B, "yT0", V["mixT"][:, 0:2, :])

        def act_s5_params(act):
            act.wait_ge(M1["cols"], 16)
            nc.scalar.activation(prm[:, 0, :], cols1[:, 32:48], ACT.Exp).then_inc(M1["dt"], 1)
            act.wait_ge(M1["ang"], 1)
            nc.scalar.activation(prm[:, 1, :], prm[:, 1, :], ACT.Exp)
            nc.scalar.activation(prm[:, 4, :], prm[:, 3, :], ACT.Sin, scale=0.5)
            nc.scalar.activation(prm[:, 5, :], prm[:, 3, :], ACT.Sin).then_inc(M1["sine"], 1)

        def act_mix1(act, chain):
            B = B1
            act_copies(act, B, "T0", hT[:, 0:2, :])
            act_copies(act, B, "T2", hT[:, 4:6, :])
            act.wait_ge(*B.full("low"))
            nc.scalar.copy(lowT[:, :], B.tile("low")[0:16, 0:SEQ]).then_inc(B.done["a"], 1)
            for i in range(2):
                act_copies(act, B, f"u{i}", W["uT"][:, 2 * i:2 * i + 2, :])
            for w in range(2):
                act.wait_ge(*B.full(f"bT{w}"))
                nc.scalar.copy(W["bT"][:, w, :, :], B.tile(f"bT{w}")[:, :].rearrange("p (q n) -> p q n", q=4))\
                  .then_inc(B.done["a"], 1)
            act.wait_ge(*B.read("ga"))
            chain.link(nc.scalar.activation(W["e1"], W["la"], ACT.Abs))
            chain.link(nc.scalar.activation(W["e1"], W["e1"], ACT.Exp, scale=-1.0))
            nc.scalar.activation(W["e1"], W["e1"], ACT.Ln, bias=1.0).then_inc(M1["gla_ln"], 1)
            act.wait_ge(M1["gla_last"], 1)
            nc.scalar.activation(W["e1"], W["bc"], ACT.Exp, scale=1.0 / 16)
            nc.scalar.activation(W["e2"], W["bc"], ACT.Exp, scale=-1.0 / 16)
            nc.scalar.activation(W["e3"], W["e3"], ACT.Exp, scale=1.0 / 16).then_inc(M1["decays"], 1)
            for t in range(TT):
                act.wait_ge(*B.full(f"v{t}"))
                nc.scalar.copy(W["v"][:, t, :], B.tile(f"v{t}")[:, :]).then_inc(B.done["a"], 1)
            act.wait_ge(M1["zeros"], 1)
            for hh in range(2):
                act.wait_ge(*B.full(f"att{hh}"))
                for b in range(2):
                    lo, hi = b * LC, (b + 1) * LC
                    src = B.tile(f"att{hh}")[lo:hi, :].rearrange("p (r t s) -> p r t s", r=2, t=TT)
                    for pr in range(2):
                        last = nc.scalar.copy(W["att"][lo:hi, 2 * pr + hh, :, lo:hi], src[:, pr, :, lo:hi])
                last.then_inc(B.done["a"], 1)
            act_copies(act, B, "keT", W["ke_tok"])
            for t in range(TT):
                act.wait_ge(*B.full(f"r{t}"))
                nc.scalar.activation(W["og"][:, t, :], B.tile(f"r{t}")[:, :], ACT.Silu).then_inc(B.done["a"], 1)
                if t == 0:
                    act_head_norm(act, M1)
            for i in range(2):
                act_copies(act, B, f"yT{i}", W["mixT"][:, 4 + 2 * i:6 + 2 * i, :])
            act.wait_ge(*B.read("y1"))
            nc.scalar.activation(W["gT"], W["gT"], ACT.Gelu_apprx_tanh).then_inc(M1["gelu5"], 1)
            for i in range(2):
                act.wait_ge(*B.full(f"gl{i}"))
                for a in range(2):
                    q = 2 * i + a
                    last = nc.scalar.activation(W["mixT"][:, q, :], B.tile(f"gl{i}")[:, a * SEQ:(a + 1) * SEQ], ACT.Sigmoid,
                                                bias=cols1[:, 52 + q:53 + q])
                last.then_inc(B.done["a"], 1)

        def act_head_norm(act, M):
            act.wait_ge(S["consts"], N_CONSTS)
            act.wait_ge(M["hstat"], 1)
            nc.scalar.activation(hrs[:, :, :], hmv[:, :, :, 1], ACT.Sqrt, bias=epsc[:, 0:1]).then_inc(M["hstd"], 1)

        def act_moe(act, l, chain):
            m = MO[l]
            for i, b in enumerate((0, 2)):
                act.wait_ge(m["tA"], 1 + i)
                nc.scalar.copy(hT[:, 2 * b:2 * b + 2, :], bank[4 + b][:, :].rearrange("p (c t) -> p c t", c=2))\
                  .then_inc(m["hT_a"], 1)
            for t in range(TT):
                nc.scalar.copy(h_part[l][0][:, t, :], h[:, t, :]).then_inc(m["top_parts"], 1)
            act.wait_ge(m["scores_psum"], 1)
            nc.scalar.activation(scores[:, :, :], bank[6][:, 0:TT * NE].rearrange("p (t e) -> p t e", t=TT),
                                 ACT.Sigmoid).then_inc(m["scores"], 1)
            for t in range(TT):
                act.wait_ge(m["rest"], t + 1)
                nc.scalar.copy(h_part[l][1][:, t, :], h_rest[t]).then_inc(m["top_parts"], 1)
            act.wait_ge(m["sh_gu"], 1)
            nc.scalar.activation(sh_silu, bank[0][:, :].rearrange("p (j t) -> p j t", j=JE), ACT.Silu)\
              .then_inc(m["sh_silu"], 1)
            act.wait_ge(m["npass"], 1)
            npass = act.value_load(npass_i[0:1, 0:1], min_val=1, max_val=MAX_PASS)

            def gathered(n):
                act.wait_ge(m["gather_lo"], n)
                nc.scalar.copy(xg[:, 0:4, :], bank[4][:, :].rearrange("p (c s) -> p c s", c=4)).then_inc(m["xg_lo"], 1)

            gathered(1)
            with act.Fori(0, npass) as ps:
                with act.Fori(0, NE // NSLOT) as it:
                    for u in range(2):
                        n = ps * PAIRS + it * 2 + u
                        act.wait_ge(m["gu_full"], n + 1)
                        nc.scalar.activation(sg[:, :], bank[6][:, 0:DE], ACT.Silu).then_inc(m["silu"], 1)
                        gathered(n + 2)
                        act.wait_ge(m["y_hi_full"], n + 1)
                        for dst in (ysb[:, 512:1024], y_part[:, 0, 512:1024]):
                            last = nc.scalar.activation(dst, bank[5][:, :], ACT.Copy, scale=slot_gate[:, u:u + 1])
                        last.then_inc(m["y_hi"], 1)

        def act_ln(act, k):
            act.wait_ge(S["consts"], N_CONSTS)
            for t in range(TT):
                act.wait_ge(S["ln_stats"], TT * k + t + 1)
                nc.scalar.activation(rstd[:, t:t + 1], mv[:, t, 1:2], ACT.Sqrt, bias=epsc[:, 0:1])\
                  .then_inc(S["ln_std"], 1)

        @block.scalar
        def _(act):
            chain = Chain(act, S["act_chain"])
            if "mix1" in stages:
                act_s5_params(act)
            for st in stages:
                if st == "mix0":
                    act_mix0(act, chain)
                if st == "mix1":
                    act_mix1(act, chain)
                if st.startswith("moe"):
                    act_moe(act, int(st[-1]), chain)
                act_ln(act, stage_no[st])

        def dve_ln(dve, chain, k, summed):
            ln = LN[k]
            for t in range(TT):
                dve.wait_ge(summed, t + 1)
                for n in range(2):
                    last = nc.vector.scalar_tensor_tensor(out=resid[:, t, n * 512:(n + 1) * 512],
                                                          in0=h[:, t, n * 512:(n + 1) * 512], scalar=ALPHA,
                                                          in1=bank[2 * t + n][:, :], op0=ALU.mult, op1=ALU.add)
                chain.link(last)
                for n in range(2):
                    last = nc.vector.bn_stats(stats[:, t, n, :], resid[:, t, n * 512:(n + 1) * 512])
                chain.link(last)
                nc.vector.bn_aggr(mv[:, t, :], stats[:, t, :, :]).then_inc(S["ln_stats"], 1)
                dve.wait_ge(S["ln_stats"], TT * k + t + 1)
                dve.wait_ge(ln["params"], 32)
                nc.vector.scalar_tensor_tensor(out=resid[:, t, :], in0=resid[:, t, :], scalar=mv[:, t, 0:1],
                                               in1=lnw[:, :], op0=ALU.subtract, op1=ALU.mult)
                dve.wait_ge(S["ln_std"], TT * k + t + 1)
                chain.link(nc.vector.reciprocal(rstd[:, t:t + 1], rstd[:, t:t + 1]))
                nc.vector.scalar_tensor_tensor(out=h[:, t, :], in0=resid[:, t, :], scalar=rstd[:, t:t + 1],
                                               in1=lnb[:, :], op0=ALU.mult, op1=ALU.add).then_inc(S["h_ready"], 1)

        def dve_copies(dve, B, name, dst):
            dve.wait_ge(*B.full(name))
            nc.vector.tensor_copy(dst, B.tile(name)[:, :].rearrange("p (a t) -> p a t", a=2)).then_inc(B.done["d"], 1)

        def dve_mix0(dve, chain):
            B = B0
            for i, row in enumerate((1, 3)):
                dve_copies(dve, B, f"T{row}", hT[:, 2 * row:2 * row + 2, :])
            nc.vector.memset(V["xbp"][:, :, 0:3], 0.0)
            chain.link(nc.vector.memset(V["v1"][:, :, :, DH:DH + 1], 1.0))
            dve.wait_ge(M0["params"], 80)
            dve.wait_ge(*B.full("gates"))
            nc.vector.tensor_scalar(rows[:, 0, :], B.tile("gates")[0:NH, 0:SEQ], cols0[0:NH, 32:33], None, ALU.add)
            nc.vector.tensor_scalar(rows[:, 1, :], B.tile("gates")[0:NH, SEQ:2 * SEQ], cols0[0:NH, 33:34], None, ALU.add)\
              .then_inc(B.done["d"], 1)
            dve.wait_ge(*B.read("gates"))
            dve.wait_ge(M0["splus"], 1)
            chain.link(nc.vector.scalar_tensor_tensor(out=rows[:, 1, :], in0=rows[:, 1, :], scalar=0.0,
                                                      in1=rows[:, 2, :], op0=ALU.min, op1=ALU.subtract))
            one = ones[0:NH, 0:1].broadcast_to([NH, SEQ])
            chain.link(nc.vector.tensor_tensor_scan(rows[:, 3, :], one, rows[:, 1, :], 0.0, ALU.mult, ALU.add))
            chain.link(nc.vector.tensor_tensor(rows[:, 0, :], rows[:, 0, :], rows[:, 3, :], ALU.subtract))
            chain.link(nc.vector.tensor_tensor_scan(rows[:, 4, :], one, rows[:, 0, :], 0.0, ALU.mult, ALU.max))
            chain.link(nc.vector.tensor_tensor(rows[:, 5, :], rows[:, 3, :], rows[:, 4, :], ALU.add))
            nc.vector.tensor_scalar(rows[:, 4, :], rows[:, 4, :], -1.0, None, ALU.mult).then_inc(M0["rows"], 1)
            dve.wait_ge(M0["lam_exp"], 1)
            L = lamb
            chain.link(nc.vector.tensor_scalar(L[:, 1, :], L[:, 0, :], 2.0, None, ALU.add))
            chain.link(nc.vector.reciprocal(L[:, 1, :], L[:, 1, :]))
            chain.link(nc.vector.tensor_tensor(L[:, 1, :], L[:, 0, :], L[:, 1, :], ALU.mult))
            chain.link(nc.vector.tensor_tensor(L[:, 2, :], L[:, 1, :], L[:, 1, :], ALU.mult))
            terms = [1.0 / (2 * q + 1) for q in range(9)]
            chain.link(nc.vector.tensor_scalar(L[:, 3, :], L[:, 2, :], terms[8], terms[7], ALU.mult, ALU.add))
            for q in range(6, -1, -1):
                chain.link(nc.vector.tensor_tensor(L[:, 3, :], L[:, 3, :], L[:, 2, :], ALU.mult))
                chain.link(nc.vector.tensor_scalar(L[:, 3, :], L[:, 3, :], terms[q], None, ALU.add))
            chain.link(nc.vector.scalar_tensor_tensor(out=L[:, 3, :], in0=L[:, 3, :], scalar=2.0, in1=L[:, 1, :],
                                                      op0=ALU.mult, op1=ALU.mult))
            chain.link(nc.vector.scalar_tensor_tensor(out=L[:, 4, :], in0=cols0[:, 28:32], scalar=0.0, in1=L[:, 3, :],
                                                      op0=ALU.min, op1=ALU.subtract))
            chain.link(nc.vector.tensor_scalar(L[:, 4, :], L[:, 4, :], 8.0, None, ALU.mult))
            dve.wait_ge(*B.read("xb1"))
            for hd in range(NH):
                last = nc.vector.tensor_scalar(V["xc"][:, hd, :], V["xbp"][:, hd, 0:SEQ], cols0[:, hd:hd + 1],
                                               cols0[:, 16 + hd:17 + hd], ALU.mult, ALU.add)
            for tap in range(1, 4):
                chain.link(last)
                for hd in range(NH):
                    last = nc.vector.scalar_tensor_tensor(out=V["xc"][:, hd, :], in0=V["xbp"][:, hd, tap:tap + SEQ],
                                                          scalar=cols0[:, 4 * tap + hd:4 * tap + hd + 1],
                                                          in1=V["xc"][:, hd, :], op0=ALU.mult, op1=ALU.add)
            last.then_inc(M0["xc"], 1)
            dve.wait_ge(*B.full("cols"))
            nc.vector.tensor_copy(gcol[:, :, :, :], B.tile("cols")[:, 0:16].rearrange("p (i t h) -> p i t h", i=2, t=TT))\
              .then_inc(B.done["d"], 1)
            dve.wait_ge(*B.read("cols"))
            for hd in range(NH):
                name, off = f"bc{hd // 2}", (hd % 2) * SEQ
                if hd % 2 == 0:
                    dve.wait_ge(*B.full(name))
                nc.vector.scalar_tensor_tensor(out=argw[:, hd, 0:SEQ], in0=B.tile(name)[:, off:off + SEQ],
                                               scalar=gcol[:, 0, 0, hd:hd + 1], in1=maskc[:, :],
                                               op0=ALU.add, op1=ALU.min)
                last = nc.vector.scalar_tensor_tensor(out=argw[:, hd, SEQ:SEQ + P],
                                                      in0=B.tile(name)[:, off + P:off + SEQ],
                                                      scalar=gcol[:, 0, 1, hd:hd + 1], in1=maskc[:, 0:P],
                                                      op0=ALU.add, op1=ALU.min)
                if hd % 2 == 1:
                    last.then_inc(B.done["d"], 1)
            dve.wait_ge(*B.read("r1"))
            nc.vector.tensor_tensor(V["rg"], V["rg"], L[:, 4, :].unsqueeze(2).broadcast_to([P, NH, SEQ]), ALU.mult)\
              .then_inc(M0["log_a"], 1)
            for hd in range(NH):
                dve.wait_ge(*B.full(f"S{hd}"))
                dve.wait_ge(M0["expd"], hd + 1)
                nc.vector.scalar_tensor_tensor(out=argw[:, hd, :], in0=B.tile(f"S{hd}")[:, 0:SEQ + P],
                                               scalar=DH ** -0.5, in1=argw[:, hd, :], op0=ALU.mult, op1=ALU.mult)\
                  .then_inc(B.done["d"], 1)
            dve.wait_ge(M0["a_t"], 1)
            chain.link(nc.vector.tensor_scalar(V["rg"], tbuf, -1.0, 1.0, ALU.mult, ALU.add))
            chain.link(nc.vector.reciprocal(V["rg"], V["rg"]))
            nc.vector.scalar_tensor_tensor(out=tbuf, in0=tbuf, scalar=-2.0, in1=V["rg"], op0=ALU.mult, op1=ALU.mult)\
              .then_inc(M0["gain"], 1)
            dve.wait_ge(*B.read("i1"))
            chain.link(nc.vector.tensor_tensor(V["ig"], V["ig"], V["xc"], ALU.mult))
            dve.wait_ge(M0["root"], 1)
            chain.link(nc.vector.tensor_tensor(V["ig"], V["ig"], tbuf, ALU.mult))
            for hd in range(NH):
                last = nc.vector.tensor_tensor_scan(V["xc"][:, hd, :], abuf[:, hd, :], V["ig"][:, hd, :], 0.0,
                                                    ALU.mult, ALU.add)
            chain.link(last)
            dve.wait_ge(*B.read("gb1"))
            nc.vector.tensor_tensor(V["mixT"][:, 4:8, :], V["xc"], V["gg"], ALU.mult).then_inc(M0["y_lru"], 1)
            for hd in range(NH):
                dve.wait_ge(*B.full(f"N{hd}"))
                acc = B.tile(f"N{hd}")
                den = acc[:, :].rearrange("p (t n) -> p t n", t=TT)[:, :, DH]
                chain.link(nc.vector.tensor_copy(rden[:, hd, :], den))
                chain.link(nc.vector.scalar_tensor_tensor(out=rden[:, hd, :], in0=rden[:, hd, :], scalar=-1.0,
                                                          in1=rden[:, hd, :], op0=ALU.mult, op1=ALU.max))
                chain.link(nc.vector.tensor_tensor(rden[:, hd, :], rden[:, hd, :], gcol[:, 1, :, hd], ALU.max))
                chain.link(nc.vector.reciprocal(rden[:, hd, :], rden[:, hd, :]))
                for t in range(TT):
                    last = nc.vector.tensor_scalar(hbuf[:, t, hd * DH:(hd + 1) * DH], acc[:, t * SEQ:t * SEQ + DH],
                                                   rden[:, hd, t:t + 1], None, ALU.mult)
                last.then_inc(B.done["d"], 1)
            dve.wait_ge(*B.read("N3"))
            dve_head_norm(dve, chain, M0, True)
            dve.wait_ge(*B.read("o1"))
            for t in range(TT):
                last = nc.vector.tensor_tensor(hbuf[:, t, :], hbuf[:, t, :], V["og"][:, t, :], ALU.mult)
            last.then_inc(M0["yhead"], 1)
            dve_copies(dve, B, "yT1", V["mixT"][:, 2:4, :])

        def dve_s5_params(dve, chain):
            p = prm
            lr, li = cols1[:, 0:16], cols1[:, 16:32]
            dve.wait_ge(M1["cols"], 16)
            dve.wait_ge(M1["dt"], 1)
            nc.vector.tensor_tensor(p[:, 1, :], lr, p[:, 0, :], ALU.mult)
            chain.link(nc.vector.tensor_tensor(p[:, 2, :], li, p[:, 0, :], ALU.mult))
            magic, turn = 1.5 * 2.0 ** 23, 2.0 * np.pi
            c1 = 6.28125
            c2 = float(np.float32(round((turn - c1) * 2 ** 20) / 2 ** 20))
            c3 = turn - c1 - c2
            chain.link(nc.vector.tensor_scalar(p[:, 3, :], p[:, 2, :], 1.0 / turn, magic, ALU.mult, ALU.add))
            chain.link(nc.vector.tensor_scalar(p[:, 3, :], p[:, 3, :], magic, None, ALU.subtract))
            for part in (c1, c2, c3):
                chain.link(nc.vector.scalar_tensor_tensor(out=p[:, 2, :], in0=p[:, 3, :], scalar=-part, in1=p[:, 2, :],
                                                          op0=ALU.mult, op1=ALU.add))
            nc.vector.tensor_scalar(p[:, 3, :], p[:, 2, :], 3.1415925, -3.1415925, ALU.min, ALU.max)\
              .then_inc(M1["ang"], 1)
            dve.wait_ge(M1["sine"], 1)
            chain.link(nc.vector.tensor_tensor(p[:, 4, :], p[:, 4, :], p[:, 4, :], ALU.mult))
            chain.link(nc.vector.tensor_scalar(p[:, 4, :], p[:, 4, :], -2.0, 1.0, ALU.mult, ALU.add))
            nc.vector.tensor_tensor(p[:, 6, :], p[:, 1, :], p[:, 4, :], ALU.mult)
            nc.vector.tensor_tensor(p[:, 7, :], p[:, 1, :], p[:, 5, :], ALU.mult)
            nc.vector.tensor_tensor(p[:, 10, :], lr, lr, ALU.mult)
            chain.link(nc.vector.tensor_tensor(p[:, 11, :], li, li, ALU.mult))
            nc.vector.tensor_tensor(p[:, 10, :], p[:, 10, :], p[:, 11, :], ALU.add)
            chain.link(nc.vector.tensor_scalar(p[:, 6, :], p[:, 6, :], 1.0, None, ALU.subtract))
            nc.vector.reciprocal(p[:, 10, :], p[:, 10, :])
            nc.vector.tensor_tensor(p[:, 8, :], p[:, 6, :], lr, ALU.mult)
            nc.vector.tensor_tensor(p[:, 11, :], p[:, 7, :], li, ALU.mult)
            nc.vector.tensor_tensor(p[:, 9, :], p[:, 7, :], lr, ALU.mult)
            chain.link(nc.vector.tensor_tensor(p[:, 12, :], p[:, 6, :], li, ALU.mult))
            nc.vector.tensor_tensor(p[:, 8, :], p[:, 8, :], p[:, 11, :], ALU.add)
            chain.link(nc.vector.tensor_tensor(p[:, 9, :], p[:, 9, :], p[:, 12, :], ALU.subtract))
            nc.vector.tensor_tensor(p[:, 8, :], p[:, 8, :], p[:, 10, :], ALU.mult)
            nc.vector.tensor_tensor(p[:, 9, :], p[:, 9, :], p[:, 10, :], ALU.mult).then_inc(M1["coef"], 1)

        def dve_mix1(dve, chain):
            B = B1
            wait_h(dve, "mix1")
            nc.vector.tensor_copy(W["cos"][:, :, 0], prm[:, 4, :]).then_inc(M1["step_re"], 1)
            nc.vector.tensor_copy(W["sin"][:, :, 0], prm[:, 5, :]).then_inc(M1["step_im"], 1)
            for row in (1, 3):
                dve_copies(dve, B, f"T{row}", hT[:, 2 * row:2 * row + 2, :])
            dve.wait_ge(M1["cols"], 32)
            nc.vector.tensor_scalar(W["craw"][:, 1], W["craw"][:, 1], -1.0, None, ALU.mult).then_inc(M1["cneg"], 1)
            for k in range(N_STEPS):
                n = 1 << k
                dve.wait_ge(M1["step_re"], k + 1)
                dve.wait_ge(M1["step_im"], k + 1)
                new = W["sin"][:, :, n:2 * n]
                tmp = W["x"].rearrange("p a b t -> p (a b t)")[:, 0:NT * n].rearrange("p (i t) -> p i t", i=NT)
                cr = W["cos"][:, :, n - 1:n].broadcast_to([P, NT, n])
                ci = W["sin"][:, :, n - 1:n].broadcast_to([P, NT, n])
                nc.vector.tensor_tensor(new, W["sin"][:, :, 0:n], cr, ALU.mult)
                chain.link(nc.vector.tensor_tensor(tmp, W["cos"][:, :, 0:n], ci, ALU.mult))
                nc.vector.tensor_tensor(new, new, tmp, ALU.add).then_inc(M1["step_im"], 1)
            dve.wait_ge(*B.full("ga"))
            for a in range(2):
                last = nc.vector.tensor_scalar(W["la"][:, a, :], B.tile("ga")[:, a * SEQ:(a + 1) * SEQ],
                                               cols1[:, 56 + a:57 + a], None, ALU.add)
            last.then_inc(B.done["d"], 1)
            dve.wait_ge(*B.read("ga"))
            dve.wait_ge(M1["gla_ln"], 1)
            chain.link(nc.vector.scalar_tensor_tensor(out=W["la"], in0=W["la"], scalar=0.0, in1=W["e1"],
                                                      op0=ALU.min, op1=ALU.subtract))
            dve.wait_ge(M1["zeros"], 1)
            for a in range(2):
                last = nc.vector.tensor_tensor_scan(W["bc"][:, a, :], restart[:, :], W["la"][:, a, :], 0.0, ALU.mult, ALU.add)
            chain.link(last)
            by_chunk = W["bc"].rearrange("p a (c s) -> p (a c) s", s=LC)
            nc.vector.tensor_tensor(W["e3"].rearrange("p a (c s) -> p (a c) s", s=LC),
                                    by_chunk[:, :, LC - 1:LC].broadcast_to([P, 2 * SEQ // LC, LC]), by_chunk,
                                    ALU.subtract).then_inc(M1["gla_last"], 1)
            dve.wait_ge(M1["step_re"], N_STEPS + 1)
            dve.wait_ge(M1["step_im"], N_STEPS + 1)

            def scan_tile(i):
                q = i % 4
                dve.wait_ge(*B.full(f"bu{i}"))
                if i == 0:
                    dve.wait_ge(*B.read("bT1"))
                if i >= 4:
                    dve.wait_ge(M1["x"], i - 3)
                bu = B.tile(f"bu{i}")[:, :].rearrange("p (w t) -> p w t", w=2)
                c = W["cos"][:, i, :].unsqueeze(1).broadcast_to([P, 2, SEQ])
                sn = W["sin"][:, i, :].unsqueeze(1).broadcast_to([P, 2, SEQ])
                nc.vector.tensor_tensor(W["m1"], bu, c, ALU.mult)
                nc.vector.tensor_tensor(W["m2"], bu, sn, ALU.mult).then_inc(B.done["d"], 1)
                dve.wait_ge(*B.read(f"bu{i}"))
                nc.vector.tensor_tensor(zin[:, 0, :], W["m1"][:, 0, :], W["m2"][:, 1, :], ALU.add)
                chain.link(nc.vector.tensor_tensor(zin[:, 1, :], W["m1"][:, 1, :], W["m2"][:, 0, :], ALU.subtract))
                mag = prm[:, 1, i:i + 1].broadcast_to([P, SEQ])
                for w in range(2):
                    last = nc.vector.tensor_tensor_scan(W["z"][:, q, w, :], mag, zin[:, w, :], 0.0, ALU.mult, ALU.add)
                last.then_inc(M1["z"], 1)

            for i in range(4):
                scan_tile(i)
            dve.wait_ge(M1["decays"], 1)
            dve.wait_ge(*B.full("qk1"))
            k_ps = B.tile("qk1")[:, :].rearrange("p (a t) -> p a t", a=2)
            nc.vector.scalar_tensor_tensor(out=W["qd"], in0=B.tile("qk0")[:, :].rearrange("p (a t) -> p a t", a=2),
                                           scalar=DK ** -0.5, in1=W["e1"], op0=ALU.mult, op1=ALU.mult)\
              .then_inc(B.done["d"], 1)
            nc.vector.tensor_tensor(W["ki"], k_ps, W["e2"], ALU.mult).then_inc(M1["ki"], 1)
            nc.vector.tensor_tensor(W["ke"], k_ps, W["e3"], ALU.mult).then_inc(B.done["d"], 1)
            for i in range(4, 13):
                scan_tile(i)
            dve.wait_ge(M1["zeros"], 1)
            for c in range(3):
                dve.wait_ge(*B.full(f"U{c}"))
                for hd in range(NH):
                    lo = (hd % 2) * DK
                    new = W["state"][lo:lo + DK, c, hd, :]
                    add = B.tile(f"U{c}")[lo:lo + DK, hd * P:(hd + 1) * P]
                    if c == 0:
                        last = nc.vector.tensor_copy(new, add)
                    else:
                        end = c * LC + LC - 1
                        last = nc.vector.scalar_tensor_tensor(out=new, in0=W["state"][lo:lo + DK, c - 1, hd, :],
                                                              scalar=W["e1"][lo:lo + DK, hd // 2, end:end + 1], in1=add,
                                                              op0=ALU.mult, op1=ALU.add)
                last.then_inc(B.done["d"], 1)
                dve.wait_ge(*B.read(f"U{c}"))
            for i in range(13, 16):
                scan_tile(i)
            for t in range(TT):
                dve.wait_ge(*B.full(f"o{t}"))
                nc.vector.tensor_copy(hbuf[:, t, :], B.tile(f"o{t}")[:, :]).then_inc(B.done["d"], 1)
            dve.wait_ge(*B.read("o1"))
            dve_head_norm(dve, chain, M1, False)
            for t in range(TT):
                dve.wait_ge(*B.read(f"r{t}"))
                last = nc.vector.tensor_tensor(hbuf[:, t, :], hbuf[:, t, :], W["og"][:, t, :], ALU.mult)
            last.then_inc(M1["yhead"], 1)
            dve.wait_ge(*B.full("y1"))
            for q in range(4):
                last = nc.vector.scalar_tensor_tensor(out=W["gT"][:, q, :], in0=W["uT"][:, q, :], scalar=cols1[:, 48 + q:49 + q],
                                                      in1=B.tile(f"y{q // 2}")[:, (q % 2) * SEQ:(q % 2 + 1) * SEQ],
                                                      op0=ALU.mult, op1=ALU.add)
                if q % 2:
                    last.then_inc(B.done["d"], 1)
            dve.wait_ge(*B.read("gl1"))
            nc.vector.tensor_tensor(W["mixT"][:, 0:4, :], W["mixT"][:, 0:4, :], W["gT"], ALU.mult).then_inc(M1["y_s5"], 1)

        def dve_head_norm(dve, chain, M, center):
            for t in range(TT):
                for hd in range(NH):
                    last = nc.vector.bn_stats(hstat[:, t, hd, :], hbuf[:, t, hd * DH:(hd + 1) * DH])
            chain.link(last)
            for t in range(TT):
                for hd in range(NH):
                    last = nc.vector.bn_aggr(hmv[:, t, hd, :], hstat[:, t, hd, :])
            if not center:
                chain.link(last)
                chain.link(nc.vector.tensor_tensor(hrs[:, :, :], hmv[:, :, :, 0], hmv[:, :, :, 0], ALU.mult))
                last = nc.vector.tensor_tensor(hmv[:, :, :, 1], hmv[:, :, :, 1], hrs[:, :, :], ALU.add)
            last.then_inc(M["hstat"], 1)
            dve.wait_ge(M["hstd"], 1)
            chain.link(nc.vector.reciprocal(hrs[:, :, :], hrs[:, :, :]))
            for t in range(TT):
                for hd in range(NH):
                    part = hbuf[:, t, hd * DH:(hd + 1) * DH]
                    if center:
                        last = nc.vector.tensor_scalar(part, part, hmv[:, t, hd, 0:1], hrs[:, t, hd:hd + 1],
                                                       ALU.subtract, ALU.mult)
                    else:
                        last = nc.vector.tensor_scalar(part, part, hrs[:, t, hd:hd + 1], None, ALU.mult)
            chain.link(last)
            for t in range(TT):
                last = nc.vector.tensor_tensor(hbuf[:, t, :], hbuf[:, t, :], normw, ALU.mult)
            chain.link(last)

        def dve_route(dve, l, chain):
            m = MO[l]
            dve.wait_ge(m["scores"], 1)
            dve.wait_ge(m["router_in"], 32)
            chain.link(nc.vector.tensor_tensor(biased[:, :, :], scores[:, :, :],
                                               rbias[:, :].unsqueeze(1).broadcast_to([P, TT, NE]), ALU.add))
            for t in range(TT):
                for g in range(NG):
                    last = nc.vector.max(top8[:, t, g, :], biased[:, t, g * 8:(g + 1) * 8])
            chain.link(last)
            chain.link(nc.vector.tensor_tensor(grp[:, :, :], top8[:, :, :, 0], top8[:, :, :, 1], ALU.add))
            for t in range(TT):
                other = grp[:, t, :].unsqueeze(1).broadcast_to([P, NG, NG])
                own = grp[:, t, :].unsqueeze(2).broadcast_to([P, NG, NG])
                nc.vector.tensor_tensor(gcmp[:, t, :, :], other, own, ALU.is_gt)
                last = nc.vector.tensor_tensor(gcmp2[:, t, :, :], other, own, ALU.is_equal)
            chain.link(last)
            for t in range(TT):
                last = nc.vector.tensor_tensor(gcmp2[:, t, :, :], gcmp2[:, t, :, :], gmask[:, :, :], ALU.mult)
            chain.link(last)
            for t in range(TT):
                last = nc.vector.tensor_tensor(gcmp[:, t, :, :], gcmp[:, t, :, :], gcmp2[:, t, :, :], ALU.add)
            chain.link(last)
            chain.link(nc.vector.tensor_reduce(grank[:, :, :], gcmp[:, :, :, :], AX.X, ALU.add))
            chain.link(nc.vector.tensor_scalar(grank[:, :, :], grank[:, :, :], TOPK_GROUPS - 0.5, -BIG,
                                               ALU.is_gt, ALU.mult))
            for t in range(TT):
                last = nc.vector.tensor_tensor(masked[:, t, :].rearrange("p (g e) -> p g e", g=NG),
                                               biased[:, t, :].rearrange("p (g e) -> p g e", g=NG),
                                               grank[:, t, :].unsqueeze(2).broadcast_to([P, NG, NE // NG]), ALU.add)
            chain.link(last)
            for t in range(TT):
                last = nc.vector.max(best[:, t, :], masked[:, t, :])
            chain.link(last)
            for t in range(TT):
                last = nc.vector.match_replace(replaced[:, t, :], best[:, t, :], masked[:, t, :], -3.0 * BIG)
            chain.link(last)
            nc.vector.tensor_tensor(chosen[:, :, :], replaced[:, :, :], masked[:, :, :], ALU.not_equal)\
              .then_inc(m["chosen"], 1)
            dve.wait_ge(m["chosen"], 1)
            chain.link(nc.vector.tensor_tensor(wts[:, :, :], chosen[:, :, :], scores[:, :, :], ALU.mult))
            chain.link(nc.vector.tensor_reduce(wsum[:, :], wts[:, :, :], AX.X, ALU.add))
            chain.link(nc.vector.reciprocal(wsum[:, :], wsum[:, :]))
            for t in range(TT):
                last = nc.vector.tensor_scalar(cw[:, t, 0:NE], wts[:, t, :], wsum[:, t:t + 1], ROUTED_SCALE,
                                               ALU.mult, ALU.mult)
            chain.link(last)
            chain.link(nc.vector.tensor_copy(cw[:, :, NE:NE + 2], cw[:, :, 0:2]))
            for t in range(TT):
                dve.wait_ge(m["top_parts"], TT + t + 1)
                last = nc.vector.tensor_tensor(h_part[l][2][:, t, :], h_rest[t], h_part[l][1][:, t, :], ALU.subtract)
                last.then_inc(m["low_part"], 1)
            dve.wait_ge(m["low_part"], TT)
            dve.wait_ge(m["rank_psum"], 1)
            chain.link(nc.vector.tensor_reduce(cnt[0:1, 0:1], bank[7][0:1, 2 * NE:3 * NE], AX.X, ALU.max))
            for i in range(1, MAX_PASS):
                last = nc.vector.tensor_scalar(cnt[0:1, i:i + 1], cnt[0:1, 0:1], CAP * i + 0.5, None, ALU.is_gt)
            chain.link(last)
            chain.link(nc.vector.tensor_reduce(cnt[0:1, MAX_PASS:MAX_PASS + 1], cnt[0:1, 1:MAX_PASS], AX.X, ALU.add))
            nc.vector.tensor_scalar(npass_i[0:1, 0:1], cnt[0:1, MAX_PASS:MAX_PASS + 1], 1.0, None, ALU.add)\
              .then_inc(m["npass"], 1)
            for t in range(TT):
                last = nc.vector.scalar_tensor_tensor(out=rank[:, t, 0:NE], in0=bank[7][:, t * NE:(t + 1) * NE],
                                                      scalar=1.0, in1=chosen[:, t, :], op0=ALU.add, op1=ALU.mult)
            chain.link(last)
            chain.link(nc.vector.tensor_scalar(rank[:, :, 0:NE], rank[:, :, 0:NE], 1.0, None, ALU.subtract))
            chain.link(nc.vector.tensor_scalar(rank[:, :, NE:NE + 2], rank[:, :, 0:2], float(CAP), None, ALU.subtract))

        def dve_moe(dve, l, chain):
            m = MO[l]
            for i, b in enumerate((1, 3)):
                dve.wait_ge(m["tD"], 1 + i)
                nc.vector.tensor_copy(hT[:, 2 * b:2 * b + 2, :], bank[4 + b][:, :].rearrange("p (c t) -> p c t", c=2))\
                  .then_inc(m["hT_d"], 1)
            dve_route(dve, l, chain)
            nc.vector.memset(onehotT[:, 1, :, :], 0.0).then_inc(m["pt_ready"], 1)
            nc.vector.memset(y_part, 0.0).then_inc(m["y_parts"], 1)
            dve.wait_ge(m["npass"], 1)
            npass = dve.value_load(npass_i[0:1, 0:1], min_val=1, max_val=MAX_PASS)
            slots = iota[:, :].unsqueeze(1).unsqueeze(1).broadcast_to([P, TT, 2, CAP])

            def select(par, e, n):
                nc.vector.tensor_tensor(onehot[:, par, :, :, :], slots,
                                        rank[:, :, bass.ds(e, 2)].unsqueeze(3).broadcast_to([P, TT, 2, CAP]),
                                        ALU.is_equal).then_inc(m["onehot"], 1)
                dve.wait_ge(m["onehot"], n)
                nc.vector.tensor_tensor(gated[:, par, :, :, :], onehot[:, par, :, :, :],
                                        cw[:, :, bass.ds(e, 2)].unsqueeze(3).broadcast_to([P, TT, 2, CAP]),
                                        ALU.mult).then_inc(m["gated"], 1)

            def gathered(par, n):
                dve.wait_ge(m["pt_full"], n)
                nc.vector.tensor_reduce(slot_gate[:, par:par + 1], bank[6][:, 0:TT * P], AX.X, ALU.add)
                nc.vector.tensor_scalar(onehotT[:, par, :, :], bank[6][:, 0:TT * P].rearrange("p (t s) -> p t s", t=TT),
                                        0.0, None, ALU.not_equal).then_inc(m["pt_ready"], 1)
                dve.wait_ge(m["gather_hi"], n)
                nc.vector.tensor_copy(xg[:, 4:8, :], bank[5][:, :].rearrange("p (c s) -> p c s", c=4))\
                  .then_inc(m["xg_hi"], 1)

            select(0, 0, 1)
            dve.wait_ge(m["sh_silu"], 1)
            dve.wait_ge(m["sh_gu"], 2)
            nc.vector.tensor_tensor(shid, sh_silu, bank[1][:, :].rearrange("p (j t) -> p j t", j=JE), ALU.mult)\
              .then_inc(m["sh_hidden"], 1)
            gathered(0, 1)
            with dve.Fori(0, npass) as ps:
                with dve.Fori(0, NE // NSLOT) as it:
                    for u in range(2):
                        n = ps * PAIRS + it * 2 + u
                        select(1 - u, it * NSLOT + 2 * u + 2, n + 2)
                        dve.wait_ge(m["silu"], n + 1)
                        nc.vector.tensor_tensor(hslot[:, :], sg[:, :], bank[6][:, DE:2 * DE], ALU.mult)\
                          .then_inc(m["hidden"], 1)
                        dve.wait_ge(m["ht_full"], n + 1)
                        nc.vector.tensor_copy(hm[:, :, :], bank[7][:, 0:JE * P].rearrange("p (j s) -> p j s", j=JE))\
                          .then_inc(m["ht_ready"], 1)
                        gathered(1 - u, n + 2)
                        dve.wait_ge(m["y_lo_full"], n + 1)
                        for dst in (ysb[:, 0:512], y_part[:, 0, 0:512]):
                            last = nc.vector.tensor_scalar(dst, bank[4][:, :], slot_gate[:, u:u + 1], None, ALU.mult)
                        last.then_inc(m["y_lo"], 1)
                        dve.wait_ge(m["y_lo"], n + 1)
                        dve.wait_ge(m["y_hi"], n + 1)
                        nc.vector.tensor_tensor(ysb[:, :], ysb[:, :], y_part[:, 0, :], ALU.subtract)\
                          .then_inc(m["y_rest"], 1)
                        dve.wait_ge(m["y_rest"], 2 * n + 1)
                        nc.vector.tensor_copy(y_part[:, 1, :], ysb[:, :]).then_inc(m["y_rest"], 1)
                        dve.wait_ge(m["y_rest"], 2 * n + 2)
                        nc.vector.tensor_tensor(y_part[:, 2, :], ysb[:, :], y_part[:, 1, :], ALU.subtract)\
                          .then_inc(m["y_parts"], 1)
                nc.vector.tensor_scalar(rank[:, :, :], rank[:, :, :], float(CAP), None, ALU.subtract)\
                  .then_inc(m["rank_next"], 1)
                dve.wait_ge(m["rank_next"], ps + 1)

        @block.vector
        def _(dve):
            chain = Chain(dve, S["dve_chain"])
            if "mix1" in stages:
                dve_s5_params(dve, chain)
            dve.wait_ge(S["consts"], N_CONSTS)
            for st in stages:
                if st == "mix0":
                    dve_mix0(dve, chain)
                if st == "mix1":
                    dve_mix1(dve, chain)
                if st.startswith("moe"):
                    dve_moe(dve, int(st[-1]), chain)
                dve_ln(dve, chain, stage_no[st], {"mix0": M0["out_full"], "mix1": M1["out_full"],
                                                  "moe0": MO[0]["acc_full"], "moe1": MO[1]["acc_full"]}[st])


_INS = ["x", "ln1_w", "ln1_b", "ln2_w", "ln2_b", "w_out", "w_in_even", "w_in_odd", "mlstm_norm_w", "gla_norm_w",
        "lru_wa", "lru_wx", "s5_glu_w", "gla_gate_w", "router_w", "router_bias",
        "exp_w_gate", "exp_w_up", "exp_w_down", "sh_w_gate", "sh_w_up", "sh_w_down"]
STAGES = ("mix0", "moe0", "mix1", "moe1")


def packed(inputs):
    def chans(a):
        a = np.asarray(a)
        return a.reshape(-1, P).T

    even = np.zeros((P, 34), np.float32)
    even[:, 0:16] = np.concatenate([chans(np.asarray(inputs["lru_conv_w"])[0, k]) for k in range(4)], axis=1)
    even[:, 16:20] = chans(inputs["lru_conv_b"])
    even[:, 20:24] = chans(inputs["lru_ba"])
    even[:, 24:28] = chans(inputs["lru_bx"])
    even[:, 28:32] = chans(inputs["lru_lambda"])
    even[0:4, 32:34] = np.asarray(inputs["mlstm_gate_b"])[0].reshape(2, 4).T

    odd = np.zeros((P, 58), np.float32)
    odd[:, 0:16] = np.asarray(inputs["s5_lam_re"]).reshape(NT, P).T
    odd[:, 16:32] = np.asarray(inputs["s5_lam_im"]).reshape(NT, P).T
    odd[:, 32:48] = np.repeat(np.asarray(inputs["s5_log_dt"]).reshape(-1), 64).reshape(NT, P).T
    odd[:, 48:52] = chans(inputs["s5_d"])
    odd[:, 52:56] = chans(inputs["s5_glu_b"])
    odd[:, 56:58] = chans(inputs["gla_gate_b"])

    def by_state(re, im):
        m = np.zeros((P, 2, NT, 32), np.float32)
        for w, a in enumerate((re, im)):
            a = a.reshape(NT, 2, 64, 16)
            for g in range(2):
                m[g * 64:(g + 1) * 64, w, :, g * 16:(g + 1) * 16] = a[:, g].transpose(1, 0, 2)
        return m.reshape(P, -1)

    b = by_state(np.asarray(inputs["s5_b_re"])[0], np.asarray(inputs["s5_b_im"])[0])
    c = by_state(np.asarray(inputs["s5_c_re"])[0].transpose(0, 2, 1), np.asarray(inputs["s5_c_im"])[0].transpose(0, 2, 1))
    return {"cols_even": even, "cols_odd": odd, "b_odd": b, "c_odd": c}


def kernel(**inputs):
    import concourse.bacc as _bacc
    from concourse.bass_utils import run_bass_kernel_spmd as _run

    nc = _bacc.Bacc("TRN2", target_bir_lowering=False, num_devices=1)
    arrays, A = {}, {}
    given = {n: np.ascontiguousarray(inputs[n]) for n in _INS}
    given.update(packed(inputs))
    for name, a in given.items():
        arrays[f"in_{name}"] = a
        A[name] = nc.dram_tensor(f"in_{name}", a.shape, mybir.dt.from_np(a.dtype), kind="ExternalInput").ap()
    out = nc.dram_tensor("out_0", (1, SEQ, D), F32, kind="ExternalOutput").ap()
    build(nc, A, out, STAGES)
    r = _run(nc, [arrays], core_ids=[0])
    return r.results[0]["out_0"]
```
